# Optimizing a Trainium2 kernel written in Bass

```python
import math
import jax, jax.numpy as jnp
from jax import lax
import numpy as np

D_MODEL = 1024
BATCH = 1
SEQ = 2048
DEPTH = 1
DEC_BATCH = 1
DEC_SEQ = 64
PAST_LEN = 1024

CHUNK = 64
A_HEADS = 6
A_HEAD_DIM = 64
A_WIDTH = A_HEADS * A_HEAD_DIM
A_PAST_CHUNKS = 8
A_PAST_ROWS = A_PAST_CHUNKS * CHUNK
A_BAND = A_PAST_ROWS + CHUNK
A_REL_MIN = -(CHUNK - 1)
A_REL_MAX = 128
A_REL_SIZE = A_REL_MAX - A_REL_MIN + 1
ATT_SCALE = A_HEAD_DIM ** -0.5
B_HEADS = 6
B_HEAD_DIM = 64
B_WIDTH = B_HEADS * B_HEAD_DIM
B_GROUPS = 2
B_HPG = B_HEADS // B_GROUPS
B_STATE = 128
B_CONV = 4
B_CONV_DIM = B_WIDTH + 2 * B_GROUPS * B_STATE
SSD_CHUNK = 128
C_GROUPS = 4
C_GROUP_DIM = 64
C_WIDTH = C_GROUPS * C_GROUP_DIM
C_CHUNK = 128
D_MIX = A_WIDTH + B_WIDTH + C_WIDTH
IN_SIZES = (A_WIDTH, A_WIDTH, A_WIDTH, B_WIDTH, B_CONV_DIM, B_HEADS, C_WIDTH, C_WIDTH)
N_IN = 3 * A_WIDTH + B_WIDTH + B_CONV_DIM + B_HEADS + 2 * C_WIDTH
D_FF = 2816
FFN_CONV = 3
DN_ALPHA = (2 * DEPTH) ** 0.25
DN_BETA = (8 * DEPTH) ** -0.25
LN_EPS = 1e-5
RMS_EPS = 1e-5

kernel_name = 'hybrid_streaming_encoder_step'

def layer_norm(x, g, b):
    xf = x.astype(jnp.float32)
    mu = jnp.mean(xf, axis=-1, keepdims=True)
    var = jnp.mean(jnp.square(xf - mu), axis=-1, keepdims=True)
    return ((xf - mu) * lax.rsqrt(var + LN_EPS) * g.astype(jnp.float32) + b.astype(jnp.float32)).astype(x.dtype)

def rms_norm(x, g):
    xf = x.astype(jnp.float32)
    return (xf * lax.rsqrt(jnp.mean(jnp.square(xf), axis=-1, keepdims=True) + RMS_EPS) * g.astype(jnp.float32)).astype(x.dtype)

def split_cols(t, sizes):
    return jnp.split(t, np.cumsum(sizes)[:-1].tolist(), axis=-1)

def causal_dwconv(x, prev, w, b):
    k_width = w.shape[0]
    L = x.shape[1]
    xp = jnp.concatenate([prev.astype(x.dtype), x], axis=1)
    y = b.astype(x.dtype) + w[0] * xp[:, 0:L]
    for j in range(1, k_width):
        y = y + w[j] * xp[:, j:j + L]
    return y, xp[:, L:]

def rel_bias_lookup(table, rel):
    idx = jnp.clip(rel, A_REL_MIN, A_REL_MAX) - A_REL_MIN
    return table[:, idx].astype(jnp.float32)

def band_attention_prompt(q, k, v, table):
    n, L, H, dh = q.shape
    nc = L // CHUNK
    qc = q.reshape(n, nc, CHUNK, H, dh)
    kidx = jnp.arange(nc)[:, None] * CHUNK - A_PAST_ROWS + jnp.arange(A_BAND)[None, :]
    valid = kidx >= 0
    kidx = jnp.maximum(kidx, 0)
    kb = jnp.take(k, kidx, axis=1)
    vb = jnp.take(v, kidx, axis=1)
    s = jnp.einsum('bcqhd,bckhd->bchqk', qc, kb).astype(jnp.float32) * ATT_SCALE
    rel = jnp.arange(CHUNK)[:, None] + A_PAST_ROWS - jnp.arange(A_BAND)[None, :]
    s = s + rel_bias_lookup(table, rel)[None, None]
    s = jnp.where(valid[None, :, None, None, :], s, -jnp.inf)
    p = jax.nn.softmax(s, axis=-1).astype(vb.dtype)
    o = jnp.einsum('bchqk,bckhd->bcqhd', p, vb)
    return o.reshape(n, L, H * dh)

def band_attention_sample(q, k_new, v_new, k_cache, v_cache, table):
    n, T = q.shape[0], q.shape[1]
    n_past = k_cache.shape[1]
    kk = jnp.concatenate([k_cache.astype(k_new.dtype), k_new], axis=1)
    vv = jnp.concatenate([v_cache.astype(v_new.dtype), v_new], axis=1)
    s = jnp.einsum('bqhd,bkhd->bhqk', q, kk).astype(jnp.float32) * ATT_SCALE
    rel = jnp.arange(T)[:, None] + n_past - jnp.arange(n_past + T)[None, :]
    s = s + rel_bias_lookup(table, rel)[None]
    p = jax.nn.softmax(s, axis=-1).astype(vv.dtype)
    o = jnp.einsum('bhqk,bkhd->bqhd', p, vv)
    return o.reshape(n, T, A_WIDTH)

def ssd_scan(x, dt, a, bm, cm, h0):
    n, L = x.shape[0], x.shape[1]
    q = SSD_CHUNK if L % SSD_CHUNK == 0 else L
    nc = L // q
    f32 = jnp.float32
    xg = x.astype(f32).reshape(n, nc, q, B_GROUPS, B_HPG, B_HEAD_DIM)
    dtg = dt.reshape(n, nc, q, B_GROUPS, B_HPG)
    bc = bm.astype(f32).reshape(n, nc, q, B_GROUPS, B_STATE)
    cc = cm.astype(f32).reshape(n, nc, q, B_GROUPS, B_STATE)
    acum = jnp.cumsum(dtg * a.reshape(B_GROUPS, B_HPG), axis=2)
    xdt = xg * dtg[..., None]
    seg = acum[:, :, :, None] - acum[:, :, None, :]
    causal = jnp.tril(jnp.ones((q, q), dtype=bool))
    decay = jnp.exp(jnp.where(causal[:, :, None, None], seg, -jnp.inf))
    cb = jnp.einsum('bclgn,bcsgn->bclsg', cc, bc)
    y_diag = jnp.einsum('bclsgr,bcsgrp->bclgrp', cb[..., None] * decay, xdt)
    decay_s = jnp.exp(acum[:, :, -1:] - acum)
    st = jnp.einsum('bclgn,bclgrp->bcgrpn', bc, xdt * decay_s[..., None])
    chunk_decay = jnp.exp(acum[:, :, -1])

    def step(h, inp):
        s_c, d_c = inp
        return h * d_c[..., None, None] + s_c, h

    h_init = h0.astype(f32).reshape(n, B_GROUPS, B_HPG, B_HEAD_DIM, B_STATE)
    h_last, h_prev = lax.scan(step, h_init, (jnp.moveaxis(st, 1, 0), jnp.moveaxis(chunk_decay, 1, 0)))
    h_prev = jnp.moveaxis(h_prev, 0, 1)
    y_off = jnp.einsum('bclgn,bcgrpn->bclgrp', cc, h_prev) * jnp.exp(acum)[..., None]
    y = (y_diag + y_off).reshape(n, L, B_HEADS, B_HEAD_DIM)
    return y, h_last.reshape(n, B_HEADS, B_HEAD_DIM, B_STATE)

def mamba_mixer(z, xbc, dt_raw, conv_prev, h0, conv_w, conv_b, dt_bias, a_log, d_skip):
    n, L = z.shape[0], z.shape[1]
    f32 = jnp.float32
    xbc, conv_state = causal_dwconv(xbc, conv_prev, conv_w, conv_b)
    xbc = jax.nn.silu(xbc)
    xs, bm, cm = split_cols(xbc, (B_WIDTH, B_GROUPS * B_STATE, B_GROUPS * B_STATE))
    xs = xs.reshape(n, L, B_HEADS, B_HEAD_DIM)
    dt = jax.nn.softplus(dt_raw.astype(f32) + dt_bias.astype(f32))
    a = -jnp.exp(a_log.astype(f32))
    y, h = ssd_scan(xs, dt, a, bm.reshape(n, L, B_GROUPS, B_STATE), cm.reshape(n, L, B_GROUPS, B_STATE), h0)
    y = y + d_skip.astype(f32)[:, None] * xs.astype(f32)
    y = y.reshape(n, L, B_WIDTH).astype(z.dtype) * jax.nn.silu(z)
    return y, conv_state, h

def chunk_mlp(u, v, w_s, b_s):
    n, L = v.shape[0], v.shape[1]
    q = min(L, C_CHUNK)
    nc = L // q
    w = jnp.tril(w_s[:, :q, :q])
    vg = v.reshape(n, nc, q, C_GROUPS, C_GROUP_DIM)
    mixed = jnp.einsum('gij,bcjgd->bcigd', w, vg) + jnp.transpose(b_s[:, :q])[None, None, :, :, None]
    return u * mixed.reshape(n, L, C_WIDTH)

def trunk_layer(x, k_cache, v_cache, ssm_conv_prev, ssm_h0, ffn_conv_prev,
                w_in, attn_rel_bias, ssm_conv_w, ssm_conv_b, ssm_dt_bias, ssm_a_log, ssm_d,
                gmlp_w, gmlp_b, mix_norm_g, w_out, ln1_g, ln1_b,
                ffn_w_in, ffn_conv_w, ffn_conv_b, ffn_w_out, ln2_g, ln2_b):
    n, L = x.shape[0], x.shape[1]
    q, k, v, z, xbc, dt_raw, u, vc = split_cols(x @ w_in, IN_SIZES)
    q = q.reshape(n, L, A_HEADS, A_HEAD_DIM)
    k = k.reshape(n, L, A_HEADS, A_HEAD_DIM)
    v = v.reshape(n, L, A_HEADS, A_HEAD_DIM)
    if k_cache is None:
        o_a = band_attention_prompt(q, k, v, attn_rel_bias)
        keep = min(A_PAST_ROWS, L)
        k_rows, v_rows = k[:, L - keep:], v[:, L - keep:]
    else:
        o_a = band_attention_sample(q, k, v, k_cache, v_cache, attn_rel_bias)
        k_rows, v_rows = k, v
    o_b, ssm_conv_state, ssm_h = mamba_mixer(z, xbc, dt_raw, ssm_conv_prev, ssm_h0, ssm_conv_w, ssm_conv_b,
                                             ssm_dt_bias, ssm_a_log, ssm_d)
    u = jax.nn.gelu(u)
    vc = jax.nn.gelu(vc)
    o_c = chunk_mlp(u, vc, gmlp_w, gmlp_b)
    g_a, g_b, g_c = split_cols(mix_norm_g, (A_WIDTH, B_WIDTH, C_WIDTH))
    mixed = jnp.concatenate([rms_norm(o_a, g_a), rms_norm(o_b, g_b), rms_norm(o_c, g_c)], axis=-1)
    x = layer_norm(DN_ALPHA * x + mixed @ w_out, ln1_g, ln1_b)
    up, ffn_conv_state = causal_dwconv(x @ ffn_w_in, ffn_conv_prev, ffn_conv_w, ffn_conv_b)
    gate, val = split_cols(up, (D_FF, D_FF))
    x = layer_norm(DN_ALPHA * x + (jax.nn.silu(gate) * val) @ ffn_w_out, ln2_g, ln2_b)
    return x, k_rows, v_rows, ssm_h, ssm_conv_state, vc, ffn_conv_state

def setup_inputs(seed: int = 0) -> dict:
    key = jax.random.key(seed)
    ks = jax.random.split(key, 28)
    f32 = jnp.float32

    def nrm(k, shape, scale):
        return jax.random.normal(k, shape, f32) * scale

    keep = min(A_PAST_ROWS, PAST_LEN)
    dt0 = jnp.exp(jax.random.uniform(ks[12], (DEPTH, B_HEADS), f32, math.log(1e-3), math.log(1e-1)))
    return {
        'x_prompt': nrm(ks[0], (BATCH, SEQ, D_MODEL), 1.0),
        'x_sample': nrm(ks[1], (DEC_BATCH, DEC_SEQ, D_MODEL), 1.0),
        'cache_attn_k': nrm(ks[2], (DEPTH, DEC_BATCH, keep, A_HEADS, A_HEAD_DIM), 1.0),
        'cache_attn_v': nrm(ks[3], (DEPTH, DEC_BATCH, keep, A_HEADS, A_HEAD_DIM), 1.0),
        'state_ssm': nrm(ks[4], (DEPTH, DEC_BATCH, B_HEADS, B_HEAD_DIM, B_STATE), 0.1),
        'state_ssm_conv': nrm(ks[5], (DEPTH, DEC_BATCH, B_CONV - 1, B_CONV_DIM), 1.0),
        'state_ffn_conv': nrm(ks[6], (DEPTH, DEC_BATCH, FFN_CONV - 1, 2 * D_FF), 1.0),
        'ln_in_g': 1.0 + nrm(ks[7], (D_MODEL,), 0.05),
        'ln_in_b': nrm(ks[8], (D_MODEL,), 0.02),
        'w_in': nrm(ks[9], (DEPTH, D_MODEL, N_IN), D_MODEL ** -0.5),
        'attn_rel_bias': nrm(ks[10], (DEPTH, A_HEADS, A_REL_SIZE), 0.5),
        'ssm_conv_w': nrm(ks[11], (DEPTH, B_CONV, B_CONV_DIM), B_CONV ** -0.5),
        'ssm_conv_b': nrm(ks[13], (DEPTH, B_CONV_DIM), 0.02),
        'ssm_dt_bias': dt0 + jnp.log(-jnp.expm1(-dt0)),
        'ssm_a_log': jnp.log(jax.random.uniform(ks[14], (DEPTH, B_HEADS), f32, 1.0, 16.0)),
        'ssm_d': 1.0 + nrm(ks[15], (DEPTH, B_HEADS), 0.1),
        'gmlp_w': nrm(ks[16], (DEPTH, C_GROUPS, C_CHUNK, C_CHUNK), C_CHUNK ** -0.5),
        'gmlp_b': 1.0 + nrm(ks[17], (DEPTH, C_GROUPS, C_CHUNK), 0.1),
        'mix_norm_g': 1.0 + nrm(ks[18], (DEPTH, D_MIX), 0.05),
        'w_out': nrm(ks[19], (DEPTH, D_MIX, D_MODEL), D_MIX ** -0.5 * DN_BETA),
        'ln1_g': 1.0 + nrm(ks[20], (DEPTH, D_MODEL), 0.05),
        'ln1_b': nrm(ks[21], (DEPTH, D_MODEL), 0.02),
        'ffn_w_in': nrm(ks[22], (DEPTH, D_MODEL, 2 * D_FF), D_MODEL ** -0.5),
        'ffn_conv_w': nrm(ks[23], (DEPTH, FFN_CONV, 2 * D_FF), FFN_CONV ** -0.5),
        'ffn_conv_b': nrm(ks[24], (DEPTH, 2 * D_FF), 0.02),
        'ffn_w_out': nrm(ks[25], (DEPTH, D_FF, D_MODEL), D_FF ** -0.5 * DN_BETA),
        'ln2_g': 1.0 + nrm(ks[26], (DEPTH, D_MODEL), 0.05),
        'ln2_b': nrm(ks[27], (DEPTH, D_MODEL), 0.02),
    }

def reference(x_prompt, x_sample, cache_attn_k, cache_attn_v, state_ssm, state_ssm_conv, state_ffn_conv,
              ln_in_g, ln_in_b, w_in, attn_rel_bias, ssm_conv_w, ssm_conv_b, ssm_dt_bias, ssm_a_log, ssm_d,
              gmlp_w, gmlp_b, mix_norm_g, w_out, ln1_g, ln1_b,
              ffn_w_in, ffn_conv_w, ffn_conv_b, ffn_w_out, ln2_g, ln2_b):
    xp = layer_norm(x_prompt, ln_in_g, ln_in_b)
    xs = layer_norm(x_sample, ln_in_g, ln_in_b)
    n_p = x_prompt.shape[0]
    zero_ssm_conv = jnp.zeros((n_p, B_CONV - 1, B_CONV_DIM), xp.dtype)
    zero_ssm = jnp.zeros((n_p, B_HEADS, B_HEAD_DIM, B_STATE), jnp.float32)
    zero_ffn_conv = jnp.zeros((n_p, FFN_CONV - 1, 2 * D_FF), xp.dtype)
    p_k, p_v, p_h, p_c, p_f = [], [], [], [], []
    s_k, s_v, s_h, s_c, s_g, s_f = [], [], [], [], [], []
    for l in range(DEPTH):
        lp = (w_in[l], attn_rel_bias[l], ssm_conv_w[l], ssm_conv_b[l], ssm_dt_bias[l], ssm_a_log[l], ssm_d[l],
              gmlp_w[l], gmlp_b[l], mix_norm_g[l], w_out[l], ln1_g[l], ln1_b[l],
              ffn_w_in[l], ffn_conv_w[l], ffn_conv_b[l], ffn_w_out[l], ln2_g[l], ln2_b[l])
        xp, kr, vr, hh, cs, _, fs = trunk_layer(xp, None, None, zero_ssm_conv, zero_ssm, zero_ffn_conv, *lp)
        p_k.append(kr); p_v.append(vr); p_h.append(hh); p_c.append(cs); p_f.append(fs)
        xs, kr, vr, hh, cs, gv, fs = trunk_layer(xs, cache_attn_k[l], cache_attn_v[l], state_ssm_conv[l],
                                                 state_ssm[l], state_ffn_conv[l], *lp)
        s_k.append(kr); s_v.append(vr); s_h.append(hh); s_c.append(cs); s_g.append(gv); s_f.append(fs)
    return (xp, xs,
            jnp.stack(p_k), jnp.stack(p_v), jnp.stack(p_h), jnp.stack(p_c), jnp.stack(p_f),
            jnp.stack(s_k), jnp.stack(s_v), jnp.stack(s_h), jnp.stack(s_c), jnp.stack(s_g), jnp.stack(s_f))


_drawn_inputs = setup_inputs


def setup_inputs(seed=0):
    import zlib

    import numpy as np

    out = dict(_drawn_inputs(seed))
    spreads = {}
    factors = {'ssm_d': 8.0, 'gmlp_b': 2.995, 'ffn_conv_b': 6.72, 'ln2_b': 3.12}
    for name, (base, spread) in spreads.items():
        noise = np.random.default_rng([zlib.crc32(name.encode()), seed]).standard_normal(out[name].shape)
        drawn = base * np.exp(spread * noise) if base else spread * noise
        out[name] = __import__('jax').numpy.asarray(drawn.astype(out[name].dtype))
    for name, factor in factors.items():
        out[name] = (out[name] * factor).astype(out[name].dtype)
    return out
```

```python
from contextlib import ExitStack

import concourse.bass as bass
from concourse import mybir

F32 = mybir.dt.float32
F32R = mybir.dt.float32r
ALU = mybir.AluOpType
ACT = mybir.ActivationFunctionType
AX_X = mybir.AxisListType.X

P = 128
D = 1024
KD = D // P
SEQ = 2048
NSMP = 64
ROWS = SEQ + NSMP
NT = SEQ // P
CACHE = 512
HEADS = 6
HD = 64
AW = HEADS * HD
STATE = 128
XBC = AW + 4 * STATE
NXBC = XBC // P
CW = 256
CG = 4
DFF = 2816
KF = DFF // P
ALPHA = 2.0 ** 0.25
EPS = 1e-5
MASKED = -1e30
REL = 192
WIN = CACHE + P
V0, Z0, X0, DT0, U0 = 2 * AW, 3 * AW, 4 * AW, 4 * AW + XBC, 4 * AW + XBC + HEADS
G0 = U0 + CW
N_IN = G0 + CW


def wait_if(eng, sem, value):
    if not isinstance(value, int) or value > 0:
        eng.wait_ge(sem, value)


def alone(eng):
    eng.nop(nofuse=True)


def tile_rows(t):
    if isinstance(t, int):
        return slice(t * P, t * P + (NSMP if t == NT else P))
    return bass.ds(t * P, P)


def n_rows(t):
    return NSMP if isinstance(t, int) and t == NT else P


class Stage:

    def __init__(self, nc, ctx, stage):
        self.nc, self.ctx, self.stage = nc, ctx, stage

    def sb(self, name, shape, dt=F32):
        return self.ctx.enter_context(self.nc.sbuf_tensor(f"{self.stage}_{name}", shape, dt))

    def ps(self, name, shape):
        return self.ctx.enter_context(self.nc.psum_tensor(f"{self.stage}_{name}", shape, F32))

    def sem(self, name):
        return self.nc.alloc_semaphore(f"{self.stage}_{name}")


def bc_row(ap1d, n):
    return ap1d.rearrange("(a n) -> a n", a=1).to_broadcast([P, n])


def products(pe, out, lhs_hi, lhs_lo, rhs_hi, rhs_lo, first, last):
    pe.matmul(out, lhs_hi, rhs_hi, start=first, stop=False)
    pe.matmul(out, lhs_hi, rhs_lo, start=False, stop=False)
    return pe.matmul(out, lhs_lo, rhs_hi, start=False, stop=last)


def make_identity(pool, ident, zero_done, ident_done):
    pool.memset(ident[:], 0.0).then_inc(zero_done, 1)
    pool.wait_ge(zero_done, 1)
    pool.affine_select(out=ident[:], in_=ident[:], compare_op=ALU.not_equal, fill=1.0, base=0,
                       pattern=[[-1, P]], channel_multiplier=1).then_inc(ident_done, 1)


def project_rows(nc, d):
    with nc.cleanup_on_exit(), ExitStack() as ctx:
        m = Stage(nc, ctx, "pr")
        cols = [(V0, 512), (V0 + 512, 256), (G0, CW), (DT0, HEADS + CW)]
        at = [0, 512, 768, 1024]
        NW = 1024 + HEADS + CW
        w_raw = m.sb("w_raw", [P, 2, NW])
        w_hi, w_lo = m.sb("w_hi", [P, KD, NW], F32R), m.sb("w_lo", [P, KD, NW], F32R)
        x = m.sb("x", [P, 2, D])
        xr = m.sb("xr", [P, 2, D])
        xt_hi, xt_lo = m.sb("xt_hi", [P, 2, KD, P], F32R), m.sb("xt_lo", [P, 2, KD, P], F32R)
        g_bc, b_bc = m.sb("g_bc", [P, D]), m.sb("b_bc", [P, D])
        stats, mv, sd, rs = m.sb("stats", [P, 2, 6]), m.sb("mv", [P, 2]), m.sb("sd", [P, 2]), m.sb("rs", [P, 1])
        ident = m.sb("ident", [P, P])
        v_out, z_out = m.sb("v_out", [P, 2, AW]), m.sb("z_out", [P, 2, AW])
        uv_out, dt_out = m.sb("uv_out", [P, 2, 2 * CW]), m.sb("dt_out", [P, 2, 8])
        ps_y, ps_t = m.ps("ps_y", [P, 2, 3, 512]), m.ps("ps_t", [P, KD, P])

        zero_done, ident_done = m.sem("zero_done"), m.sem("ident_done")
        w_loaded = [m.sem("w_loaded0"), m.sem("w_loaded1")]
        w_hi_done, w_lo_done = m.sem("w_hi_done"), m.sem("w_lo_done")
        gb_loaded = m.sem("gb_loaded")
        x_loaded = [m.sem("x_loaded0"), m.sem("x_loaded1")]
        bn_done, aggr_done, var_done, sd_done = m.sem("bn_done"), m.sem("aggr_done"), m.sem("var_done"), m.sem("sd_done")
        rs_done, xhat_done, xg_done, xr_done = m.sem("rs_done"), m.sem("xhat_done"), m.sem("xg_done"), m.sem("xr_done")
        t_done, hi_done, lo_done, y_done = m.sem("t_done"), m.sem("hi_done"), m.sem("lo_done"), m.sem("y_done")
        vdt_done, act_out_done = m.sem("vdt_done"), m.sem("act_out_done")
        xr_stored = [m.sem("xr_stored0"), m.sem("xr_stored1")]
        xt_stored = [m.sem("xt_stored0"), m.sem("xt_stored1")]
        y_stored = [m.sem("y_stored0"), m.sem("y_stored1")]

        def half(t):
            return t // 2

        def tiles(eng, step):
            step(0, 0, 0)
            step(1, 1, 0)
            with eng.Fori(1, 7) as i:
                step(2 * i, 0, i)
                step(2 * i + 1, 1, i)
            for t in (14, 15, 16):
                step(t, t % 2, t // 2)

        with nc.Block() as block:
            @block.sync
            def _(sp):
                for k in range(KD):
                    if k >= 2:
                        sp.wait_ge(w_hi_done, k - 1)
                        sp.wait_ge(w_lo_done, k - 1)
                    for (c, n), a in zip(cols, at):
                        sp.dma_start(w_raw[:, k % 2, a:a + n], d["w_in"][k * P:(k + 1) * P, c:c + n]).then_inc(w_loaded[k % 2], 16)
                def step(t, p, i):
                    n = n_rows(t)
                    sp.wait_ge(xr_done, t + 1)
                    alone(sp)
                    sp.dma_start(d["x_rows"][tile_rows(t), :], xr[:n, p, :]).then_inc(xr_stored[p], 16)
                    sp.wait_ge(hi_done, t + 1)
                    alone(sp)
                    sp.dma_start(d["xt_hi"][:, :, tile_rows(t)], xt_hi[:, p, :, :n].bitcast(F32)).then_inc(xt_stored[p], 16)
                    sp.wait_ge(lo_done, t + 1)
                    alone(sp)
                    sp.dma_start(d["xt_lo"][:, :, tile_rows(t)], xt_lo[:, p, :, :n].bitcast(F32)).then_inc(xt_stored[p], 16)
                    sp.wait_ge(vdt_done, t + 1)
                    alone(sp)
                    sp.dma_start(d["v_rows"][tile_rows(t), :], v_out[:n, p, :]).then_inc(y_stored[p], 16)
                    sp.dma_start(d["dt_rows"][tile_rows(t), :], dt_out[:n, p, :HEADS]).then_inc(y_stored[p], 16)
                    sp.wait_ge(act_out_done, t + 1)
                    alone(sp)
                    sp.dma_start(d["z_rows"][tile_rows(t), :], z_out[:n, p, :]).then_inc(y_stored[p], 16)
                    sp.dma_start(d["uv_rows"][tile_rows(t), :], uv_out[:n, p, :]).then_inc(y_stored[p], 16)
                tiles(sp, step)
                for p, count in ((0, 9), (1, 8)):
                    sp.wait_ge(xr_stored[p], 16 * count)
                    sp.wait_ge(xt_stored[p], 32 * count)
                    sp.wait_ge(y_stored[p], 64 * count)

            @block.gpsimd
            def _(pool):
                make_identity(pool, ident, zero_done, ident_done)

                def load_x(t, p):
                    if isinstance(t, int) and t == NT:
                        pool.dma_start(x[:NSMP, p, :], d["x_sample"]).then_inc(x_loaded[p], 16)
                    else:
                        pool.dma_start(x[:, p, :], d["x_prompt"][tile_rows(t), :]).then_inc(x_loaded[p], 16)

                load_x(0, 0)
                load_x(1, 1)
                pool.dma_start(g_bc[:], bc_row(d["ln_in_g"], D)).then_inc(gb_loaded, 16)
                pool.dma_start(b_bc[:], bc_row(d["ln_in_b"], D)).then_inc(gb_loaded, 16)
                pool.wait_ge(gb_loaded, 32)

                def step(t, p, i):
                    n = n_rows(t)
                    pool.wait_ge(xhat_done, t + 1)
                    if not (isinstance(t, int) and t < 2):
                        pool.wait_ge(xr_stored[p], 16 * i)
                        pool.wait_ge(t_done, t - 1)
                    pool.tensor_tensor(xr[:n, p, :], x[:n, p, :], g_bc[:n, :], ALU.mult).then_inc(xg_done, 1)
                    pool.wait_ge(xg_done, t + 1)
                    pool.tensor_tensor(xr[:n, p, :], xr[:n, p, :], b_bc[:n, :], ALU.add).then_inc(xr_done, 1)
                    if not isinstance(t, int) or t + 2 <= NT:
                        load_x(t + 2, p)
                tiles(pool, step)

            @block.scalar
            def _(act):
                for k in range(KD):
                    act.wait_ge(w_loaded[k % 2], 64 * (k // 2 + 1))
                    act.copy(w_hi[:, k, :], w_raw[:, k % 2, :]).then_inc(w_hi_done, 1)

                def root(t):
                    n = n_rows(t)
                    act.wait_ge(var_done, t + 1)
                    act.activation(sd[:n, 1:2], sd[:n, 0:1], ACT.Sqrt).then_inc(sd_done, 1)

                def hi(t, p, i):
                    n = n_rows(t)
                    act.wait_ge(t_done, t + 1)
                    if not (isinstance(t, int) and t < 2):
                        act.wait_ge(xt_stored[p], 32 * i)
                        act.wait_ge(y_done, t - 1)
                    act.copy(xt_hi[:, p, :, :n], ps_t[:, :, :n]).then_inc(hi_done, 1)

                root(0)
                hi(0, 0, 0)
                root(1)

                def step(t, p, i):
                    n = n_rows(t)
                    if not isinstance(t, int) or t + 1 <= NT:
                        hi(t + 1, 1 - p, i + p)
                    if not isinstance(t, int) or t + 2 <= NT:
                        root(t + 2)
                    act.wait_ge(y_done, t + 1)
                    if not (isinstance(t, int) and t < 2):
                        act.wait_ge(y_stored[p], 64 * i)
                    y = ps_y[:, p]
                    act.activation(z_out[:n, p, 0:128], y[:n, 0, AW:512], ACT.Silu)
                    act.activation(z_out[:n, p, 128:AW], y[:n, 1, 0:256], ACT.Silu)
                    act.activation(uv_out[:n, p, CW:], y[:n, 1, 256:512], ACT.Gelu_apprx_tanh)
                    act.activation(uv_out[:n, p, :CW], y[:n, 2, HEADS:HEADS + CW],
                                   ACT.Gelu_apprx_tanh).then_inc(act_out_done, 1)
                tiles(act, step)

            @block.vector
            def _(dve):
                for k in range(KD):
                    dve.wait_ge(w_hi_done, k + 1)
                    dve.tensor_tensor(w_lo[:, k, :], w_raw[:, k % 2, :], w_hi[:, k, :].bitcast(F32),
                                      ALU.subtract).then_inc(w_lo_done, 1)

                def norm(t, p, i):
                    n = n_rows(t)
                    dve.wait_ge(x_loaded[p], 16 * (i + 1))
                    for c in range(2):
                        last = dve.bn_stats(stats[:n, c, :], x[:n, p, c * 512:(c + 1) * 512])
                    last.then_inc(bn_done, 1)
                    dve.wait_ge(bn_done, t + 1)
                    alone(dve)
                    dve.bn_aggr(mv[:n, :], stats[:n].rearrange("p a b -> p (a b)")).then_inc(aggr_done, 1)
                    dve.wait_ge(aggr_done, t + 1)
                    dve.tensor_scalar(sd[:n, 0:1], mv[:n, 1:2], EPS, None, ALU.add).then_inc(var_done, 1)
                    dve.wait_ge(sd_done, t + 1)
                    dve.reciprocal(rs[:n, :], sd[:n, 1:2]).then_inc(rs_done, 1)
                    dve.wait_ge(rs_done, t + 1)
                    dve.tensor_scalar(x[:n, p, :], x[:n, p, :], mv[:n, 0:1], rs[:n, :], ALU.subtract,
                                      ALU.mult).then_inc(xhat_done, 1)

                def lo(t, p):
                    n = n_rows(t)
                    dve.wait_ge(hi_done, t + 1)
                    dve.tensor_tensor(xt_lo[:, p, :, :n], ps_t[:, :, :n], xt_hi[:, p, :, :n].bitcast(F32),
                                      ALU.subtract).then_inc(lo_done, 1)

                norm(0, 0, 0)
                lo(0, 0)
                norm(1, 1, 0)

                def step(t, p, i):
                    n = n_rows(t)
                    if not isinstance(t, int) or t + 1 <= NT:
                        lo(t + 1, 1 - p)
                    if not isinstance(t, int) or t + 2 <= NT:
                        norm(t + 2, p, i + 1)
                    dve.wait_ge(y_done, t + 1)
                    dve.wait_ge(act_out_done, t + 1)
                    if not (isinstance(t, int) and t < 2):
                        dve.wait_ge(y_stored[p], 64 * i)
                    dve.tensor_copy(v_out[:n, p, :], ps_y[:n, p, 0, 0:AW])
                    dve.tensor_copy(dt_out[:n, p, :HEADS], ps_y[:n, p, 2, 0:HEADS]).then_inc(vdt_done, 1)
                tiles(dve, step)

            @block.tensor
            def _(pe):
                pe.wait_ge(ident_done, 1)

                def turn(t, p):
                    n = n_rows(t)
                    pe.wait_ge(xr_done, t + 1)
                    wait_if(pe, lo_done, t)
                    for k in range(KD):
                        last = pe.transpose(ps_t[:, k, :n], xr[:n, p, k * P:(k + 1) * P], ident[:n, :n])
                    last.then_inc(t_done, 1)

                turn(0, 0)

                def step(t, p, i):
                    n = n_rows(t)
                    if not isinstance(t, int) or t + 1 <= NT:
                        turn(t + 1, 1 - p)
                    pe.wait_ge(lo_done, t + 1)
                    if not (isinstance(t, int) and t < 2):
                        pe.wait_ge(vdt_done, t - 1)
                    outs = [ps_y[:n, p, 0, :], ps_y[:n, p, 1, 0:256], ps_y[:n, p, 1, 256:512],
                            ps_y[:n, p, 2, 0:HEADS + CW]]
                    for out, a, (c, w) in zip(outs, at, cols):
                        for k in range(KD):
                            if isinstance(t, int) and t == 0 and a == 0:
                                pe.wait_ge(w_lo_done, k + 1)
                            last = products(pe, out, xt_hi[:, p, k, :n], xt_lo[:, p, k, :n],
                                            w_hi[:, k, a:a + w], w_lo[:, k, a:a + w], k == 0, k == KD - 1)
                    last.then_inc(y_done, 1)
                tiles(pe, step)


def project_features(nc, d):
    with nc.cleanup_on_exit(), ExitStack() as ctx:
        m = Stage(nc, ctx, "pf")
        GN = 512
        NG = SEQ // GN
        NM = (2 * AW + XBC) // P
        NQK = 2 * AW // P
        W = 2 * AW + XBC
        w_raw = m.sb("w_raw", [P, 2, W])
        w_hi, w_lo = m.sb("w_hi", [P, KD, W], F32R), m.sb("w_lo", [P, KD, W], F32R)
        xt_hi, xt_lo = m.sb("xt_hi", [P, 2, KD, GN], F32R), m.sb("xt_lo", [P, 2, KD, GN], F32R)
        qk_out = m.sb("qk_out", [P, 2, GN])
        cin = m.sb("cin", [P, 2, 3 + GN])
        conv, conv_out = m.sb("conv", [P, 2, GN]), m.sb("conv_out", [P, 2, GN])
        halo, halo_smp = m.sb("halo", [P, NXBC, 3]), m.sb("halo_smp", [P, NXBC, 3])
        taps, shift = m.sb("taps", [P, NXBC, 4]), m.sb("shift", [P, NXBC])
        ps_y = m.ps("ps_y", [P, 8, GN])

        w_loaded = [m.sem("w_loaded0"), m.sem("w_loaded1")]
        w_hi_done, w_lo_done = m.sem("w_hi_done"), m.sem("w_lo_done")
        small_loaded, halo_zeroed = m.sem("small_loaded"), m.sem("halo_zeroed")
        xt_loaded = [m.sem("xt_loaded0"), m.sem("xt_loaded1")]
        y_done, evac_done = m.sem("y_done"), m.sem("evac_done")
        halo_in_done, conv_done, tap_done, silu_done = m.sem("halo_in_done"), m.sem("conv_done"), m.sem("tap_done"), m.sem("silu_done")
        qk_stored = [m.sem("qk_stored0"), m.sem("qk_stored1")]
        xbc_stored = [m.sem("xbc_stored0"), m.sem("xbc_stored1")]
        state_stored = m.sem("state_stored")

        def width(g):
            return NSMP if isinstance(g, int) and g == NG else GN

        def gcols(g):
            if isinstance(g, int):
                return slice(g * GN, g * GN + width(g))
            return bass.ds(g * GN, GN)

        def groups(eng, step):
            step(0, 0, 0)
            step(1, 1, 0)
            with eng.Fori(1, NG // 2) as i:
                step(2 * i, 0, i)
                step(2 * i + 1, 1, i)
            step(NG, 0, NG // 2)

        def xbc_count(g, j):
            return (NXBC + 1 - j % 2) // 2 * g + j // 2

        with nc.Block() as block:
            @block.sync
            def _(sp):
                for k in range(KD):
                    if k >= 2:
                        sp.wait_ge(w_hi_done, k - 1)
                        sp.wait_ge(w_lo_done, k - 1)
                    rows = slice(k * P, (k + 1) * P)
                    sp.dma_start(w_raw[:, k % 2, 0:2 * AW], d["w_in"][rows, 0:2 * AW]).then_inc(w_loaded[k % 2], 16)
                    sp.dma_start(w_raw[:, k % 2, 2 * AW:], d["w_in"][rows, X0:X0 + XBC]).then_inc(w_loaded[k % 2], 16)

                def step(g, p, i):
                    n = width(g)
                    for j in range(NQK):
                        sp.wait_ge(evac_done, NM * g + j + 1)
                        alone(sp)
                        sp.dma_start(d["qk_t"][j * P:(j + 1) * P, gcols(g)], qk_out[:, j % 2, :n]).then_inc(qk_stored[j % 2], 16)
                    for j in range(NXBC):
                        sp.wait_ge(silu_done, NXBC * g + j + 1)
                        alone(sp)
                        sp.dma_start(d["xbc_t"][:, j, gcols(g)], conv_out[:, j % 2, :n]).then_inc(xbc_stored[j % 2], 16)
                groups(sp, step)
                for p in range(2):
                    sp.wait_ge(qk_stored[p], 16 * (NQK // 2) * (NG + 1))
                    sp.wait_ge(xbc_stored[p], 16 * xbc_count(NG + 1, p))

            @block.gpsimd
            def _(pool):
                def load_xt(g, p):
                    n = width(g)
                    pool.dma_start(xt_hi[:, p, :, :n].bitcast(F32), d["xt_hi"][:, :, gcols(g)]).then_inc(xt_loaded[p], 16)
                    pool.dma_start(xt_lo[:, p, :, :n].bitcast(F32), d["xt_lo"][:, :, gcols(g)]).then_inc(xt_loaded[p], 16)

                load_xt(0, 0)
                for c in range(4):
                    pool.dma_start(taps[:, :, c], d["ssm_conv_w"][c].rearrange("(m p) -> p m", p=P),
                                   allow_slow_non_contiguous=True).then_inc(small_loaded, 16)
                pool.dma_start(shift[:], d["ssm_conv_b"].rearrange("(m p) -> p m", p=P), allow_slow_non_contiguous=True).then_inc(small_loaded, 16)
                for c in range(3):
                    pool.dma_start(halo_smp[:, :, c], d["state_ssm_conv"][c].rearrange("(m p) -> p m", p=P),
                                   allow_slow_non_contiguous=True).then_inc(small_loaded, 16)
                pool.memset(halo[:], 0.0).then_inc(halo_zeroed, 1)
                load_xt(1, 1)

                def step(g, p, i):
                    if not isinstance(g, int) or g + 2 <= NG:
                        pool.wait_ge(y_done, NM * (g + 1))
                        load_xt(g + 2, p)
                step(0, 0, 0)
                step(1, 1, 0)
                pool.wait_ge(y_done, NM * 3)
                load_xt(NG, 0)
                pool.wait_ge(conv_done, NXBC * NG)
                for c in range(3):
                    pool.dma_start(d["prompt_ssm_conv"][c].rearrange("(m p) -> p m", p=P), halo[:, :, c], allow_slow_non_contiguous=True).then_inc(state_stored, 16)
                pool.wait_ge(conv_done, NXBC * (NG + 1))
                for c in range(3):
                    pool.dma_start(d["sample_ssm_conv"][c].rearrange("(m p) -> p m", p=P), halo_smp[:, :, c], allow_slow_non_contiguous=True).then_inc(state_stored, 16)
                pool.wait_ge(state_stored, 16 * 6)

            @block.scalar
            def _(act):
                for k in range(KD):
                    act.wait_ge(w_loaded[k % 2], 32 * (k // 2 + 1))
                    act.copy(w_hi[:, k, :], w_raw[:, k % 2, :]).then_inc(w_hi_done, 1)

                def step(g, p, i):
                    n = width(g)
                    for j in range(NQK):
                        if not (isinstance(g, int) and g == 0 and j < 2):
                            act.wait_ge(qk_stored[j % 2], 16 * (NQK // 2 * g + j // 2))
                        act.wait_ge(y_done, NM * g + j + 1)
                        act.mul(qk_out[:, j % 2, :n], ps_y[:, j, :n],
                                HD ** -0.5 if j < NQK // 2 else 1.0).then_inc(evac_done, 1)

                    def silu(j):
                        if not (isinstance(g, int) and g == 0 and j < 2):
                            act.wait_ge(xbc_stored[j % 2], 16 * xbc_count(g, j))
                        act.wait_ge(conv_done, NXBC * g + j + 1)
                        act.activation(conv_out[:, j % 2, :n], conv[:, j % 2, :n], ACT.Silu).then_inc(silu_done, 1)

                    for j in range(NXBC):
                        wait_if(act, conv_done, NXBC * g + j - (1 if j != 0 else 0) if j != 1 else NXBC * g)
                        act.wait_ge(y_done, NM * g + NQK + j + 1)
                        act.copy(cin[:, j % 2, 3:3 + n], ps_y[:, (NQK + j) % 8, :n]).then_inc(evac_done, 1)
                        if j >= 1:
                            silu(j - 1)
                    silu(NXBC - 1)
                groups(act, step)

            @block.vector
            def _(dve):
                for k in range(KD):
                    dve.wait_ge(w_hi_done, k + 1)
                    dve.tensor_tensor(w_lo[:, k, :], w_raw[:, k % 2, :], w_hi[:, k, :].bitcast(F32),
                                      ALU.subtract).then_inc(w_lo_done, 1)
                dve.wait_ge(small_loaded, 128)
                dve.wait_ge(halo_zeroed, 1)

                def step(g, p, i):
                    n = width(g)
                    h = halo_smp if isinstance(g, int) and g == NG else halo
                    for j in range(NXBC):
                        u, b = NXBC * g + j, j % 2
                        c, y = cin[:, b], conv[:, b, :n]
                        dve.wait_ge(evac_done, NM * g + NQK + j + 1)
                        dve.tensor_copy(c[:, 0:3], h[:, j, :]).then_inc(halo_in_done, 1)
                        if not (isinstance(g, int) and g == 0 and j < 2):
                            dve.wait_ge(silu_done, u if j == 0 else u - 1)
                        dve.wait_ge(halo_in_done, u + 1)
                        dve.tensor_scalar(y, c[:, 0:n], taps[:, j, 0:1], shift[:, j:j + 1], ALU.mult,
                                          ALU.add).then_inc(tap_done, 1)
                        for e in (1, 2):
                            dve.wait_ge(tap_done, 3 * u + e)
                            dve.scalar_tensor_tensor(out=y, in0=c[:, e:e + n], scalar=taps[:, j, e:e + 1], in1=y,
                                                     op0=ALU.mult, op1=ALU.add).then_inc(tap_done, 1)
                        dve.tensor_copy(h[:, j, :], c[:, n:n + 3])
                        dve.wait_ge(tap_done, 3 * u + 3)
                        dve.scalar_tensor_tensor(out=y, in0=c[:, 3:3 + n], scalar=taps[:, j, 3:4], in1=y,
                                                 op0=ALU.mult, op1=ALU.add).then_inc(conv_done, 1)
                groups(dve, step)

            @block.tensor
            def _(pe):
                def step(g, p, i):
                    n = width(g)
                    pe.wait_ge(xt_loaded[p], 32 * (i + 1))
                    for j in range(NM):
                        wait_if(pe, evac_done, NM * g + j - 4)
                        for k in range(KD):
                            if isinstance(g, int) and g == 0 and j == 0:
                                pe.wait_ge(w_lo_done, k + 1)
                            c = slice(j * P, (j + 1) * P)
                            last = products(pe, ps_y[:, j % 8, :n], w_hi[:, k, c], w_lo[:, k, c],
                                            xt_hi[:, p, k, :n], xt_lo[:, p, k, :n], k == 0, k == KD - 1)
                        last.then_inc(y_done, 1)
                groups(pe, step)


class Band:

    def __init__(self, t):
        self.t = t
        self.smp = isinstance(t, int) and t == NT
        self.nb = min(t + 1, 5) if isinstance(t, int) else 5
        self.nq = NSMP if self.smp else P
        self.width = CACHE + NSMP if self.smp else self.nb * P
        self.col0 = 0 if self.smp else WIN - self.width

    def block_rows(self, b):
        return min(P, self.width - b * P)


def attention(nc, d):
    with nc.cleanup_on_exit(), ExitStack() as ctx:
        m = Stage(nc, ctx, "at")
        NP_ = HEADS // 2
        q, kw, vw = m.sb("q", [P, 2, NP_, P]), m.sb("kw", [P, 2, NP_, WIN]), m.sb("vw", [P, 2, 5, AW])
        q_smp, k_smp, v_smp = m.sb("q_smp", [P, NP_, NSMP]), m.sb("k_smp", [P, NP_, CACHE + NSMP]), m.sb("v_smp", [P, 5, AW])
        cache = m.sb("cache", [P, 4, AW])
        bias, bias_up = m.sb("bias", [P, HEADS, WIN]), m.sb("bias_up", [P, HEADS, WIN])
        flip = m.sb("flip", [P, P])
        ext = m.sb("ext", [HEADS, WIN + P])
        ident = m.sb("ident", [P, P])
        s = m.sb("s", [P, 2, WIN])
        pt = m.sb("pt", [P, 2, 5, P])
        top, ntop, total, inv = m.sb("top", [P, 2]), m.sb("ntop", [P, 2]), m.sb("total", [P, 3]), m.sb("inv", [P, 2])
        o = m.sb("o", [P, 2, AW])
        k_rows = m.sb("k_rows", [P, 5, AW])
        ps_s, ps_t, ps_o = m.ps("ps_s", [P, 2, 1024]), m.ps("ps_t", [P, 1024]), m.ps("ps_o", [P, 2, 512])

        zero_done, ident_done = m.sem("zero_done"), m.sem("ident_done")
        table_loaded, ext_done, ext_stored, bias_loaded, bias_done = (
            m.sem("table_loaded"), m.sem("ext_done"), m.sem("ext_stored"), m.sem("bias_loaded"), m.sem("bias_done"))
        flip_done, bias_flipped, bias_copied = m.sem("flip_done"), m.sem("bias_flipped"), m.sem("bias_copied")
        cache_loaded, cache_turned, cache_done = m.sem("cache_loaded"), m.sem("cache_turned"), m.sem("cache_done")
        qk_loaded = [m.sem("qk_loaded0"), m.sem("qk_loaded1")]
        v_loaded = [m.sem("v_loaded0"), m.sem("v_loaded1")]
        smp_qk_loaded, smp_v_loaded = m.sem("smp_qk_loaded"), m.sem("smp_v_loaded")
        s_done, biased, ntop_done, exp_done = m.sem("s_done"), m.sem("biased"), m.sem("ntop_done"), m.sem("exp_done")
        turned, pt_done, pv_done, inv_done, o_done = m.sem("turned"), m.sem("pt_done"), m.sem("pv_done"), m.sem("inv_done"), m.sem("o_done")
        o_stored = [m.sem("o_stored0"), m.sem("o_stored1")]
        rows_turned, rows_done, rows_stored = m.sem("rows_turned"), m.sem("rows_done"), m.sem("rows_stored")
        caches_stored = m.sem("caches_stored")

        LOOP0, LOOP1 = 6, 14

        def tiles(eng, step):
            def straight(t):
                step(Band(t - 1) if t else None, Band(t), Band(t + 1) if t < NT else None, t % 2, t // 2)
            for t in range(LOOP0):
                straight(t)
            with eng.Fori(LOOP0 // 2, LOOP1 // 2) as i:
                for p in range(2):
                    t = 2 * i + p
                    step(Band(t - 1), Band(t), Band(t + 1), p, i)
            for t in range(LOOP1, NT + 1):
                straight(t)

        def heads(eng, step):
            def tile_step(before, cur, after, p, i):
                for h in range(HEADS):
                    prev = (cur, p, h - 1) if h else (before, 1 - p, HEADS - 1) if before else None
                    nxt = (cur, p, h + 1) if h < HEADS - 1 else (after, 1 - p, 0) if after else None
                    step(prev, (cur, p, h), nxt)
            tiles(eng, tile_step)

        def key_ap(b, p):
            return k_smp if b.smp else kw[:, p]

        with nc.Block() as block:
            @block.sync
            def _(sp):
                back = bass.AP(d["rel_bias"].tensor, REL - 1, [[REL, HEADS], [-1, REL]])
                sp.dma_start(ext[:, WIN - P - 1:WIN - P - 1 + REL], back, allow_slow_non_contiguous=True).then_inc(table_loaded, 16)
                sp.wait_ge(ext_done, 1)
                sp.dma_start(d["rel_ext"], ext[:]).then_inc(ext_stored, 16)
                sp.wait_ge(ext_stored, 16)
                toeplitz = bass.AP(d["rel_ext"].tensor, 0, [[1, P], [WIN + P, HEADS], [1, WIN]])
                sp.dma_start(bias_up[:], toeplitz).then_inc(bias_loaded, 16)
                k_t = d["qk_t"].rearrange("(m p) c -> p m c", p=P)

                def load_qk(b, p):
                    if b.smp:
                        return
                    alone(sp) if not isinstance(b.t, int) else None
                    sp.dma_start(q[:, p], k_t[:, 0:NP_, tile_rows(b.t)]).then_inc(qk_loaded[p], 16)
                    first = (b.t + 1 - b.nb) * P
                    cols = slice(first, first + b.width) if isinstance(b.t, int) else bass.ds(first, b.width)
                    sp.dma_start(kw[:, p, :, :b.width], k_t[:, NP_:, cols]).then_inc(qk_loaded[p], 16)

                load_qk(Band(0), 0)
                sp.dma_start(q_smp[:], k_t[:, 0:NP_, SEQ:ROWS]).then_inc(smp_qk_loaded, 16)
                sp.dma_start(k_smp[:, :, CACHE:], k_t[:, NP_:, SEQ:ROWS]).then_inc(smp_qk_loaded, 16)

                def step(before, cur, after, p, i):
                    if after is not None and not after.smp:
                        wait_if(sp, s_done, HEADS * cur.t)
                        load_qk(after, 1 - p)
                tiles(sp, step)
                sp.wait_ge(rows_done, 5)
                sp.dma_start(d["prompt_k"].rearrange("(b p) w -> p b w", p=P), k_rows[:, 0:4, :]).then_inc(rows_stored, 16)
                sp.dma_start(d["sample_k"], k_rows[:NSMP, 4, :]).then_inc(rows_stored, 16)
                sp.wait_ge(rows_stored, 32)

            @block.gpsimd
            def _(pool):
                pool.dma_start(cache[:], d["cache_k"].rearrange("(b p) w -> p b w", p=P)).then_inc(cache_loaded, 16)
                make_identity(pool, ident, zero_done, ident_done)
                v_blocks = d["v_rows"][0:SEQ, :].rearrange("(b p) w -> p b w", p=P)

                def load_v(b, p):
                    if b.smp:
                        return
                    first = b.t + 1 - b.nb
                    blocks = slice(first, first + b.nb) if isinstance(b.t, int) else bass.ds(first, b.nb)
                    alone(pool) if not isinstance(b.t, int) else None
                    pool.dma_start(vw[:, p, :b.nb, :], v_blocks[:, blocks, :]).then_inc(v_loaded[p], 16)

                pool.memset(flip[:], 0.0).then_inc(zero_done, 1)
                pool.wait_ge(zero_done, 2)
                pool.affine_select(out=flip[:], in_=flip[:], compare_op=ALU.not_equal, fill=1.0, base=1 - P,
                                   pattern=[[1, P]], channel_multiplier=1).then_inc(flip_done, 1)
                load_v(Band(0), 0)
                pool.dma_start(v_smp[:, 0:4, :], d["cache_v"].rearrange("(b p) w -> p b w", p=P)).then_inc(smp_v_loaded, 16)
                pool.dma_start(v_smp[:NSMP, 4, :], d["v_rows"][SEQ:ROWS, :]).then_inc(smp_v_loaded, 16)
                pool.dma_start(d["prompt_v"], d["v_rows"][SEQ - 512:SEQ, :]).then_inc(caches_stored, 16)
                pool.dma_start(d["sample_v"], d["v_rows"][SEQ:ROWS, :]).then_inc(caches_stored, 16)
                pool.dma_start(d["sample_gmlp_v"], d["uv_rows"][SEQ:ROWS, CW:]).then_inc(caches_stored, 16)
                pool.wait_ge(bias_copied, HEADS)
                pool.memset(bias[0:64, :, WIN - 64:], MASKED)
                pool.memset(bias[64:P, :, 0:64], MASKED).then_inc(bias_done, 1)

                def store_o(b, p):
                    pool.wait_ge(o_done, HEADS * (b.t + 1))
                    alone(pool)
                    pool.dma_start(d["mixed"][tile_rows(b.t), 0:AW], o[:b.nq, p, :]).then_inc(o_stored[p], 16)

                def step(before, cur, after, p, i):
                    if after is not None and not after.smp:
                        wait_if(pool, pv_done, HEADS * cur.t)
                        load_v(after, 1 - p)
                    if before is not None:
                        store_o(before, 1 - p)
                tiles(pool, step)
                store_o(Band(NT), 0)
                pool.wait_ge(o_stored[0], 16 * 9)
                pool.wait_ge(o_stored[1], 16 * 8)
                pool.wait_ge(caches_stored, 48)

            @block.vector
            def _(dve):
                dve.wait_ge(table_loaded, 16)
                lo, hi = WIN - P - 1, WIN - P - 1 + REL
                dve.tensor_copy(ext[:, 0:lo], ext[:, lo:lo + 1].to_broadcast([HEADS, lo]))
                dve.tensor_copy(ext[:, hi:], ext[:, hi - 1:hi].to_broadcast([HEADS, WIN + P - hi])).then_inc(ext_done, 1)
                dve.wait_ge(bias_done, 1)

                def add_bias(x):
                    b, p, h = x
                    n, par = HEADS * b.t + h, h % 2
                    dve.wait_ge(s_done, n + 1)
                    wait_if(dve, turned, n - 1)
                    alone(dve)
                    dve.tensor_tensor_reduce(out=s[:b.nq, par, :b.width], in0=ps_s[:b.nq, par, :b.width],
                                             in1=bias[:b.nq, h, b.col0:b.col0 + b.width], scale=1.0, scalar=-3e38,
                                             op0=ALU.add, op1=ALU.max, accum_out=top[:b.nq, par:par + 1]).then_inc(biased, 1)
                    dve.wait_ge(biased, n + 1)
                    dve.tensor_scalar(ntop[:b.nq, par:par + 1], top[:b.nq, par:par + 1], -1.0, None,
                                      ALU.mult).then_inc(ntop_done, 1)

                def normalise(x):
                    b, p, h = x
                    n, par = HEADS * b.t + h, h % 2
                    if h == 0 and not (isinstance(b.t, int) and b.t < 2):
                        dve.wait_ge(o_stored[p], 16 * (b.t // 2) if isinstance(b.t, int) else o_before(b, p))
                    dve.wait_ge(pv_done, n + 1)
                    dve.reciprocal(inv[:b.nq, par:par + 1], total[:b.nq, h % 3:h % 3 + 1]).then_inc(inv_done, 1)
                    dve.wait_ge(inv_done, n + 1)
                    dve.tensor_scalar(o[:b.nq, p, h * HD:(h + 1) * HD], ps_o[:b.nq, par, 0:HD], inv[:b.nq, par:par + 1],
                                      None, ALU.mult).then_inc(o_done, 1)

                def o_before(b, p):
                    return 8 * (b.t - p)

                add_bias((Band(0), 0, 0))

                def step(prev, cur, nxt):
                    if nxt:
                        add_bias(nxt)
                    if prev:
                        normalise(prev)
                heads(dve, step)
                normalise((Band(NT), 0, HEADS - 1))
                for b in range(5):
                    n = P if b < 4 else NSMP
                    dve.wait_ge(rows_turned, b + 1)
                    src = ps_s[:n, b // 2, (b % 2) * 512:(b % 2) * 512 + AW] if b < 4 else ps_t[:n, 0:AW]
                    dve.tensor_copy(k_rows[:n, b, :], src).then_inc(rows_done, 1)

            @block.scalar
            def _(act):
                for b in range(4):
                    act.wait_ge(cache_turned, b + 1)
                    bank = ps_s[:, b // 2, (b % 2) * 512:(b % 2) * 512 + AW].rearrange("p (m c) -> p m c", m=NP_)
                    act.copy(k_smp[:, :, b * P:(b + 1) * P], bank).then_inc(cache_done, 1)

                def exp(x):
                    b, p, h = x
                    n, par = HEADS * b.t + h, h % 2
                    act.wait_ge(ntop_done, n + 1)
                    act.activation(s[:b.nq, par, :b.width], s[:b.nq, par, :b.width], ACT.Exp,
                                   bias=ntop[:b.nq, par:par + 1],
                                   accum_out=total[:b.nq, h % 3:h % 3 + 1]).then_inc(exp_done, 1)

                def take_pt(x):
                    b, p, h = x
                    n, par = HEADS * b.t + h, h % 2
                    act.wait_ge(turned, n + 1)
                    wait_if(act, pv_done, n - 1)
                    full = b.width // P
                    ins = act.copy(pt[:, par, 0:full, :b.nq],
                                   ps_t[:, 0:full * P].rearrange("p (b c) -> p b c", b=full)[:, :, :b.nq])
                    if b.width % P:
                        w = b.width % P
                        ins = act.copy(pt[:w, par, full, :b.nq], ps_t[:w, full * P:full * P + b.nq])
                    ins.then_inc(pt_done, 1)

                for h in range(HEADS):
                    act.wait_ge(bias_flipped, h + 1)
                    act.copy(bias[:, h, :], (ps_s[:, 0] if h % 2 == 0 else ps_t)[:, 0:WIN]).then_inc(bias_copied, 1)

                exp((Band(0), 0, 0))

                def step(prev, cur, nxt):
                    take_pt(cur)
                    if nxt:
                        exp(nxt)
                heads(act, step)

            @block.tensor
            def _(pe):
                pe.wait_ge(ident_done, 1)
                pe.wait_ge(cache_loaded, 16)
                for b in range(4):
                    bank = ps_s[:, b // 2, (b % 2) * 512:(b % 2) * 512 + AW]
                    for j in range(NP_):
                        last = pe.transpose(bank[:, j * P:(j + 1) * P], cache[:, b, j * P:(j + 1) * P], ident[:])
                    last.then_inc(cache_turned, 1)
                pe.wait_ge(cache_done, 4)
                pe.wait_ge(flip_done, 1)
                pe.wait_ge(bias_loaded, 16)
                for h in range(HEADS):
                    wait_if(pe, bias_copied, h - 1)
                    dst = ps_s[:, 0] if h % 2 == 0 else ps_t
                    pe.matmul(dst[:, 0:512], flip[:], bias_up[:, h, 0:512], start=True, stop=True)
                    pe.matmul(dst[:, 512:WIN], flip[:], bias_up[:, h, 512:], start=True, stop=True).then_inc(bias_flipped, 1)
                pe.wait_ge(bias_copied, HEADS)
                pe.wait_ge(smp_qk_loaded, 32)
                pe.wait_ge(smp_v_loaded, 32)

                def score(x):
                    b, p, h = x
                    n, par = HEADS * b.t + h, h % 2
                    if h == 0 and not b.smp:
                        pe.wait_ge(qk_loaded[p], 32 * (b.t // 2 + 1) if isinstance(b.t, int) else 16 * (b.t - p) + 32)
                    wait_if(pe, biased, n - 1)
                    rows = slice(64 * par, 64 * par + 64)
                    keys = key_ap(b, p)
                    queries = q_smp if b.smp else q[:, p]
                    for c in range(0, b.width, 512):
                        w = min(512, b.width - c)
                        last = pe.matmul(ps_s[:b.nq, par, c:c + w], queries[rows, h // 2, :b.nq],
                                         keys[rows, h // 2, c:c + w], start=True, stop=True)
                    last.then_inc(s_done, 1)

                def turn(x):
                    b, p, h = x
                    n, par = HEADS * b.t + h, h % 2
                    pe.wait_ge(exp_done, n + 1)
                    wait_if(pe, pt_done, n)
                    for k in range(b.nb if not b.smp else 5):
                        w = b.block_rows(k)
                        last = pe.transpose(ps_t[:w, k * P:k * P + b.nq], s[:b.nq, par, k * P:k * P + w],
                                            ident[:b.nq, :b.nq])
                    last.then_inc(turned, 1)

                def out(x):
                    b, p, h = x
                    n, par = HEADS * b.t + h, h % 2
                    if h == 0 and not b.smp:
                        pe.wait_ge(v_loaded[p], 16 * (b.t // 2 + 1) if isinstance(b.t, int) else 8 * (b.t - p) + 16)
                    pe.wait_ge(pt_done, n + 1)
                    wait_if(pe, o_done, n - 1)
                    vals = v_smp if b.smp else vw[:, p]
                    nb = 5 if b.smp else b.nb
                    for k in range(nb):
                        w = b.block_rows(k)
                        last = pe.matmul(ps_o[:b.nq, par, 0:HD], pt[:w, par, k, :b.nq],
                                         vals[:w, k, h * HD:(h + 1) * HD], start=(k == 0), stop=(k == nb - 1))
                    last.then_inc(pv_done, 1)

                score((Band(0), 0, 0))

                def step(prev, cur, nxt):
                    if nxt:
                        score(nxt)
                    turn(cur)
                    if prev:
                        out(prev)
                heads(pe, step)
                out((Band(NT), 0, HEADS - 1))
                for b in range(5):
                    if b == 4:
                        pe.wait_ge(pt_done, HEADS * (NT + 1))
                    n = P if b < 4 else NSMP
                    dst = ps_s[:n, b // 2, (b % 2) * 512:(b % 2) * 512 + AW] if b < 4 else ps_t[:n, 0:AW]
                    for j in range(NP_):
                        src = kw[:, 1, j, (b + 1) * P:(b + 2) * P] if b < 4 else k_smp[:, j, CACHE:]
                        last = pe.transpose(dst[:, j * P:(j + 1) * P], src, ident[:])
                    last.then_inc(rows_turned, 1)


def ssd_and_gmlp(nc, d):
    with nc.cleanup_on_exit(), ExitStack() as ctx:
        m = Stage(nc, ctx, "sg")
        NC_ = NT + 1
        ident, upper, ones = m.sb("ident", [P, P]), m.sb("upper", [P, P]), m.sb("ones", [P, P])
        dt = m.sb("dt", [P, NC_, HEADS])
        e, w2, num, den = m.sb("e", [P, NC_, HEADS]), m.sb("w2", [P, NC_, HEADS]), m.sb("num", [P, NC_, HEADS]), m.sb("den", [P, NC_, HEADS])
        dta, ncum, ecum, dts, etot = (m.sb("dta", [P, NC_, HEADS]), m.sb("ncum", [P, NC_, HEADS]), m.sb("ecum", [P, NC_, HEADS]),
                                      m.sb("dts", [P, NC_, HEADS]), m.sb("etot", [P, NC_, HEADS]))
        dt_bias, a_row, d_row = m.sb("dt_bias", [P, HEADS]), m.sb("a_row", [P, HEADS]), m.sb("d_row", [P, HEADS])
        ws, wt, gb = m.sb("ws", [P, CG, P]), m.sb("wt", [P, CG, P]), m.sb("gb", [P, CG])
        st_in, st_out = m.sb("st_in", [P, 3, P]), m.sb("st_out", [P, 2, 3, P])
        state = m.sb("state", [P, AW])
        decayed = m.sb("decayed", [P, AW])
        xbc = m.sb("xbc", [P, 2, NXBC, P])
        z, uv = m.sb("z", [P, 2, AW]), m.sb("uv", [P, 2, 2 * CW])
        dta_t = m.sb("dta_t", [P, 2, HEADS])
        rows = m.sb("rows", [P, 2, AW + 2 * STATE])
        xdt, xds, xd = m.sb("xdt", [P, 2, AW]), m.sb("xds", [P, 2, AW]), m.sb("xd", [P, 2, AW])
        seg, cbm, mix = m.sb("seg", [P, 2, HEADS, P]), m.sb("cbm", [P, 2, 2, P]), m.sb("mix", [P, 2, HEADS, P])
        y1, y2, y3 = m.sb("y1", [P, AW]), m.sb("y2", [P, AW]), m.sb("y3", [P, AW])
        ob, oc = m.sb("ob", [P, 2, AW]), m.sb("oc", [P, 2, CW])
        ps_a, ps_r = m.ps("ps_a", [P, 1024]), m.ps("ps_r", [P, 1024])
        ps_c, ps_off, ps_diag, ps_st = m.ps("ps_c", [P, 512]), m.ps("ps_off", [P, 512]), m.ps("ps_diag", [P, 512]), m.ps("ps_st", [P, 512])

        zero_done, ident_done, const_done = m.sem("zero_done"), m.sem("ident_done"), m.sem("const_done")
        small_loaded, prep, prep_done, prep_act, prep_pe = (m.sem("small_loaded"), m.sem("prep"), m.sem("prep_done"), m.sem("prep_act"),
                                                           m.sem("prep_pe"))
        loaded = [m.sem("loaded0"), m.sem("loaded1")]
        dta_done, cum_done, rows_turned, cb_done = m.sem("dta_done"), m.sem("cum_done"), m.sem("rows_turned"), m.sem("cb_done")
        rows_done, seg_done, clip_done, exp_done, cbm_done, mix_done = (m.sem("rows_done"), m.sem("seg_done"), m.sem("clip_done"),
                                                                        m.sem("exp_done"), m.sem("cbm_done"), m.sem("mix_done"))
        scaled, off_done, st_done, diag_done, gm_done = m.sem("scaled"), m.sem("off_done"), m.sem("st_done"), m.sem("diag_done"), m.sem("gm_done")
        y1_done, y2_done, y3_done, ob_done, oc_done = m.sem("y1_done"), m.sem("y2_done"), m.sem("y3_done"), m.sem("ob_done"), m.sem("oc_done")
        decayed_done, state_done = m.sem("decayed_done"), m.sem("state_done")
        o_stored = [m.sem("o_stored0"), m.sem("o_stored1")]
        ncum_done, dta_all_done = m.sem("ncum_done"), m.sem("dta_all_done")
        fin_turned, fin_done, fin_stored, init_turned = m.sem("fin_turned"), m.sem("fin_done"), m.sem("fin_stored"), m.sem("init_turned")

        def chunks(eng, step):
            step(0, 0, 0)
            step(1, 1, 0)
            with eng.Fori(1, 7) as i:
                step(2 * i, 0, i)
                step(2 * i + 1, 1, i)
            for t in (14, 15, 16):
                step(t, t % 2, t // 2)

        def col(t):
            return slice(t, t + 1) if isinstance(t, int) else bass.ds(t, 1)

        def per_head(a, t):
            return a[:, col(t), :].rearrange("p a h -> p (a h)").unsqueeze(2).to_broadcast([P, HEADS, HD])

        def by_head(a):
            return a.rearrange("p (h c) -> p h c", h=HEADS)

        with nc.Block() as block:
            @block.sync
            def _(sp):
                sp.dma_start(dt[:, 0:NT, :], d["dt_rows"][0:SEQ, :].rearrange("(t p) h -> p t h", p=P)).then_inc(small_loaded, 16)
                sp.dma_start(dt[:NSMP, NT, :], d["dt_rows"][SEQ:ROWS, :]).then_inc(small_loaded, 16)
                sp.dma_start(dt_bias[:], bc_row(d["ssm_dt_bias"], HEADS)).then_inc(small_loaded, 16)
                sp.dma_start(a_row[:], bc_row(d["ssm_a_log"], HEADS)).then_inc(small_loaded, 16)
                sp.dma_start(d_row[:], bc_row(d["ssm_d"], HEADS)).then_inc(small_loaded, 16)
                sp.dma_start(ws[:], d["gmlp_w"].rearrange("g i j -> i g j")).then_inc(small_loaded, 16)
                sp.dma_start(gb[:], d["gmlp_b"].rearrange("g i -> i g"), allow_slow_non_contiguous=True).then_inc(small_loaded, 16)
                sp.dma_start(st_in[:], d["state_ssm"].rearrange("(m p) n -> p m n", p=P)).then_inc(small_loaded, 16)

                def load(t, p):
                    n = n_rows(t)
                    sp.dma_start(xbc[:, p, :, :n], d["xbc_t"][:, :, tile_rows(t)]).then_inc(loaded[p], 16)
                    sp.dma_start(z[:n, p, :], d["z_rows"][tile_rows(t), :]).then_inc(loaded[p], 16)
                    sp.dma_start(uv[:n, p, :], d["uv_rows"][tile_rows(t), :]).then_inc(loaded[p], 16)

                load(0, 0)
                load(1, 1)

                def step(t, p, i):
                    if not isinstance(t, int) or t + 2 <= NT:
                        sp.wait_ge(gm_done, t + 1)
                        sp.wait_ge(ob_done, t + 1)
                        sp.wait_ge(oc_done, t + 1)
                        alone(sp)
                        load(t + 2, p)
                chunks(sp, step)

            @block.gpsimd
            def _(pool):
                make_identity(pool, ident, zero_done, ident_done)
                pool.memset(ones[:], 1.0).then_inc(zero_done, 1)
                pool.wait_ge(zero_done, 2)
                pool.affine_select(out=upper[:], in_=ones[:], compare_op=ALU.is_ge, fill=0.0, base=0,
                                   pattern=[[1, P]], channel_multiplier=-1).then_inc(const_done, 1)

                def scale(t, p, i):
                    n = n_rows(t)
                    pool.wait_ge(rows_done, t + 1)
                    if not (isinstance(t, int) and t < 2):
                        pool.wait_ge(diag_done, t - 1)
                        pool.wait_ge(y2_done, t - 1)
                    x = by_head(rows[:n, p, 0:AW])
                    pool.tensor_tensor(by_head(xdt[:n, p, :]), x, per_head(dt, t)[:n], ALU.mult)
                    pool.tensor_tensor(by_head(xds[:n, p, :]), x, per_head(dts, t)[:n], ALU.mult)
                    pool.tensor_tensor(by_head(xd[:n, p, :]), x, d_row[:n, :].unsqueeze(2).to_broadcast([n, HEADS, HD]),
                                       ALU.mult).then_inc(scaled, 1)

                def front(t, p, i):
                    n = n_rows(t)
                    pool.wait_ge(seg_done, t + 1)
                    alone(pool)
                    pool.tensor_scalar(seg[:n, p, :, :n], seg[:n, p, :, :n], 0.0, None, ALU.min).then_inc(clip_done, 1)
                    scale(t, p, i)

                def back(t, p, i):
                    n = n_rows(t)
                    pool.wait_ge(state_done, NT + 2 if isinstance(t, int) and t == NT else t + 1)
                    pool.tensor_tensor(by_head(decayed[:]), by_head(state[:]), per_head(etot, t), ALU.mult).then_inc(decayed_done, 1)
                    pool.wait_ge(y1_done, t + 1)
                    wait_if(pool, y3_done, t)
                    pool.tensor_tensor(y2[:n, :], y1[:n, :], xd[:n, p, :], ALU.add).then_inc(y2_done, 1)
                    pool.wait_ge(y3_done, t + 1)
                    if not (isinstance(t, int) and t < 2):
                        pool.wait_ge(o_stored[p], 32 * i)
                    pool.tensor_tensor(ob[:n, p, :], y3[:n, :], z[:n, p, :], ALU.mult).then_inc(ob_done, 1)
                    pool.wait_ge(ob_done, t + 1)
                    alone(pool)
                    pool.dma_start(d["mixed"][tile_rows(t), AW:2 * AW], ob[:n, p, :]).then_inc(o_stored[p], 16)
                    pool.wait_ge(oc_done, t + 1)
                    alone(pool)
                    pool.dma_start(d["mixed"][tile_rows(t), 2 * AW:], oc[:n, p, :]).then_inc(o_stored[p], 16)

                pool.wait_ge(prep_done, 1)
                front(0, 0, 0)

                def step(t, p, i):
                    if not isinstance(t, int) or t + 1 <= NT:
                        front(t + 1, 1 - p, i + p)
                    back(t, p, i)
                chunks(pool, step)
                pool.wait_ge(fin_done, 1)
                pool.dma_start(d["prompt_ssm"].rearrange("(m p) n -> p m n", p=P), st_out[:, 0]).then_inc(fin_stored, 16)
                pool.wait_ge(fin_done, 2)
                pool.dma_start(d["sample_ssm"].rearrange("(m p) n -> p m n", p=P), st_out[:, 1]).then_inc(fin_stored, 16)
                pool.wait_ge(fin_stored, 32)
                pool.wait_ge(o_stored[0], 32 * 9)
                pool.wait_ge(o_stored[1], 32 * 8)

            @block.scalar
            def _(act):
                act.wait_ge(small_loaded, 128)
                act.activation(a_row[:], a_row[:], ACT.Exp).then_inc(prep_act, 1)
                act.wait_ge(prep, 2)
                act.activation(e[:], e[:], ACT.Exp).then_inc(prep_act, 1)
                act.wait_ge(ncum_done, 2)
                act.activation(ecum[:], ncum[:], ACT.Exp, scale=-1.0)
                act.activation(etot[:], ps_r[:, 0:NC_ * HEADS].rearrange("p (t h) -> p t h", h=HEADS), ACT.Exp)
                act.activation(den[:], num[:], ACT.Exp).then_inc(prep_act, 1)
                act.wait_ge(prep_done, 1)

                def front(t, p, i):
                    n = n_rows(t)
                    act.wait_ge(rows_turned, t + 1)
                    if not (isinstance(t, int) and t < 2):
                        act.wait_ge(scaled, t - 1)
                        act.wait_ge(st_done, t - 1)
                    act.copy(rows[:n, p, :], ps_r[:n, 0:AW + 2 * STATE]).then_inc(rows_done, 1)
                    act.wait_ge(clip_done, t + 1)
                    act.activation(seg[:n, p, :, :n], seg[:n, p, :, :n], ACT.Exp).then_inc(exp_done, 1)

                front(0, 0, 0)

                def step(t, p, i):
                    if not isinstance(t, int) or t + 1 <= NT:
                        front(t + 1, 1 - p, i + p)
                chunks(act, step)
                for f in range(2):
                    act.wait_ge(fin_turned, f + 1)
                    act.copy(st_out[:, f], ps_st[:, 0:AW].rearrange("p (m n) -> p m n", m=3)).then_inc(fin_done, 1)

            @block.vector
            def _(dve):
                count = [0]

                def link(ins):
                    count[0] += 1
                    ins.then_inc(prep, 1)
                    dve.wait_ge(prep, count[0])

                dve.memset(dt[NSMP:, NT, :], 0.0)
                dve.memset(state[:], 0.0).then_inc(state_done, 1)
                dve.wait_ge(state_done, 1)
                dve.wait_ge(small_loaded, 128)
                link(dve.tensor_tensor(dt[:], dt[:], dt_bias[:].unsqueeze(1).to_broadcast([P, NC_, HEADS]), ALU.add))
                link(dve.scalar_tensor_tensor(out=e[:], in0=dt[:], scalar=-1.0, in1=dt[:], op0=ALU.mult, op1=ALU.min))
                dve.wait_ge(prep_act, 2)
                link(dve.tensor_scalar(den[:], e[:], 2.0, None, ALU.add))
                link(dve.reciprocal(den[:], den[:]))
                link(dve.tensor_tensor(e[:], e[:], den[:], ALU.mult))
                link(dve.tensor_tensor(w2[:], e[:], e[:], ALU.mult))
                link(dve.tensor_scalar(num[:], w2[:], 1.0 / 17, None, ALU.mult))
                for k in (15, 13, 11, 9, 7, 5, 3):
                    link(dve.scalar_tensor_tensor(out=num[:], in0=num[:], scalar=1.0 / k, in1=w2[:], op0=ALU.add, op1=ALU.mult))
                link(dve.scalar_tensor_tensor(out=num[:], in0=num[:], scalar=1.0, in1=e[:], op0=ALU.add, op1=ALU.mult))
                link(dve.tensor_scalar(dt[:], dt[:], 0.0, None, ALU.max))
                link(dve.scalar_tensor_tensor(out=dt[:], in0=num[:], scalar=2.0, in1=dt[:], op0=ALU.mult, op1=ALU.add))
                link(dve.tensor_scalar(a_row[:], a_row[:], -1.0, None, ALU.mult))
                link(dve.tensor_tensor(dta[:], dt[:], a_row[:].unsqueeze(1).to_broadcast([P, NC_, HEADS]), ALU.mult))
                dve.memset(dta[NSMP:, NT, :], 0.0).then_inc(dta_all_done, 1)
                dve.wait_ge(dta_all_done, 1)
                dve.wait_ge(prep_pe, 1)
                dve.tensor_scalar(ncum[:], ps_a[:, 0:NC_ * HEADS].rearrange("p (t h) -> p t h", h=HEADS), -1.0, None,
                                  ALU.mult).then_inc(ncum_done, 1)
                dve.wait_ge(ncum_done, 1)
                dve.tensor_tensor(num[:], ncum[:], ps_r[:, 0:NC_ * HEADS].rearrange("p (t h) -> p t h", h=HEADS),
                                  ALU.add).then_inc(ncum_done, 1)
                dve.wait_ge(prep_pe, 2)
                dve.tensor_tensor(wt[:], ps_off[:].rearrange("p (g j) -> p g j", g=CG),
                                  upper[:].unsqueeze(1).to_broadcast([P, CG, P]), ALU.mult)
                dve.wait_ge(prep_act, 3)
                dve.tensor_tensor(dts[:], dt[:], den[:], ALU.mult).then_inc(prep_done, 1)

                def take_dta(t, p):
                    if not (isinstance(t, int) and t < 2):
                        dve.wait_ge(cum_done, t - 1)
                    dve.tensor_copy(dta_t[:, p, :], dta[:, col(t), :].rearrange("p a h -> p (a h)")).then_inc(dta_done, 1)

                def differences(t, p):
                    n = n_rows(t)
                    dve.wait_ge(cum_done, t + 1)
                    dve.tensor_tensor(seg[:n, p, :, :n], ps_a[:n, 0:HEADS * P].rearrange("p (h l) -> p h l", h=HEADS)[:, :, :n],
                                      ncum[:n, col(t), :].rearrange("p a h -> p (a h)").unsqueeze(2).to_broadcast([n, HEADS, n]),
                                      ALU.add).then_inc(seg_done, 1)
                    dve.wait_ge(cb_done, t + 1)
                    dve.tensor_tensor(cbm[:n, p, :, :n], ps_c[:n, 0:2 * P].rearrange("p (g l) -> p g l", g=2)[:, :, :n],
                                      upper[:n, :n].unsqueeze(1).to_broadcast([n, 2, n]), ALU.mult).then_inc(cbm_done, 1)

                def mixing(t, p):
                    n = n_rows(t)
                    dve.wait_ge(exp_done, t + 1)
                    dve.wait_ge(cbm_done, t + 1)
                    if not (isinstance(t, int) and t < 2):
                        dve.wait_ge(diag_done, t - 1)
                    for g in range(2):
                        last = dve.tensor_tensor(mix[:n, p, 3 * g:3 * g + 3, :n], seg[:n, p, 3 * g:3 * g + 3, :n],
                                                 cbm[:n, p, g, :n].unsqueeze(1).to_broadcast([n, 3, n]), ALU.mult)
                    last.then_inc(mix_done, 1)

                take_dta(0, 0)
                take_dta(1, 1)
                differences(0, 0)
                mixing(0, 0)

                def step(t, p, i):
                    n = n_rows(t)
                    more = not isinstance(t, int) or t + 1 <= NT
                    if not isinstance(t, int) or t + 2 <= NT:
                        take_dta(t + 2, p)
                    if more:
                        differences(t + 1, 1 - p)
                    dve.wait_ge(off_done, t + 1)
                    wait_if(dve, y2_done, t)
                    dve.tensor_tensor(by_head(y1[:n, :]), by_head(ps_off[:n, 0:AW]), per_head(ecum, t)[:n], ALU.mult).then_inc(y1_done, 1)
                    dve.wait_ge(decayed_done, t + 1)
                    dve.tensor_tensor(state[:], decayed[:], ps_st[:, 0:AW], ALU.add).then_inc(state_done, 1)
                    if more:
                        mixing(t + 1, 1 - p)
                    dve.wait_ge(diag_done, t + 1)
                    dve.wait_ge(y2_done, t + 1)
                    wait_if(dve, ob_done, t)
                    dve.tensor_tensor(y3[:n, :], y2[:n, :], ps_diag[:n, 0:AW], ALU.add).then_inc(y3_done, 1)
                    dve.wait_ge(gm_done, t + 1)
                    if not (isinstance(t, int) and t < 2):
                        dve.wait_ge(o_stored[p], 32 * i)
                    for g in range(CG):
                        c = slice(g * 64, g * 64 + 64)
                        last = dve.scalar_tensor_tensor(out=oc[:n, p, c], in0=ps_c[:n, 2 * P + g * 64:2 * P + g * 64 + 64],
                                                        scalar=gb[:n, g:g + 1], in1=uv[:n, p, c], op0=ALU.add, op1=ALU.mult)
                    last.then_inc(oc_done, 1)
                    if isinstance(t, int) and t == NT - 1:
                        dve.wait_ge(init_turned, 1)
                        dve.tensor_copy(state[:], ps_st[:, 0:AW]).then_inc(state_done, 1)
                chunks(dve, step)

            @block.tensor
            def _(pe):
                pe.wait_ge(const_done, 1)
                pe.wait_ge(ident_done, 1)
                pe.wait_ge(small_loaded, 128)
                for g in range(CG):
                    last = pe.transpose(ps_off[:, g * P:(g + 1) * P], ws[:, g, :], ident[:])
                pe.wait_ge(dta_all_done, 1)
                flat = dta[:].rearrange("p t h -> p (t h)")
                pe.matmul(ps_a[:, 0:NC_ * HEADS], upper[:], flat, start=True, stop=True)
                pe.matmul(ps_r[:, 0:NC_ * HEADS], ones[:], flat, start=True, stop=True).then_inc(prep_pe, 1)
                pe.transpose(ps_off[:, 3 * P:4 * P], ws[:, 3, :], ident[:]).then_inc(prep_pe, 1)

                def front(t, p, i):
                    n = n_rows(t)
                    pe.wait_ge(loaded[p], 48 * (i + 1))
                    if isinstance(t, int) and t == 0:
                        pe.wait_ge(prep_done, 1)
                    wait_if(pe, rows_done, t)
                    for j in range(5):
                        last = pe.transpose(ps_r[:n, j * P:(j + 1) * P], xbc[:, p, j, :n], ident[:])
                    last.then_inc(rows_turned, 1)
                    pe.wait_ge(dta_done, t + 1)
                    wait_if(pe, seg_done, t)
                    for h in range(HEADS):
                        last = pe.matmul(ps_a[:n, h * P:h * P + n], dta_t[:n, p, h:h + 1].to_broadcast([n, n]), upper[:n, :n],
                                         start=True, stop=True)
                    last.then_inc(cum_done, 1)
                    wait_if(pe, cbm_done, t)
                    wait_if(pe, oc_done, t - 1)
                    for g in range(2):
                        last = pe.matmul(ps_c[:n, g * P:g * P + n], xbc[:, p, 3 + g, :n], xbc[:, p, 5 + g, :n], start=True, stop=True)
                    last.then_inc(cb_done, 1)

                front(0, 0, 0)

                def step(t, p, i):
                    n = n_rows(t)
                    more = not isinstance(t, int) or t + 1 <= NT
                    if more:
                        front(t + 1, 1 - p, i + p)
                    pe.wait_ge(scaled, t + 1)
                    pe.wait_ge(state_done, NT + 2 if isinstance(t, int) and t == NT else t + 1)
                    for g in range(2):
                        c = slice(3 * g * HD, 3 * (g + 1) * HD)
                        last = pe.matmul(ps_st[:, c], rows[:n, p, AW + g * P:AW + (g + 1) * P], xds[:n, p, c], start=True, stop=True)
                    last.then_inc(st_done, 1)
                    wait_if(pe, y1_done, t)
                    for g in range(2):
                        c = slice(3 * g * HD, 3 * (g + 1) * HD)
                        last = pe.matmul(ps_off[:n, c], xbc[:, p, 5 + g, :n], state[:, c], start=True, stop=True)
                    last.then_inc(off_done, 1)
                    pe.wait_ge(mix_done, t + 1)
                    wait_if(pe, y3_done, t)
                    for h in range(HEADS):
                        c = slice(h * HD, (h + 1) * HD)
                        last = pe.matmul(ps_diag[:n, c], mix[:n, p, h, :n], xdt[:n, p, c], start=True, stop=True)
                    last.then_inc(diag_done, 1)
                    if more:
                        pe.wait_ge(cbm_done, t + 2)
                    for g in range(CG):
                        last = pe.matmul(ps_c[:n, 2 * P + g * 64:2 * P + g * 64 + 64], wt[:n, g, :n],
                                         uv[:n, p, CW + g * 64:CW + (g + 1) * 64], start=True, stop=True)
                    last.then_inc(gm_done, 1)
                    if isinstance(t, int) and t == NT - 1:
                        turn_state(NT + 1)
                        pe.wait_ge(fin_done, 1)
                        for j in range(3):
                            last = pe.transpose(ps_st[:, j * P:(j + 1) * P], st_in[:, j, :], ident[:])
                        last.then_inc(init_turned, 1)

                def turn_state(value):
                    pe.wait_ge(state_done, value)
                    for j in range(3):
                        last = pe.transpose(ps_st[:, j * P:(j + 1) * P], state[:, j * P:(j + 1) * P], ident[:])
                    last.then_inc(fin_turned, 1)
                chunks(pe, step)
                turn_state(NT + 3)


def mix_out(nc, d):
    with nc.cleanup_on_exit(), ExitStack() as ctx:
        m = Stage(nc, ctx, "mo")
        segs = [(0, AW), (AW, AW), (2 * AW, CW)]
        w_raw = m.sb("w_raw", [P, 2, D])
        w_hi, w_lo = m.sb("w_hi", [P, KD, D], F32R), m.sb("w_lo", [P, KD, D], F32R)
        g_mix, g_ln, b_ln = m.sb("g_mix", [P, D]), m.sb("g_ln", [P, D]), m.sb("b_ln", [P, D])
        mx, x, y = m.sb("mx", [P, 2, D]), m.sb("x", [P, 2, D]), m.sb("y", [P, 2, D])
        sq, ss, rms, inv = m.sb("sq", [P, D]), m.sb("ss", [P, 3]), m.sb("rms", [P, 3]), m.sb("inv", [P, 3])
        mt_hi, mt_lo = m.sb("mt_hi", [P, 2, KD, P], F32R), m.sb("mt_lo", [P, 2, KD, P], F32R)
        yt_hi, yt_lo = m.sb("yt_hi", [P, 2, KD, P], F32R), m.sb("yt_lo", [P, 2, KD, P], F32R)
        stats, mv, sd, rs = m.sb("stats", [P, 2, 6]), m.sb("mv", [P, 2]), m.sb("sd", [P, 2]), m.sb("rs", [P, 1])
        ident = m.sb("ident", [P, P])
        ps_m, ps_y, ps_t = m.ps("ps_m", [P, KD, P]), m.ps("ps_y", [P, 2, D]), m.ps("ps_t", [P, KD, P])

        zero_done, ident_done = m.sem("zero_done"), m.sem("ident_done")
        w_loaded = [m.sem("w_loaded0"), m.sem("w_loaded1")]
        w_hi_done, w_lo_done, vec_loaded = m.sem("w_hi_done"), m.sem("w_lo_done"), m.sem("vec_loaded")
        mx_loaded, x_loaded = [m.sem("mx_loaded0"), m.sem("mx_loaded1")], [m.sem("x_loaded0"), m.sem("x_loaded1")]
        sq_done, ms_done, rms_done, inv_done, scaled, mx_done = (m.sem("sq_done"), m.sem("ms_done"), m.sem("rms_done"),
                                                                 m.sem("inv_done"), m.sem("scaled"), m.sem("mx_done"))
        m_turned, m_hi_done, m_lo_done, mm_done = m.sem("m_turned"), m.sem("m_hi_done"), m.sem("m_lo_done"), m.sem("mm_done")
        sum_done, bn_done, aggr_done, var_done, sd_done = (m.sem("sum_done"), m.sem("bn_done"), m.sem("aggr_done"), m.sem("var_done"),
                                                           m.sem("sd_done"))
        rs_done, xhat_done, gain_done, y_done = m.sem("rs_done"), m.sem("xhat_done"), m.sem("gain_done"), m.sem("y_done")
        y_turned, y_hi_done, y_lo_done = m.sem("y_turned"), m.sem("y_hi_done"), m.sem("y_lo_done")
        y_stored, yt_stored = [m.sem("y_stored0"), m.sem("y_stored1")], [m.sem("yt_stored0"), m.sem("yt_stored1")]

        def tiles(eng, step):
            step(0, 0, 0)
            step(1, 1, 0)
            with eng.Fori(1, 7) as i:
                step(2 * i, 0, i)
                step(2 * i + 1, 1, i)
            for t in (14, 15, 16):
                step(t, t % 2, t // 2)

        def early(t):
            return isinstance(t, int) and t < 2

        def exists(t, ahead):
            return not isinstance(t, int) or t + ahead <= NT

        with nc.Block() as block:
            @block.sync
            def _(sp):
                def load_mx(t, p):
                    n = n_rows(t)
                    if not early(t):
                        sp.wait_ge(m_turned, t - 1)
                    alone(sp) if not early(t) else None
                    sp.dma_start(mx[:n, p, :], d["mixed"][tile_rows(t), :]).then_inc(mx_loaded[p], 16)

                def load_x(t, p):
                    n = n_rows(t)
                    if not early(t):
                        sp.wait_ge(sum_done, t - 1)
                    alone(sp) if not early(t) else None
                    sp.dma_start(x[:n, p, :], d["x_rows"][tile_rows(t), :]).then_inc(x_loaded[p], 16)

                load_mx(0, 0)
                load_mx(1, 1)
                for k in range(KD):
                    if k >= 2:
                        sp.wait_ge(w_hi_done, k - 1)
                        sp.wait_ge(w_lo_done, k - 1)
                    sp.dma_start(w_raw[:, k % 2, :], d["w_out"][k * P:(k + 1) * P, :]).then_inc(w_loaded[k % 2], 16)
                load_x(0, 0)
                load_x(1, 1)

                def step(t, p, i):
                    if exists(t, 2):
                        load_mx(t + 2, p)
                    if exists(t, 2):
                        load_x(t + 2, p)
                tiles(sp, step)

            @block.gpsimd
            def _(pool):
                make_identity(pool, ident, zero_done, ident_done)
                pool.dma_start(g_mix[:], bc_row(d["mix_norm_g"], D)).then_inc(vec_loaded, 16)
                pool.dma_start(g_ln[:], bc_row(d["ln1_g"], D)).then_inc(vec_loaded, 16)
                pool.dma_start(b_ln[:], bc_row(d["ln1_b"], D)).then_inc(vec_loaded, 16)
                pool.wait_ge(vec_loaded, 48)

                def gain_mx(t, p):
                    n = n_rows(t)
                    pool.wait_ge(scaled, t + 1)
                    pool.tensor_tensor(mx[:n, p, :], mx[:n, p, :], g_mix[:n, :], ALU.mult).then_inc(mx_done, 1)

                def store_yt(t, p):
                    n = n_rows(t)
                    pool.wait_ge(y_hi_done, t + 1)
                    alone(pool)
                    pool.dma_start(d["x1t_hi"][:, :, tile_rows(t)], yt_hi[:, p, :, :n].bitcast(F32)).then_inc(yt_stored[p], 16)
                    pool.wait_ge(y_lo_done, t + 1)
                    alone(pool)
                    pool.dma_start(d["x1t_lo"][:, :, tile_rows(t)], yt_lo[:, p, :, :n].bitcast(F32)).then_inc(yt_stored[p], 16)

                gain_mx(0, 0)
                gain_mx(1, 1)

                def step(t, p, i):
                    n = n_rows(t)
                    if exists(t, 2):
                        gain_mx(t + 2, p)
                    pool.wait_ge(xhat_done, t + 1)
                    pool.tensor_tensor(y[:n, p, :], y[:n, p, :], g_ln[:n, :], ALU.mult).then_inc(gain_done, 1)
                    pool.wait_ge(gain_done, t + 1)
                    pool.tensor_tensor(y[:n, p, :], y[:n, p, :], b_ln[:n, :], ALU.add).then_inc(y_done, 1)
                    pool.wait_ge(y_done, t + 1)
                    alone(pool)
                    pool.dma_start(d["x1_rows"][tile_rows(t), :], y[:n, p, :]).then_inc(y_stored[p], 16)
                    if not (isinstance(t, int) and t == 0):
                        store_yt(t - 1, 1 - p)
                tiles(pool, step)
                store_yt(NT, 0)
                for p, count in ((0, 9), (1, 8)):
                    pool.wait_ge(y_stored[p], 16 * count)
                    pool.wait_ge(yt_stored[p], 32 * count)

            @block.scalar
            def _(act):
                def squares(t, p, i):
                    n = n_rows(t)
                    act.wait_ge(mx_loaded[p], 16 * (i + 1))
                    for s, (c, w) in enumerate(segs):
                        last = act.activation(sq[:n, c:c + w], mx[:n, p, c:c + w], ACT.Square, accum_out=ss[:n, s:s + 1])
                    last.then_inc(sq_done, 1)
                    act.wait_ge(ms_done, t + 1)
                    act.activation(rms[:n, :], ss[:n, :], ACT.Sqrt).then_inc(rms_done, 1)

                def hi_m(t, p):
                    n = n_rows(t)
                    act.wait_ge(m_turned, t + 1)
                    if not early(t):
                        act.wait_ge(mm_done, t - 1)
                    act.copy(mt_hi[:, p, :, :n], ps_m[:, :, :n]).then_inc(m_hi_done, 1)

                def hi_y(t, p, i):
                    n = n_rows(t)
                    act.wait_ge(y_turned, t + 1)
                    if not early(t):
                        act.wait_ge(yt_stored[p], 32 * i)
                    act.copy(yt_hi[:, p, :, :n], ps_t[:, :, :n]).then_inc(y_hi_done, 1)

                squares(0, 0, 0)
                for k in range(KD):
                    act.wait_ge(w_loaded[k % 2], 16 * (k // 2 + 1))
                    act.copy(w_hi[:, k, :], w_raw[:, k % 2, :]).then_inc(w_hi_done, 1)
                hi_m(0, 0)
                squares(1, 1, 0)

                def step(t, p, i):
                    n = n_rows(t)
                    if exists(t, 1):
                        hi_m(t + 1, 1 - p)
                    if exists(t, 2):
                        squares(t + 2, p, i + 1)
                    act.wait_ge(var_done, t + 1)
                    act.activation(sd[:n, 1:2], sd[:n, 0:1], ACT.Sqrt).then_inc(sd_done, 1)
                    if not (isinstance(t, int) and t == 0):
                        hi_y(t - 1, 1 - p, i - 1 + p)
                tiles(act, step)
                hi_y(NT, 0, NT // 2)

            @block.vector
            def _(dve):
                def scale(t, p):
                    n = n_rows(t)
                    dve.wait_ge(sq_done, t + 1)
                    dve.tensor_scalar(ss[:n, 0:2], ss[:n, 0:2], 1.0 / AW, EPS, ALU.mult, ALU.add)
                    dve.tensor_scalar(ss[:n, 2:3], ss[:n, 2:3], 1.0 / CW, EPS, ALU.mult, ALU.add).then_inc(ms_done, 1)
                    dve.wait_ge(rms_done, t + 1)
                    dve.reciprocal(inv[:n, :], rms[:n, :]).then_inc(inv_done, 1)
                    dve.wait_ge(inv_done, t + 1)
                    for s, (c, w) in enumerate(segs):
                        last = dve.tensor_scalar(mx[:n, p, c:c + w], mx[:n, p, c:c + w], inv[:n, s:s + 1], None, ALU.mult)
                    last.then_inc(scaled, 1)

                def lo_m(t, p):
                    n = n_rows(t)
                    dve.wait_ge(m_hi_done, t + 1)
                    dve.tensor_tensor(mt_lo[:, p, :, :n], ps_m[:, :, :n], mt_hi[:, p, :, :n].bitcast(F32),
                                      ALU.subtract).then_inc(m_lo_done, 1)

                def lo_y(t, p):
                    n = n_rows(t)
                    dve.wait_ge(y_hi_done, t + 1)
                    dve.tensor_tensor(yt_lo[:, p, :, :n], ps_t[:, :, :n], yt_hi[:, p, :, :n].bitcast(F32),
                                      ALU.subtract).then_inc(y_lo_done, 1)

                scale(0, 0)
                for k in range(KD):
                    dve.wait_ge(w_hi_done, k + 1)
                    dve.tensor_tensor(w_lo[:, k, :], w_raw[:, k % 2, :], w_hi[:, k, :].bitcast(F32),
                                      ALU.subtract).then_inc(w_lo_done, 1)
                lo_m(0, 0)
                scale(1, 1)

                def step(t, p, i):
                    n = n_rows(t)
                    if exists(t, 1):
                        lo_m(t + 1, 1 - p)
                    if exists(t, 2):
                        scale(t + 2, p)
                    dve.wait_ge(x_loaded[p], 16 * (i + 1))
                    dve.wait_ge(mm_done, t + 1)
                    if not early(t):
                        dve.wait_ge(y_stored[p], 16 * i)
                        dve.wait_ge(y_turned, t - 1)
                    dve.scalar_tensor_tensor(out=y[:n, p, :], in0=x[:n, p, :], scalar=ALPHA, in1=ps_y[:n, p, :],
                                             op0=ALU.mult, op1=ALU.add).then_inc(sum_done, 1)
                    dve.wait_ge(sum_done, t + 1)
                    for c in range(2):
                        last = dve.bn_stats(stats[:n, c, :], y[:n, p, c * 512:(c + 1) * 512])
                    last.then_inc(bn_done, 1)
                    dve.wait_ge(bn_done, t + 1)
                    alone(dve)
                    dve.bn_aggr(mv[:n, :], stats[:n].rearrange("p a b -> p (a b)")).then_inc(aggr_done, 1)
                    dve.wait_ge(aggr_done, t + 1)
                    dve.tensor_scalar(sd[:n, 0:1], mv[:n, 1:2], EPS, None, ALU.add).then_inc(var_done, 1)
                    dve.wait_ge(sd_done, t + 1)
                    dve.reciprocal(rs[:n, :], sd[:n, 1:2]).then_inc(rs_done, 1)
                    dve.wait_ge(rs_done, t + 1)
                    dve.tensor_scalar(y[:n, p, :], y[:n, p, :], mv[:n, 0:1], rs[:n, :], ALU.subtract,
                                      ALU.mult).then_inc(xhat_done, 1)
                    if not (isinstance(t, int) and t == 0):
                        lo_y(t - 1, 1 - p)
                tiles(dve, step)
                lo_y(NT, 0)

            @block.tensor
            def _(pe):
                pe.wait_ge(ident_done, 1)

                def turn_m(t, p):
                    n = n_rows(t)
                    pe.wait_ge(mx_done, t + 1)
                    wait_if(pe, m_lo_done, t)
                    for k in range(KD):
                        last = pe.transpose(ps_m[:, k, :n], mx[:n, p, k * P:(k + 1) * P], ident[:n, :n])
                    last.then_inc(m_turned, 1)

                def turn_y(t, p):
                    n = n_rows(t)
                    pe.wait_ge(y_done, t + 1)
                    wait_if(pe, y_lo_done, t)
                    for k in range(KD):
                        last = pe.transpose(ps_t[:, k, :n], y[:n, p, k * P:(k + 1) * P], ident[:n, :n])
                    last.then_inc(y_turned, 1)

                turn_m(0, 0)

                def step(t, p, i):
                    n = n_rows(t)
                    if exists(t, 1):
                        turn_m(t + 1, 1 - p)
                    pe.wait_ge(m_lo_done, t + 1)
                    if not early(t):
                        pe.wait_ge(sum_done, t - 1)
                    for c in range(0, D, 512):
                        for k in range(KD):
                            if isinstance(t, int) and t == 0 and c == 0:
                                pe.wait_ge(w_lo_done, k + 1)
                            last = products(pe, ps_y[:n, p, c:c + 512], mt_hi[:, p, k, :n], mt_lo[:, p, k, :n],
                                            w_hi[:, k, c:c + 512], w_lo[:, k, c:c + 512], k == 0, k == KD - 1)
                    last.then_inc(mm_done, 1)
                    if not (isinstance(t, int) and t == 0):
                        turn_y(t - 1, 1 - p)
                tiles(pe, step)
                turn_y(NT, 0)


def ffn_up(nc, d):
    with nc.cleanup_on_exit(), ExitStack() as ctx:
        m = Stage(nc, ctx, "fu")
        H = 2
        GW = 424
        NG = -(-ROWS // GW)
        REST = SEQ - (NG - 1) * GW
        LASTW = REST + NSMP
        U = 2 * NG
        MT = 2 * KF
        xt_hi, xt_lo = m.sb("xt_hi", [P, KD, H + ROWS], F32R), m.sb("xt_lo", [P, KD, H + ROWS], F32R)
        w_raw = m.sb("w_raw", [P, 2, KD, P])
        w_hi, w_lo = m.sb("w_hi", [P, 2, KD, P], F32R), m.sb("w_lo", [P, 2, KD, P], F32R)
        vec_rows, vecs = m.sb("vec_rows", [2 * MT, 3, P]), m.sb("vecs", [P, 6, MT])
        smp = m.sb("smp", [P, 2, H + NSMP])
        conv = m.sb("conv", [P, 2, GW])
        gate, h = m.sb("gate", [P, NG, GW]), m.sb("h", [P, 2, GW])
        states, states_t = m.sb("states", [P, 4, MT]), m.sb("states_t", [2 * MT, 2, P])
        ident = m.sb("ident", [P, P])
        ps_y = m.ps("ps_y", [P, 8, 512])

        zero_done, ident_done = m.sem("zero_done"), m.sem("ident_done")
        vec_loaded, vec_turned, vec_done, edge_done = m.sem("vec_loaded"), m.sem("vec_turned"), m.sem("vec_done"), m.sem("edge_done")
        xt_loaded = [m.sem(f"xt_loaded{g}") for g in range(NG)]
        w_loaded = [m.sem("w_loaded0"), m.sem("w_loaded1")]
        w_hi_done, w_lo_done = m.sem("w_hi_done"), m.sem("w_lo_done")
        mm_done, smp_done, tap0_done, smp_in_done, tap1_done, conv_done, gate_done, h_done = (
            m.sem("mm_done"), m.sem("smp_done"), m.sem("tap0_done"), m.sem("smp_in_done"), m.sem("tap1_done"), m.sem("conv_done"),
            m.sem("gate_done"), m.sem("h_done"))
        h_stored = [m.sem("h_stored0"), m.sem("h_stored1")]
        states_turned, states_done, states_stored = m.sem("states_turned"), m.sem("states_done"), m.sem("states_stored")

        def pairs(eng, step):
            step(0)
            with eng.Fori(1, KF) as j:
                step(j)

        def one(a, m_):
            return a[:, m_:m_ + 1] if isinstance(m_, int) else a[:, bass.ds(m_, 1)]

        def gwidth(g):
            return LASTW if g == NG - 1 else GW

        def stored_before(j, g):
            return ((NG + 1) // 2 if g % 2 == 0 else NG // 2) * j + g // 2

        with nc.Block() as block:
            @block.sync
            def _(sp):
                def load_w(j, half):
                    c = (j * P if isinstance(j, int) else j * P) + half * DFF
                    cols = slice(c, c + P) if isinstance(c, int) else bass.ds(c, P)
                    sp.dma_start(w_raw[:, half], d["ffn_w_in"][:, cols].rearrange("(k p) c -> p k c", p=P)).then_inc(w_loaded[half], 16)

                def load_xt(g):
                    c = slice(g * GW, g * GW + gwidth(g))
                    to = slice(H + g * GW, H + g * GW + gwidth(g))
                    sp.dma_start(xt_hi[:, :, to].bitcast(F32), d["x1t_hi"][:, :, c]).then_inc(xt_loaded[g], 16)
                    sp.dma_start(xt_lo[:, :, to].bitcast(F32), d["x1t_lo"][:, :, c]).then_inc(xt_loaded[g], 16)

                load_w(0, 0)
                load_xt(0)
                taps = d["ffn_conv_w"].rearrange("c (m p) -> (c m) p", p=P)
                sp.dma_start(vec_rows[:, 0, :], taps[0:2 * MT, :]).then_inc(vec_loaded, 16)
                sp.dma_start(vec_rows[0:MT, 1, :], taps[2 * MT:3 * MT, :]).then_inc(vec_loaded, 16)
                sp.dma_start(vec_rows[MT:2 * MT, 1, :], d["ffn_conv_b"].rearrange("(m p) -> m p", p=P)).then_inc(vec_loaded, 16)
                sp.dma_start(vec_rows[:, 2, :], d["state_ffn_conv"].rearrange("c (m p) -> (c m) p", p=P)).then_inc(vec_loaded, 16)
                load_w(0, 1)
                for g in range(1, NG):
                    load_xt(g)

                def step(j):
                    if isinstance(j, int):
                        for half in range(2):
                            sp.wait_ge(w_hi_done, half + 1)
                            sp.wait_ge(w_lo_done, half + 1)
                            load_w(j + 1, half)
                step(0)
                with sp.Fori(1, KF - 1) as j:
                    for half in range(2):
                        sp.wait_ge(w_hi_done, 2 * j + half + 1)
                        sp.wait_ge(w_lo_done, 2 * j + half + 1)
                        alone(sp)
                        load_w(j + 1, half)
                sp.wait_ge(states_done, 2)
                sp.dma_start(d["prompt_ffn_conv"].rearrange("c (m p) -> (c m) p", p=P), states_t[:, 0, :]).then_inc(states_stored, 16)
                sp.dma_start(d["sample_ffn_conv"].rearrange("c (m p) -> (c m) p", p=P), states_t[:, 1, :]).then_inc(states_stored, 16)
                sp.wait_ge(states_stored, 32)

            @block.gpsimd
            def _(pool):
                pool.memset(xt_hi[:, :, 0:H].bitcast(F32), 0.0)
                pool.memset(xt_lo[:, :, 0:H].bitcast(F32), 0.0).then_inc(edge_done, 1)
                make_identity(pool, ident, zero_done, ident_done)

                def step(j):
                    for g in range(NG):
                        n = gwidth(g)
                        pool.wait_ge(conv_done, U * j + NG + g + 1)
                        pool.wait_ge(gate_done, NG * j + g + 1)
                        if not (isinstance(j, int) and g < 2):
                            pool.wait_ge(h_stored[g % 2], 16 * stored_before(j, g))
                        v = NG + g
                        pool.tensor_tensor(h[:, g % 2, :n], conv[:, v % 2, :n], gate[:, g, :n], ALU.mult).then_inc(h_done, 1)
                        pool.wait_ge(h_done, NG * j + g + 1)
                        alone(pool)
                        k = slice(j, j + 1) if isinstance(j, int) else bass.ds(j, 1)
                        pool.dma_start(d["h_t"][:, k, g * GW:g * GW + n].rearrange("p a c -> p (a c)"),
                                       h[:, g % 2, :n]).then_inc(h_stored[g % 2], 16)
                pairs(pool, step)
                pool.wait_ge(h_stored[0], 16 * stored_before(KF, 0))
                pool.wait_ge(h_stored[1], 16 * stored_before(KF, 1))

            @block.scalar
            def _(act):
                def split_hi(j, half):
                    act.wait_ge(w_loaded[half], 16 * (j + 1))
                    wait_if(act, mm_done, U * (j - 1) + NG * (half + 1))
                    act.copy(w_hi[:, half], w_raw[:, half]).then_inc(w_hi_done, 1)

                split_hi(0, 0)
                act.wait_ge(vec_turned, 1)
                act.copy(vecs[:].rearrange("p a b -> p (a b)"), ps_y[:, 0, 0:6 * MT]).then_inc(vec_done, 1)
                act.wait_ge(vec_done, 1)
                split_hi(0, 1)

                def step(j):
                    for v in range(U):
                        half, g = v // NG, v % NG
                        u = U * j + v
                        mt = j + half * KF
                        n = REST if g == NG - 1 else GW
                        act.wait_ge(mm_done, u + 1)
                        if v >= NG:
                            if v - NG >= 2:
                                act.wait_ge(h_done, NG * j + v - NG - 1)
                        elif v < 2:
                            wait_if(act, h_done, NG * j - 1 + v)
                        if 2 <= v < NG + 2:
                            act.wait_ge(gate_done, NG * j + v - 1)
                        if g == NG - 1:
                            act.copy(smp[:, half, H:], ps_y[:, v % 8, H + REST:H + LASTW])
                            last2 = ps_y[:, v % 8, REST:REST + 2 * NSMP].rearrange("p (a b) -> p a b", b=NSMP)[:, :, 0:2]
                            act.copy(one_state(mt), last2).then_inc(smp_done, 1)
                        alone(act)
                        act.activation(conv[:, v % 2, :n], ps_y[:, v % 8, 0:n], ACT.Identity,
                                       bias=one(vecs[:, 3, :], mt), scale=one(vecs[:, 0, :], mt)).then_inc(tap0_done, 1)
                        if half == 0:
                            act.wait_ge(conv_done, u + 1)
                            wait_if(act, h_done, NG * (j - 1) + g + 1)
                            act.activation(gate[:, g, :gwidth(g)], conv[:, v % 2, :gwidth(g)], ACT.Silu).then_inc(gate_done, 1)
                        if v in (NG, U - 1):
                            nxt(j, 0 if v == NG else 1)

                def one_state(mt):
                    a = states[:, :, mt:mt + 1] if isinstance(mt, int) else states[:, :, bass.ds(mt, 1)]
                    return a.rearrange("p (x y) b -> p x (y b)", x=2)

                def nxt(j, half):
                    if peel[0]:
                        return
                    split_hi(j + 1, half)

                peel = [False]
                step(0)
                with act.Fori(1, KF - 1) as j:
                    step(j)
                peel[0] = True
                step(KF - 1)
                act.wait_ge(states_turned, 1)
                act.copy(states_t[:, 0, :], ps_y[0:2 * MT, 0, 0:P]).then_inc(states_done, 1)
                act.copy(states_t[:, 1, :], ps_y[0:2 * MT, 0, P:2 * P]).then_inc(states_done, 1)

            @block.vector
            def _(dve):
                def split_lo(j, half):
                    dve.wait_ge(w_hi_done, 2 * j + half + 1)
                    dve.tensor_tensor(w_lo[:, half], w_raw[:, half], w_hi[:, half].bitcast(F32), ALU.subtract).then_inc(w_lo_done, 1)

                split_lo(0, 0)
                split_lo(0, 1)
                dve.wait_ge(vec_done, 1)

                def step(j, more):
                    for v in range(U):
                        half, g = v // NG, v % NG
                        u = U * j + v
                        mt = j + half * KF
                        n = REST if g == NG - 1 else GW
                        c, y = conv[:, v % 2], ps_y[:, v % 8]
                        w0, w1, w2, b = (one(vecs[:, e, :], mt) for e in (0, 1, 2, 3))
                        dve.wait_ge(tap0_done, u + 1)
                        if g == NG - 1:
                            dve.wait_ge(smp_done, 2 * j + half + 1)
                            s = smp[:, half]
                            m_ = slice(mt, mt + 1) if isinstance(mt, int) else bass.ds(mt, 1)
                            dve.tensor_copy(s[:, 0:H], vecs[:, 4:6, m_].rearrange("p a b -> p (a b)")).then_inc(smp_in_done, 1)
                            dve.wait_ge(smp_in_done, 4 * (2 * j + half) + 1)
                            cs = c[:, REST:LASTW]
                            dve.tensor_scalar(cs, s[:, 0:NSMP], w0, b, ALU.mult, ALU.add).then_inc(smp_in_done, 1)
                            dve.wait_ge(smp_in_done, 4 * (2 * j + half) + 2)
                            dve.scalar_tensor_tensor(out=cs, in0=s[:, 1:1 + NSMP], scalar=w1, in1=cs, op0=ALU.mult,
                                                     op1=ALU.add).then_inc(smp_in_done, 1)
                            dve.wait_ge(smp_in_done, 4 * (2 * j + half) + 3)
                            dve.scalar_tensor_tensor(out=cs, in0=s[:, 2:2 + NSMP], scalar=w2, in1=cs, op0=ALU.mult,
                                                     op1=ALU.add).then_inc(smp_in_done, 1)
                        dve.scalar_tensor_tensor(out=c[:, :n], in0=y[:, 1:1 + n], scalar=w1, in1=c[:, :n], op0=ALU.mult,
                                                 op1=ALU.add).then_inc(tap1_done, 1)
                        dve.wait_ge(tap1_done, u + 1)
                        dve.scalar_tensor_tensor(out=c[:, :n], in0=y[:, 2:2 + n], scalar=w2, in1=c[:, :n], op0=ALU.mult,
                                                 op1=ALU.add).then_inc(conv_done, 1)
                        if more and v in (NG, U - 1):
                            split_lo(j + 1, 0 if v == NG else 1)
                step(0, True)
                with dve.Fori(1, KF - 1) as j:
                    step(j, True)
                step(KF - 1, False)

            @block.tensor
            def _(pe):
                pe.wait_ge(ident_done, 1)
                pe.wait_ge(vec_loaded, 64)
                for e in range(3):
                    last = pe.transpose(ps_y[:, 0, 2 * MT * e:2 * MT * (e + 1)], vec_rows[:, e, :], ident[0:2 * MT, 0:2 * MT])
                last.then_inc(vec_turned, 1)
                pe.wait_ge(vec_done, 1)
                pe.wait_ge(edge_done, 1)

                def step(j):
                    for v in range(U):
                        half, g = v // NG, v % NG
                        if isinstance(j, int) and j == 0 and half == 0:
                            pe.wait_ge(xt_loaded[g], 32)
                        if g == 0:
                            pe.wait_ge(w_lo_done, 2 * j + half + 1)
                        wait_if(pe, conv_done, U * j + v - 1)
                        n = H + gwidth(g)
                        for k in range(KD):
                            last = products(pe, ps_y[:, v % 8, :n], w_hi[:, half, k, :], w_lo[:, half, k, :],
                                            xt_hi[:, k, g * GW:g * GW + n], xt_lo[:, k, g * GW:g * GW + n],
                                            k == 0, k == KD - 1)
                        last.then_inc(mm_done, 1)
                pairs(pe, step)
                pe.wait_ge(conv_done, U * KF)
                for e in range(2):
                    last = pe.transpose(ps_y[0:2 * MT, 0, e * P:(e + 1) * P],
                                        states[:, 2 * e:2 * e + 2, :].rearrange("p a b -> p (a b)"), ident[:])
                last.then_inc(states_turned, 1)


def ffn_down(nc, d):
    with nc.cleanup_on_exit(), ExitStack() as ctx:
        m = Stage(nc, ctx, "fd")
        PK = 2
        NPC = KF // PK
        RING = 4
        w_hi, w_lo = m.sb("w_hi", [P, KF, D], F32R), m.sb("w_lo", [P, KF, D], F32R)
        h_raw = m.sb("h_raw", [P, RING, PK, P])
        h_hi, h_lo = m.sb("h_hi", [P, RING, PK, P], F32R), m.sb("h_lo", [P, RING, PK, P], F32R)
        y = m.sb("y", [P, 2, D])
        g_ln, b_ln = m.sb("g_ln", [P, D]), m.sb("b_ln", [P, D])
        stats, mv, sd, rs = m.sb("stats", [P, 2, 6]), m.sb("mv", [P, 2]), m.sb("sd", [P, 2]), m.sb("rs", [P, 1])
        ps_y = m.ps("ps_y", [P, 2, D])

        w_loaded = [m.sem("w_loaded0"), m.sem("w_loaded1")]
        w_hi_done, w_lo_done, vec_loaded = m.sem("w_hi_done"), m.sem("w_lo_done"), m.sem("vec_loaded")
        h_loaded = [m.sem(f"h_loaded{s}") for s in range(RING)]
        x_loaded = [m.sem("x_loaded0"), m.sem("x_loaded1")]
        h_hi_done, h_lo_done, piece_done = m.sem("h_hi_done"), m.sem("h_lo_done"), m.sem("piece_done")
        sum_done, bn_done, aggr_done, var_done, sd_done = (m.sem("sum_done"), m.sem("bn_done"), m.sem("aggr_done"), m.sem("var_done"),
                                                           m.sem("sd_done"))
        rs_done, xhat_done, gain_done, y_done = m.sem("rs_done"), m.sem("xhat_done"), m.sem("gain_done"), m.sem("y_done")
        y_stored = [m.sem("y_stored0"), m.sem("y_stored1")]

        def tiles(eng, step):
            step(0, 0, 0)
            step(1, 1, 0)
            with eng.Fori(1, NT // 2) as i:
                step(2 * i, 0, i)
                step(2 * i + 1, 1, i)
            step(NT, 0, NT // 2)

        def slot_loads(t, c):
            a_tile = len(range(c % RING, NPC, RING))
            return a_tile * t + c // RING + 1

        with nc.Block() as block:
            @block.sync
            def _(sp):
                for k in range(KF):
                    if k >= 2:
                        sp.wait_ge(w_hi_done, k - 1)
                        sp.wait_ge(w_lo_done, k - 1)
                    sp.dma_start(y[:, k % 2, :], d["ffn_w_out"][k * P:(k + 1) * P, :]).then_inc(w_loaded[k % 2], 16)
                sp.wait_ge(w_lo_done, KF)

                def step(t, p, i):
                    n = n_rows(t)
                    if not (isinstance(t, int) and t < 2):
                        sp.wait_ge(y_stored[p], 16 * i)
                    alone(sp)
                    sp.dma_start(y[:n, p, :], d["x1_rows"][tile_rows(t), :]).then_inc(x_loaded[p], 16)
                tiles(sp, step)

            @block.gpsimd
            def _(pool):
                pool.dma_start(g_ln[:], bc_row(d["ln2_g"], D)).then_inc(vec_loaded, 16)
                pool.dma_start(b_ln[:], bc_row(d["ln2_b"], D)).then_inc(vec_loaded, 16)

                def load_piece(t, c):
                    n = n_rows(t)
                    wait_if(pool, h_lo_done, NPC * t + c - 2)
                    alone(pool) if not isinstance(t, int) else None
                    pool.dma_start(h_raw[:, c % RING, :, :n], d["h_t"][:, PK * c:PK * (c + 1), tile_rows(t)]).then_inc(h_loaded[c % RING], 16)

                def finish(t, p):
                    n = n_rows(t)
                    pool.wait_ge(xhat_done, t + 1)
                    pool.tensor_tensor(y[:n, p, :], y[:n, p, :], g_ln[:n, :], ALU.mult).then_inc(gain_done, 1)
                    pool.wait_ge(gain_done, t + 1)
                    pool.tensor_tensor(y[:n, p, :], y[:n, p, :], b_ln[:n, :], ALU.add).then_inc(y_done, 1)
                    pool.wait_ge(y_done, t + 1)
                    alone(pool)
                    if isinstance(t, int) and t == NT:
                        pool.dma_start(d["y_sample"], y[:n, p, :]).then_inc(y_stored[p], 16)
                    else:
                        pool.dma_start(d["y_prompt"][tile_rows(t), :], y[:n, p, :]).then_inc(y_stored[p], 16)

                def step(t, p, i):
                    for c in range(NPC):
                        load_piece(t, c)
                        if c == NPC - 3 and not (isinstance(t, int) and t == 0):
                            finish(t - 1, 1 - p)
                    if isinstance(t, int) and t == 0:
                        pool.wait_ge(vec_loaded, 32)
                tiles(pool, step)
                finish(NT, 0)
                pool.wait_ge(y_stored[0], 16 * 9)
                pool.wait_ge(y_stored[1], 16 * 8)

            @block.scalar
            def _(act):
                def hi(t, c):
                    n = n_rows(t)
                    act.wait_ge(h_loaded[c % RING], 16 * slot_loads(t, c))
                    wait_if(act, piece_done, NPC * t + c - 2)
                    act.copy(h_hi[:, c % RING, :, :n], h_raw[:, c % RING, :, :n]).then_inc(h_hi_done, 1)

                def split_w(k):
                    act.wait_ge(w_loaded[k % 2], 16 * (k // 2 + 1))
                    act.copy(w_hi[:, k, :], y[:, k % 2, :]).then_inc(w_hi_done, 1)

                def step(t, p, i):
                    n = n_rows(t)
                    for c in range(NPC):
                        if isinstance(t, int) and t == 0:
                            split_w(2 * c)
                            split_w(2 * c + 1)
                        hi(t, c)
                        if c == 4 and not (isinstance(t, int) and t == 0):
                            root(t - 1)

                def root(t):
                    n = n_rows(t)
                    act.wait_ge(var_done, t + 1)
                    act.activation(sd[:n, 1:2], sd[:n, 0:1], ACT.Sqrt).then_inc(sd_done, 1)
                tiles(act, step)
                root(NT)

            @block.vector
            def _(dve):
                def lo(t, c):
                    n = n_rows(t)
                    dve.wait_ge(h_hi_done, NPC * t + c + 1)
                    dve.tensor_tensor(h_lo[:, c % RING, :, :n], h_raw[:, c % RING, :, :n], h_hi[:, c % RING, :, :n].bitcast(F32),
                                      ALU.subtract).then_inc(h_lo_done, 1)

                def norm(t, p, i):
                    n = n_rows(t)
                    dve.wait_ge(x_loaded[p], 16 * (i + 1))
                    dve.wait_ge(piece_done, NPC * (t + 1))
                    dve.scalar_tensor_tensor(out=y[:n, p, :], in0=y[:n, p, :], scalar=ALPHA, in1=ps_y[:n, p, :],
                                             op0=ALU.mult, op1=ALU.add).then_inc(sum_done, 1)
                    dve.wait_ge(sum_done, t + 1)
                    for c in range(2):
                        last = dve.bn_stats(stats[:n, c, :], y[:n, p, c * 512:(c + 1) * 512])
                    last.then_inc(bn_done, 1)
                    dve.wait_ge(bn_done, t + 1)
                    alone(dve)
                    dve.bn_aggr(mv[:n, :], stats[:n].rearrange("p a b -> p (a b)")).then_inc(aggr_done, 1)
                    dve.wait_ge(aggr_done, t + 1)
                    dve.tensor_scalar(sd[:n, 0:1], mv[:n, 1:2], EPS, None, ALU.add).then_inc(var_done, 1)

                def finish(t, p):
                    n = n_rows(t)
                    dve.wait_ge(sd_done, t + 1)
                    dve.reciprocal(rs[:n, :], sd[:n, 1:2]).then_inc(rs_done, 1)
                    dve.wait_ge(rs_done, t + 1)
                    dve.tensor_scalar(y[:n, p, :], y[:n, p, :], mv[:n, 0:1], rs[:n, :], ALU.subtract,
                                      ALU.mult).then_inc(xhat_done, 1)

                def step(t, p, i):
                    for c in range(NPC):
                        if isinstance(t, int) and t == 0:
                            for k in (2 * c, 2 * c + 1):
                                dve.wait_ge(w_hi_done, k + 1)
                                dve.tensor_tensor(w_lo[:, k, :], y[:, k % 2, :], w_hi[:, k, :].bitcast(F32),
                                                  ALU.subtract).then_inc(w_lo_done, 1)
                        lo(t, c)
                        if not (isinstance(t, int) and t == 0):
                            if c == 2:
                                norm(t - 1, 1 - p, i - 1 + p)
                            if c == 5:
                                finish(t - 1, 1 - p)
                tiles(dve, step)
                norm(NT, 0, NT // 2)
                finish(NT, 0)

            @block.tensor
            def _(pe):
                def step(t, p, i):
                    n = n_rows(t)
                    if not (isinstance(t, int) and t < 2):
                        pe.wait_ge(sum_done, t - 1)
                    for c in range(NPC):
                        if isinstance(t, int) and t == 0:
                            pe.wait_ge(w_lo_done, PK * (c + 1))
                        pe.wait_ge(h_lo_done, NPC * t + c + 1)
                        for e in range(PK):
                            k = PK * c + e
                            for col in range(0, D, 512):
                                last = products(pe, ps_y[:n, p, col:col + 512], h_hi[:, c % RING, e, :n], h_lo[:, c % RING, e, :n],
                                                w_hi[:, k, col:col + 512], w_lo[:, k, col:col + 512], k == 0, k == KF - 1)
                        last.then_inc(piece_done, 1)
                tiles(pe, step)


INPUTS = [
    ("x_prompt", (SEQ, D)), ("x_sample", (NSMP, D)), ("cache_k", (CACHE, AW)), ("cache_v", (CACHE, AW)),
    ("state_ssm", (AW, STATE)), ("state_ssm_conv", (3, XBC)), ("state_ffn_conv", (2, 2 * DFF)),
    ("ln_in_g", (D,)), ("ln_in_b", (D,)), ("w_in", (D, N_IN)), ("rel_bias", (HEADS, REL)),
    ("ssm_conv_w", (4, XBC)), ("ssm_conv_b", (XBC,)), ("ssm_dt_bias", (HEADS,)), ("ssm_a_log", (HEADS,)), ("ssm_d", (HEADS,)),
    ("gmlp_w", (CG, P, P)), ("gmlp_b", (CG, P)), ("mix_norm_g", (D,)), ("w_out", (D, D)), ("ln1_g", (D,)), ("ln1_b", (D,)),
    ("ffn_w_in", (D, 2 * DFF)), ("ffn_conv_w", (3, 2 * DFF)), ("ffn_conv_b", (2 * DFF,)), ("ffn_w_out", (DFF, D)),
    ("ln2_g", (D,)), ("ln2_b", (D,)),
]
ARGUMENT = {"cache_k": "cache_attn_k", "cache_v": "cache_attn_v", "rel_bias": "attn_rel_bias"}
OUTPUTS = [
    ("y_prompt", (SEQ, D), (1, SEQ, D)), ("y_sample", (NSMP, D), (1, NSMP, D)),
    ("prompt_k", (CACHE, AW), (1, 1, CACHE, HEADS, HD)), ("prompt_v", (CACHE, AW), (1, 1, CACHE, HEADS, HD)),
    ("prompt_ssm", (AW, STATE), (1, 1, HEADS, HD, STATE)), ("prompt_ssm_conv", (3, XBC), (1, 1, 3, XBC)),
    ("prompt_ffn_conv", (2, 2 * DFF), (1, 1, 2, 2 * DFF)),
    ("sample_k", (NSMP, AW), (1, 1, NSMP, HEADS, HD)), ("sample_v", (NSMP, AW), (1, 1, NSMP, HEADS, HD)),
    ("sample_ssm", (AW, STATE), (1, 1, HEADS, HD, STATE)), ("sample_ssm_conv", (3, XBC), (1, 1, 3, XBC)),
    ("sample_gmlp_v", (NSMP, CW), (1, 1, NSMP, CW)), ("sample_ffn_conv", (2, 2 * DFF), (1, 1, 2, 2 * DFF)),
]
SCRATCH = [
    ("x_rows", (ROWS, D), F32), ("xt_hi", (P, KD, ROWS), F32), ("xt_lo", (P, KD, ROWS), F32),
    ("v_rows", (ROWS, AW), F32), ("z_rows", (ROWS, AW), F32), ("dt_rows", (ROWS, HEADS), F32), ("uv_rows", (ROWS, 2 * CW), F32),
    ("qk_t", (2 * AW, ROWS), F32), ("xbc_t", (P, NXBC, ROWS), F32), ("rel_ext", (HEADS, WIN + P), F32),
    ("mixed", (ROWS, D), F32), ("x1_rows", (ROWS, D), F32), ("x1t_hi", (P, KD, ROWS), F32), ("x1t_lo", (P, KD, ROWS), F32),
    ("h_t", (P, KF, ROWS), F32),
]


def build(nc):
    d = {name: nc.dram_tensor(name, shape, F32, kind="ExternalInput").ap() for name, shape in INPUTS}
    d.update({name: nc.dram_tensor(name, shape, F32, kind="ExternalOutput").ap() for name, shape, _ in OUTPUTS})
    d.update({name: nc.dram_tensor(name, shape, dt, kind="Internal").ap() for name, shape, dt in SCRATCH})
    for stage in STAGES:
        stage(nc, d)


STAGES = (project_rows, project_features, attention, ssd_and_gmlp, mix_out, ffn_up, ffn_down)


def kernel(**inputs):
    import numpy as np
    import concourse.bacc as bacc
    from concourse.bass_utils import run_bass_kernel_spmd

    nc = bacc.Bacc("TRN2", target_bir_lowering=False, num_devices=1)
    build(nc)
    arrays = {name: np.ascontiguousarray(inputs[ARGUMENT.get(name, name)]).reshape(shape) for name, shape in INPUTS}
    r = run_bass_kernel_spmd(nc, [arrays], core_ids=[0])
    return tuple(r.results[0][name].reshape(shape) for name, _, shape in OUTPUTS)
```

```python
from contextlib import ExitStack

import concourse.bass as bass
from concourse import mybir

F32 = mybir.dt.float32
F32R = mybir.dt.float32r
ALU = mybir.AluOpType
ACT = mybir.ActivationFunctionType
AX_X = mybir.AxisListType.X

P = 128
D = 1024
KD = D // P
SEQ = 2048
NSMP = 64
ROWS = SEQ + NSMP
NT = SEQ // P
CACHE = 512
HEADS = 6
HD = 64
AW = HEADS * HD
STATE = 128
XBC = AW + 4 * STATE
NXBC = XBC // P
CW = 256
CG = 4
DFF = 2816
KF = DFF // P
ALPHA = 2.0 ** 0.25
EPS = 1e-5
MASKED = -1e30
REL = 192
WIN = CACHE + P
V0, Z0, X0, DT0, U0 = 2 * AW, 3 * AW, 4 * AW, 4 * AW + XBC, 4 * AW + XBC + HEADS
G0 = U0 + CW
N_IN = G0 + CW


def wait_if(eng, sem, value):
    if not isinstance(value, int) or value > 0:
        eng.wait_ge(sem, value)


def alone(eng):
    eng.nop(nofuse=True)


def tile_rows(t):
    if isinstance(t, int):
        return slice(t * P, t * P + (NSMP if t == NT else P))
    return bass.ds(t * P, P)


def n_rows(t):
    return NSMP if isinstance(t, int) and t == NT else P


class Stage:

    def __init__(self, nc, ctx, stage):
        self.nc, self.ctx, self.stage = nc, ctx, stage

    def sb(self, name, shape, dt=F32):
        return self.ctx.enter_context(self.nc.sbuf_tensor(f"{self.stage}_{name}", shape, dt))

    def ps(self, name, shape):
        return self.ctx.enter_context(self.nc.psum_tensor(f"{self.stage}_{name}", shape, F32))

    def sem(self, name):
        return self.nc.alloc_semaphore(f"{self.stage}_{name}")


def bc_row(ap1d, n):
    return ap1d.rearrange("(a n) -> a n", a=1).to_broadcast([P, n])


def products(pe, out, lhs_hi, lhs_lo, rhs_hi, rhs_lo, first, last):
    pe.matmul(out, lhs_hi, rhs_hi, start=first, stop=False)
    pe.matmul(out, lhs_hi, rhs_lo, start=False, stop=False)
    return pe.matmul(out, lhs_lo, rhs_hi, start=False, stop=last)


def make_identity(pool, ident, zero_done, ident_done):
    pool.memset(ident[:], 0.0).then_inc(zero_done, 1)
    pool.wait_ge(zero_done, 1)
    pool.affine_select(out=ident[:], in_=ident[:], compare_op=ALU.not_equal, fill=1.0, base=0,
                       pattern=[[-1, P]], channel_multiplier=1).then_inc(ident_done, 1)


def project_rows(nc, d):
    with nc.cleanup_on_exit(), ExitStack() as ctx:
        m = Stage(nc, ctx, "pr")
        cols = [(V0, 512), (V0 + 512, 256), (G0, CW), (DT0, HEADS + CW)]
        at = [0, 512, 768, 1024]
        NW = 1024 + HEADS + CW
        w_raw = m.sb("w_raw", [P, 2, NW])
        w_hi, w_lo = m.sb("w_hi", [P, KD, NW], F32R), m.sb("w_lo", [P, KD, NW], F32R)
        x = m.sb("x", [P, 2, D])
        xr = m.sb("xr", [P, 2, D])
        xt_hi, xt_lo = m.sb("xt_hi", [P, 2, KD, P], F32R), m.sb("xt_lo", [P, 2, KD, P], F32R)
        g_bc, b_bc = m.sb("g_bc", [P, D]), m.sb("b_bc", [P, D])
        stats, mv, sd, rs = m.sb("stats", [P, 2, 6]), m.sb("mv", [P, 2]), m.sb("sd", [P, 2]), m.sb("rs", [P, 1])
        ident = m.sb("ident", [P, P])
        v_out, z_out = m.sb("v_out", [P, 2, AW]), m.sb("z_out", [P, 2, AW])
        uv_out, dt_out = m.sb("uv_out", [P, 2, 2 * CW]), m.sb("dt_out", [P, 2, 8])
        ps_y, ps_t = m.ps("ps_y", [P, 2, 3, 512]), m.ps("ps_t", [P, KD, P])

        zero_done, ident_done = m.sem("zero_done"), m.sem("ident_done")
        w_loaded = [m.sem("w_loaded0"), m.sem("w_loaded1")]
        w_hi_done, w_lo_done = m.sem("w_hi_done"), m.sem("w_lo_done")
        gb_loaded = m.sem("gb_loaded")
        x_loaded = [m.sem("x_loaded0"), m.sem("x_loaded1")]
        bn_done, aggr_done, var_done, sd_done = m.sem("bn_done"), m.sem("aggr_done"), m.sem("var_done"), m.sem("sd_done")
        rs_done, xhat_done, xg_done, xr_done = m.sem("rs_done"), m.sem("xhat_done"), m.sem("xg_done"), m.sem("xr_done")
        t_done, hi_done, lo_done, y_done = m.sem("t_done"), m.sem("hi_done"), m.sem("lo_done"), m.sem("y_done")
        vdt_done, act_out_done = m.sem("vdt_done"), m.sem("act_out_done")
        xr_stored = [m.sem("xr_stored0"), m.sem("xr_stored1")]
        xt_stored = [m.sem("xt_stored0"), m.sem("xt_stored1")]
        y_stored = [m.sem("y_stored0"), m.sem("y_stored1")]

        def half(t):
            return t // 2

        def tiles(eng, step):
            step(0, 0, 0)
            step(1, 1, 0)
            with eng.Fori(1, 7) as i:
                step(2 * i, 0, i)
                step(2 * i + 1, 1, i)
            for t in (14, 15, 16):
                step(t, t % 2, t // 2)

        with nc.Block() as block:
            @block.sync
            def _(sp):
                for k in range(KD):
                    if k >= 2:
                        sp.wait_ge(w_hi_done, k - 1)
                        sp.wait_ge(w_lo_done, k - 1)
                    for (c, n), a in zip(cols, at):
                        sp.dma_start(w_raw[:, k % 2, a:a + n], d["w_in"][k * P:(k + 1) * P, c:c + n]).then_inc(w_loaded[k % 2], 16)
                def step(t, p, i):
                    n = n_rows(t)
                    sp.wait_ge(xr_done, t + 1)
                    alone(sp)
                    sp.dma_start(d["x_rows"][tile_rows(t), :], xr[:n, p, :]).then_inc(xr_stored[p], 16)
                    sp.wait_ge(hi_done, t + 1)
                    alone(sp)
                    sp.dma_start(d["xt_hi"][:, :, tile_rows(t)], xt_hi[:, p, :, :n].bitcast(F32)).then_inc(xt_stored[p], 16)
                    sp.wait_ge(lo_done, t + 1)
                    alone(sp)
                    sp.dma_start(d["xt_lo"][:, :, tile_rows(t)], xt_lo[:, p, :, :n].bitcast(F32)).then_inc(xt_stored[p], 16)
                    sp.wait_ge(vdt_done, t + 1)
                    alone(sp)
                    sp.dma_start(d["v_rows"][tile_rows(t), :], v_out[:n, p, :]).then_inc(y_stored[p], 16)
                    sp.dma_start(d["dt_rows"][tile_rows(t), :], dt_out[:n, p, :HEADS]).then_inc(y_stored[p], 16)
                    sp.wait_ge(act_out_done, t + 1)
                    alone(sp)
                    sp.dma_start(d["z_rows"][tile_rows(t), :], z_out[:n, p, :]).then_inc(y_stored[p], 16)
                    sp.dma_start(d["uv_rows"][tile_rows(t), :], uv_out[:n, p, :]).then_inc(y_stored[p], 16)
                tiles(sp, step)
                for p, count in ((0, 9), (1, 8)):
                    sp.wait_ge(xr_stored[p], 16 * count)
                    sp.wait_ge(xt_stored[p], 32 * count)
                    sp.wait_ge(y_stored[p], 64 * count)

            @block.gpsimd
            def _(pool):
                make_identity(pool, ident, zero_done, ident_done)

                def load_x(t, p):
                    if isinstance(t, int) and t == NT:
                        pool.dma_start(x[:NSMP, p, :], d["x_sample"]).then_inc(x_loaded[p], 16)
                    else:
                        pool.dma_start(x[:, p, :], d["x_prompt"][tile_rows(t), :]).then_inc(x_loaded[p], 16)

                load_x(0, 0)
                load_x(1, 1)
                pool.dma_start(g_bc[:], bc_row(d["ln_in_g"], D)).then_inc(gb_loaded, 16)
                pool.dma_start(b_bc[:], bc_row(d["ln_in_b"], D)).then_inc(gb_loaded, 16)
                pool.wait_ge(gb_loaded, 32)

                def step(t, p, i):
                    n = n_rows(t)
                    pool.wait_ge(xhat_done, t + 1)
                    if not (isinstance(t, int) and t < 2):
                        pool.wait_ge(xr_stored[p], 16 * i)
                        pool.wait_ge(t_done, t - 1)
                    pool.tensor_tensor(xr[:n, p, :], x[:n, p, :], g_bc[:n, :], ALU.mult).then_inc(xg_done, 1)
                    pool.wait_ge(xg_done, t + 1)
                    pool.tensor_tensor(xr[:n, p, :], xr[:n, p, :], b_bc[:n, :], ALU.add).then_inc(xr_done, 1)
                    if not isinstance(t, int) or t + 2 <= NT:
                        load_x(t + 2, p)
                tiles(pool, step)

            @block.scalar
            def _(act):
                for k in range(KD):
                    act.wait_ge(w_loaded[k % 2], 64 * (k // 2 + 1))
                    act.copy(w_hi[:, k, :], w_raw[:, k % 2, :]).then_inc(w_hi_done, 1)

                def root(t):
                    n = n_rows(t)
                    act.wait_ge(var_done, t + 1)
                    act.activation(sd[:n, 1:2], sd[:n, 0:1], ACT.Sqrt).then_inc(sd_done, 1)

                def hi(t, p, i):
                    n = n_rows(t)
                    act.wait_ge(t_done, t + 1)
                    if not (isinstance(t, int) and t < 2):
                        act.wait_ge(xt_stored[p], 32 * i)
                        act.wait_ge(y_done, t - 1)
                    act.copy(xt_hi[:, p, :, :n], ps_t[:, :, :n]).then_inc(hi_done, 1)

                root(0)
                hi(0, 0, 0)
                root(1)

                def step(t, p, i):
                    n = n_rows(t)
                    if not isinstance(t, int) or t + 1 <= NT:
                        hi(t + 1, 1 - p, i + p)
                    if not isinstance(t, int) or t + 2 <= NT:
                        root(t + 2)
                    act.wait_ge(y_done, t + 1)
                    if not (isinstance(t, int) and t < 2):
                        act.wait_ge(y_stored[p], 64 * i)
                    y = ps_y[:, p]
                    act.activation(z_out[:n, p, 0:128], y[:n, 0, AW:512], ACT.Silu)
                    act.activation(z_out[:n, p, 128:AW], y[:n, 1, 0:256], ACT.Silu)
                    act.activation(uv_out[:n, p, CW:], y[:n, 1, 256:512], ACT.Gelu_apprx_tanh)
                    act.activation(uv_out[:n, p, :CW], y[:n, 2, HEADS:HEADS + CW],
                                   ACT.Gelu_apprx_tanh).then_inc(act_out_done, 1)
                tiles(act, step)

            @block.vector
            def _(dve):
                for k in range(KD):
                    dve.wait_ge(w_hi_done, k + 1)
                    dve.tensor_tensor(w_lo[:, k, :], w_raw[:, k % 2, :], w_hi[:, k, :].bitcast(F32),
                                      ALU.subtract).then_inc(w_lo_done, 1)

                def norm(t, p, i):
                    n = n_rows(t)
                    dve.wait_ge(x_loaded[p], 16 * (i + 1))
                    for c in range(2):
                        last = dve.bn_stats(stats[:n, c, :], x[:n, p, c * 512:(c + 1) * 512])
                    last.then_inc(bn_done, 1)
                    dve.wait_ge(bn_done, t + 1)
                    alone(dve)
                    dve.bn_aggr(mv[:n, :], stats[:n].rearrange("p a b -> p (a b)")).then_inc(aggr_done, 1)
                    dve.wait_ge(aggr_done, t + 1)
                    dve.tensor_scalar(sd[:n, 0:1], mv[:n, 1:2], EPS, None, ALU.add).then_inc(var_done, 1)
                    dve.wait_ge(sd_done, t + 1)
                    dve.reciprocal(rs[:n, :], sd[:n, 1:2]).then_inc(rs_done, 1)
                    dve.wait_ge(rs_done, t + 1)
                    dve.tensor_scalar(x[:n, p, :], x[:n, p, :], mv[:n, 0:1], rs[:n, :], ALU.subtract,
                                      ALU.mult).then_inc(xhat_done, 1)

                def lo(t, p):
                    n = n_rows(t)
                    dve.wait_ge(hi_done, t + 1)
                    dve.tensor_tensor(xt_lo[:, p, :, :n], ps_t[:, :, :n], xt_hi[:, p, :, :n].bitcast(F32),
                                      ALU.subtract).then_inc(lo_done, 1)

                norm(0, 0, 0)
                lo(0, 0)
                norm(1, 1, 0)

                def step(t, p, i):
                    n = n_rows(t)
                    if not isinstance(t, int) or t + 1 <= NT:
                        lo(t + 1, 1 - p)
                    if not isinstance(t, int) or t + 2 <= NT:
                        norm(t + 2, p, i + 1)
                    dve.wait_ge(y_done, t + 1)
                    dve.wait_ge(act_out_done, t + 1)
                    if not (isinstance(t, int) and t < 2):
                        dve.wait_ge(y_stored[p], 64 * i)
                    dve.tensor_copy(v_out[:n, p, :], ps_y[:n, p, 0, 0:AW])
                    dve.tensor_copy(dt_out[:n, p, :HEADS], ps_y[:n, p, 2, 0:HEADS]).then_inc(vdt_done, 1)
                tiles(dve, step)

            @block.tensor
            def _(pe):
                pe.wait_ge(ident_done, 1)

                def turn(t, p):
                    n = n_rows(t)
                    pe.wait_ge(xr_done, t + 1)
                    wait_if(pe, lo_done, t)
                    for k in range(KD):
                        last = pe.transpose(ps_t[:, k, :n], xr[:n, p, k * P:(k + 1) * P], ident[:n, :n])
                    last.then_inc(t_done, 1)

                turn(0, 0)

                def step(t, p, i):
                    n = n_rows(t)
                    if not isinstance(t, int) or t + 1 <= NT:
                        turn(t + 1, 1 - p)
                    pe.wait_ge(lo_done, t + 1)
                    if not (isinstance(t, int) and t < 2):
                        pe.wait_ge(vdt_done, t - 1)
                    outs = [ps_y[:n, p, 0, :], ps_y[:n, p, 1, 0:256], ps_y[:n, p, 1, 256:512],
                            ps_y[:n, p, 2, 0:HEADS + CW]]
                    for out, a, (c, w) in zip(outs, at, cols):
                        for k in range(KD):
                            if isinstance(t, int) and t == 0 and a == 0:
                                pe.wait_ge(w_lo_done, k + 1)
                            last = products(pe, out, xt_hi[:, p, k, :n], xt_lo[:, p, k, :n],
                                            w_hi[:, k, a:a + w], w_lo[:, k, a:a + w], k == 0, k == KD - 1)
                    last.then_inc(y_done, 1)
                tiles(pe, step)


def project_features(nc, d):
    with nc.cleanup_on_exit(), ExitStack() as ctx:
        m = Stage(nc, ctx, "pf")
        GN = 512
        NG = SEQ // GN
        NM = (2 * AW + XBC) // P
        NQK = 2 * AW // P
        W = 2 * AW + XBC
        w_raw = m.sb("w_raw", [P, 2, W])
        w_hi, w_lo = m.sb("w_hi", [P, KD, W], F32R), m.sb("w_lo", [P, KD, W], F32R)
        xt_hi, xt_lo = m.sb("xt_hi", [P, 2, KD, GN], F32R), m.sb("xt_lo", [P, 2, KD, GN], F32R)
        qk_hi, qk_lo = m.sb("qk_hi", [P, 2, GN], F32R), m.sb("qk_lo", [P, 2, GN], F32R)
        cin = m.sb("cin", [P, 2, 3 + GN])
        conv, conv_out = m.sb("conv", [P, 2, GN]), m.sb("conv_out", [P, 2, GN])
        halo, halo_smp = m.sb("halo", [P, NXBC, 3]), m.sb("halo_smp", [P, NXBC, 3])
        taps, shift = m.sb("taps", [P, NXBC, 4]), m.sb("shift", [P, NXBC])
        ps_y = m.ps("ps_y", [P, 8, GN])

        w_loaded = [m.sem("w_loaded0"), m.sem("w_loaded1")]
        w_hi_done, w_lo_done = m.sem("w_hi_done"), m.sem("w_lo_done")
        small_loaded, halo_zeroed = m.sem("small_loaded"), m.sem("halo_zeroed")
        xt_loaded = [m.sem("xt_loaded0"), m.sem("xt_loaded1")]
        y_done, evac_done, qk_lo_done = m.sem("y_done"), m.sem("evac_done"), m.sem("qk_lo_done")
        halo_in_done, conv_done, tap_done, silu_done = m.sem("halo_in_done"), m.sem("conv_done"), m.sem("tap_done"), m.sem("silu_done")
        qk_stored = [m.sem("qk_stored0"), m.sem("qk_stored1")]
        xbc_stored = [m.sem("xbc_stored0"), m.sem("xbc_stored1")]
        state_stored = m.sem("state_stored")

        def width(g):
            return NSMP if isinstance(g, int) and g == NG else GN

        def gcols(g):
            if isinstance(g, int):
                return slice(g * GN, g * GN + width(g))
            return bass.ds(g * GN, GN)

        def groups(eng, step):
            step(0, 0, 0)
            step(1, 1, 0)
            with eng.Fori(1, NG // 2) as i:
                step(2 * i, 0, i)
                step(2 * i + 1, 1, i)
            step(NG, 0, NG // 2)

        def scale(j):
            return HD ** -0.5 if j < NQK // 2 else 1.0

        def xbc_count(g, j):
            return (NXBC + 1 - j % 2) // 2 * g + j // 2

        with nc.Block() as block:
            @block.sync
            def _(sp):
                for k in range(KD):
                    if k >= 2:
                        sp.wait_ge(w_hi_done, k - 1)
                        sp.wait_ge(w_lo_done, k - 1)
                    rows = slice(k * P, (k + 1) * P)
                    sp.dma_start(w_raw[:, k % 2, 0:2 * AW], d["w_in"][rows, 0:2 * AW]).then_inc(w_loaded[k % 2], 16)
                    sp.dma_start(w_raw[:, k % 2, 2 * AW:], d["w_in"][rows, X0:X0 + XBC]).then_inc(w_loaded[k % 2], 16)

                def step(g, p, i):
                    n = width(g)
                    for j in range(NQK):
                        sp.wait_ge(qk_lo_done, NQK * g + j + 1)
                        alone(sp)
                        rows = slice(j * P, (j + 1) * P)
                        sp.dma_start(d["qk_hi"][rows, gcols(g)], qk_hi[:, j % 2, :n].bitcast(F32)).then_inc(qk_stored[j % 2], 16)
                        sp.dma_start(d["qk_lo"][rows, gcols(g)], qk_lo[:, j % 2, :n].bitcast(F32)).then_inc(qk_stored[j % 2], 16)
                    for j in range(NXBC):
                        sp.wait_ge(silu_done, NXBC * g + j + 1)
                        alone(sp)
                        sp.dma_start(d["xbc_t"][:, j, gcols(g)], conv_out[:, j % 2, :n]).then_inc(xbc_stored[j % 2], 16)
                groups(sp, step)
                for p in range(2):
                    sp.wait_ge(qk_stored[p], 32 * (NQK // 2) * (NG + 1))
                    sp.wait_ge(xbc_stored[p], 16 * xbc_count(NG + 1, p))

            @block.gpsimd
            def _(pool):
                def load_xt(g, p):
                    n = width(g)
                    pool.dma_start(xt_hi[:, p, :, :n].bitcast(F32), d["xt_hi"][:, :, gcols(g)]).then_inc(xt_loaded[p], 16)
                    pool.dma_start(xt_lo[:, p, :, :n].bitcast(F32), d["xt_lo"][:, :, gcols(g)]).then_inc(xt_loaded[p], 16)

                load_xt(0, 0)
                for c in range(4):
                    pool.dma_start(taps[:, :, c], d["ssm_conv_w"][c].rearrange("(m p) -> p m", p=P),
                                   allow_slow_non_contiguous=True).then_inc(small_loaded, 16)
                pool.dma_start(shift[:], d["ssm_conv_b"].rearrange("(m p) -> p m", p=P), allow_slow_non_contiguous=True).then_inc(small_loaded, 16)
                for c in range(3):
                    pool.dma_start(halo_smp[:, :, c], d["state_ssm_conv"][c].rearrange("(m p) -> p m", p=P),
                                   allow_slow_non_contiguous=True).then_inc(small_loaded, 16)
                pool.memset(halo[:], 0.0).then_inc(halo_zeroed, 1)
                load_xt(1, 1)

                def step(g, p, i):
                    if not isinstance(g, int) or g + 2 <= NG:
                        pool.wait_ge(y_done, NM * (g + 1))
                        load_xt(g + 2, p)
                step(0, 0, 0)
                step(1, 1, 0)
                pool.wait_ge(y_done, NM * 3)
                load_xt(NG, 0)
                pool.wait_ge(conv_done, NXBC * NG)
                for c in range(3):
                    pool.dma_start(d["prompt_ssm_conv"][c].rearrange("(m p) -> p m", p=P), halo[:, :, c], allow_slow_non_contiguous=True).then_inc(state_stored, 16)
                pool.wait_ge(conv_done, NXBC * (NG + 1))
                for c in range(3):
                    pool.dma_start(d["sample_ssm_conv"][c].rearrange("(m p) -> p m", p=P), halo_smp[:, :, c], allow_slow_non_contiguous=True).then_inc(state_stored, 16)
                pool.wait_ge(state_stored, 16 * 6)

            @block.scalar
            def _(act):
                for k in range(KD):
                    act.wait_ge(w_loaded[k % 2], 32 * (k // 2 + 1))
                    act.copy(w_hi[:, k, :], w_raw[:, k % 2, :]).then_inc(w_hi_done, 1)

                def step(g, p, i):
                    n = width(g)
                    for j in range(NQK):
                        if not (isinstance(g, int) and g == 0 and j < 2):
                            act.wait_ge(qk_stored[j % 2], 32 * (NQK // 2 * g + j // 2))
                        act.wait_ge(y_done, NM * g + j + 1)
                        act.mul(qk_hi[:, j % 2, :n], ps_y[:, j, :n], scale(j)).then_inc(evac_done, 1)

                    def silu(j):
                        if not (isinstance(g, int) and g == 0 and j < 2):
                            act.wait_ge(xbc_stored[j % 2], 16 * xbc_count(g, j))
                        act.wait_ge(conv_done, NXBC * g + j + 1)
                        act.activation(conv_out[:, j % 2, :n], conv[:, j % 2, :n], ACT.Silu).then_inc(silu_done, 1)

                    for j in range(NXBC):
                        wait_if(act, conv_done, NXBC * g + j - (1 if j != 0 else 0) if j != 1 else NXBC * g)
                        act.wait_ge(y_done, NM * g + NQK + j + 1)
                        act.copy(cin[:, j % 2, 3:3 + n], ps_y[:, (NQK + j) % 8, :n]).then_inc(evac_done, 1)
                        if j >= 1:
                            silu(j - 1)
                    silu(NXBC - 1)
                groups(act, step)

            @block.vector
            def _(dve):
                for k in range(KD):
                    dve.wait_ge(w_hi_done, k + 1)
                    dve.tensor_tensor(w_lo[:, k, :], w_raw[:, k % 2, :], w_hi[:, k, :].bitcast(F32),
                                      ALU.subtract).then_inc(w_lo_done, 1)
                dve.wait_ge(small_loaded, 128)
                dve.wait_ge(halo_zeroed, 1)

                def step(g, p, i):
                    n = width(g)
                    h = halo_smp if isinstance(g, int) and g == NG else halo
                    for j in range(NQK):
                        if not (isinstance(g, int) and g == 0 and j < 2):
                            dve.wait_ge(qk_stored[j % 2], 32 * (NQK // 2 * g + j // 2))
                        dve.wait_ge(evac_done, NM * g + j + 1)
                        alone(dve)
                        dve.scalar_tensor_tensor(out=qk_lo[:, j % 2, :n], in0=ps_y[:, j, :n], scalar=scale(j),
                                                 in1=qk_hi[:, j % 2, :n].bitcast(F32), op0=ALU.mult,
                                                 op1=ALU.subtract).then_inc(qk_lo_done, 1)
                    for j in range(NXBC):
                        u, b = NXBC * g + j, j % 2
                        c, y = cin[:, b], conv[:, b, :n]
                        dve.wait_ge(evac_done, NM * g + NQK + j + 1)
                        dve.tensor_copy(c[:, 0:3], h[:, j, :]).then_inc(halo_in_done, 1)
                        if not (isinstance(g, int) and g == 0 and j < 2):
                            dve.wait_ge(silu_done, u if j == 0 else u - 1)
                        dve.wait_ge(halo_in_done, u + 1)
                        dve.tensor_scalar(y, c[:, 0:n], taps[:, j, 0:1], shift[:, j:j + 1], ALU.mult,
                                          ALU.add).then_inc(tap_done, 1)
                        for e in (1, 2):
                            dve.wait_ge(tap_done, 3 * u + e)
                            dve.scalar_tensor_tensor(out=y, in0=c[:, e:e + n], scalar=taps[:, j, e:e + 1], in1=y,
                                                     op0=ALU.mult, op1=ALU.add).then_inc(tap_done, 1)
                        dve.tensor_copy(h[:, j, :], c[:, n:n + 3])
                        dve.wait_ge(tap_done, 3 * u + 3)
                        dve.scalar_tensor_tensor(out=y, in0=c[:, 3:3 + n], scalar=taps[:, j, 3:4], in1=y,
                                                 op0=ALU.mult, op1=ALU.add).then_inc(conv_done, 1)
                groups(dve, step)

            @block.tensor
            def _(pe):
                def step(g, p, i):
                    n = width(g)
                    pe.wait_ge(xt_loaded[p], 32 * (i + 1))
                    for j in range(NM):
                        wait_if(pe, evac_done, NM * g + j - 4)
                        if j == NQK - 1:
                            wait_if(pe, qk_lo_done, NQK * g)
                        if j >= 8:
                            pe.wait_ge(qk_lo_done, NQK * g + j - 7)
                        for k in range(KD):
                            if isinstance(g, int) and g == 0 and j == 0:
                                pe.wait_ge(w_lo_done, k + 1)
                            c = slice(j * P, (j + 1) * P)
                            last = products(pe, ps_y[:, j % 8, :n], w_hi[:, k, c], w_lo[:, k, c],
                                            xt_hi[:, p, k, :n], xt_lo[:, p, k, :n], k == 0, k == KD - 1)
                        last.then_inc(y_done, 1)
                groups(pe, step)


class Band:

    def __init__(self, t):
        self.t = t
        self.smp = isinstance(t, int) and t == NT
        self.nb = min(t + 1, 5) if isinstance(t, int) else 5
        self.nq = NSMP if self.smp else P
        self.width = CACHE + NSMP if self.smp else self.nb * P
        self.col0 = 0 if self.smp else WIN - self.width

    def block_rows(self, k):
        return min(P, self.width - k * P)

    def first(self):
        return self.t + 1 - self.nb

    def block(self, k):
        return (k if k < CACHE // P else NT) if self.smp else self.first() + k

    def key_cols(self, c, n):
        if self.smp:
            return slice(c, c + n) if c < CACHE else slice(SEQ + c - CACHE, SEQ + c - CACHE + n)
        at = self.first() * P + c
        return slice(at, at + n) if isinstance(at, int) else bass.ds(at, n)


def attention(nc, d):
    with nc.cleanup_on_exit(), ExitStack() as ctx:
        m = Stage(nc, ctx, "at")
        k_hi, k_lo, v = m.sb("k_hi", [P, HEADS, ROWS], F32R), m.sb("k_lo", [P, HEADS, ROWS], F32R), m.sb("v", [P, NT + 1, AW])
        q, q_smp = m.sb("q", [P, 2, HEADS, P], F32R), m.sb("q_smp", [P, HEADS, NSMP], F32R)
        cache = m.sb("cache", [P, 4, HEADS, 2, HD])
        bias, bias_up = m.sb("bias", [P, HEADS, WIN]), m.sb("bias_up", [P, HEADS, WIN])
        ident, flip, ident_r = m.sb("ident", [P, P]), m.sb("flip", [P, P]), m.sb("ident_r", [P, HD], F32R)
        ext = m.sb("ext", [HEADS, WIN + P])
        s = m.sb("s", [P, 3, WIN])
        pt = m.sb("pt", [P, 2, 5, P])
        top, ntop, total, inv = (m.sb("top", [P, HEADS]), m.sb("ntop", [P, HEADS]), m.sb("total", [P, HEADS]), m.sb("inv", [P, HEADS]))
        o = m.sb("o", [P, 2, AW])
        k_rows = m.sb("k_rows", [P, 5, AW])
        ps_s, ps_t, ps_o = m.ps("ps_s", [P, 2, 1024]), m.ps("ps_t", [P, 1024]), m.ps("ps_o", [P, 2, 512])
        NFIRST, REST = 3, 512
        NO_REST = HEADS * NFIRST

        zero_done, ident_done, ident_r_done = m.sem("zero_done"), m.sem("ident_done"), m.sem("ident_r_done")
        table_loaded, ext_done, ext_stored, bias_loaded, bias_done = (
            m.sem("table_loaded"), m.sem("ext_done"), m.sem("ext_stored"), m.sem("bias_loaded"), m.sem("bias_done"))
        flip_done, bias_flipped, bias_copied = m.sem("flip_done"), m.sem("bias_flipped"), m.sem("bias_copied")
        cache_loaded, cache_turned, cache_hi_done, cache_lo_done = (
            m.sem("cache_loaded"), m.sem("cache_turned"), m.sem("cache_hi_done"), m.sem("cache_lo_done"))
        loaded = [m.sem("loaded0"), m.sem("loaded1")]
        smp_loaded = m.sem("smp_loaded")
        s_done, biased, ntop_done, exp_done = m.sem("s_done"), m.sem("biased"), m.sem("ntop_done"), m.sem("exp_done")
        turned, pt_done = m.sem("turned"), m.sem("pt_done")
        rest_turned, rest_done = m.sem("rest_turned"), m.sem("rest_done")
        pv_done, inv_done, o_done = m.sem("pv_done"), m.sem("inv_done"), m.sem("o_done")
        o_stored = [m.sem("o_stored0"), m.sem("o_stored1")]
        rows_turned, rows_done, rows_stored = m.sem("rows_turned"), m.sem("rows_done"), m.sem("rows_stored")
        caches_stored = m.sem("caches_stored")

        LOOP0, LOOP1 = 6, 14

        def tiles(eng, step, before_last=None):
            def straight(t):
                step(Band(t - 1) if t else None, Band(t), Band(t + 1) if t < NT else None, t % 2)
            for t in range(LOOP0):
                straight(t)
            with eng.Fori(LOOP0 // 2, LOOP1 // 2) as i:
                for p in range(2):
                    t = 2 * i + p
                    step(Band(t - 1), Band(t), Band(t + 1), p)
            if before_last:
                before_last()
            for t in range(LOOP1, NT + 1):
                straight(t)

        def heads(eng, step, before_last=None):
            def tile_step(before, cur, after, p):
                for h in range(HEADS):
                    prev = (cur, p, h - 1) if h else (before, 1 - p, HEADS - 1) if before else None
                    nxt, nxt2 = [(cur, p, x) if x < HEADS else (after, 1 - p, x - HEADS) if after else None
                                 for x in (h + 1, h + 2)]
                    step(prev, (cur, p, h), nxt, nxt2)
            tiles(eng, tile_step, before_last)

        def tile_count(b, p, each, ahead=0):
            return each * (b.t // 2 + ahead) if isinstance(b.t, int) else each // 2 * (b.t - p) + each * ahead

        with nc.Block() as block:
            @block.sync
            def _(sp):
                back = bass.AP(d["rel_bias"].tensor, REL - 1, [[REL, HEADS], [-1, REL]])
                sp.dma_start(ext[:, WIN - P - 1:WIN - P - 1 + REL], back, allow_slow_non_contiguous=True).then_inc(table_loaded, 16)
                by_head = {name: d[name].rearrange("(h f) c -> f h c", f=HD) for name in ("qk_hi", "qk_lo")}

                def load(b, p):
                    done = smp_loaded if b.smp else loaded[p]
                    n = b.nq
                    cols = tile_rows(b.t)
                    for part, at in (("qk_hi", 0), ("qk_lo", HD)):
                        dst = q_smp[at:at + HD, :, :] if b.smp else q[at:at + HD, p, :, :]
                        sp.dma_start(dst.bitcast(F32), by_head[part][:, 0:HEADS, cols]).then_inc(done, 16)
                    for part, k_part in (("qk_hi", k_hi), ("qk_lo", k_lo)):
                        for at in (0, HD):
                            sp.dma_start(k_part[at:at + HD, :, cols].bitcast(F32), by_head[part][:, HEADS:, cols]).then_inc(done, 16)
                    blk = slice(b.t, b.t + 1) if isinstance(b.t, int) else bass.ds(b.t, 1)
                    sp.dma_start(v[:n, blk, :], d["v_rows"][cols, :].rearrange("(a p) w -> p a w", a=1)).then_inc(done, 16)

                load(Band(0), 0)
                sp.wait_ge(ext_done, 1)
                sp.dma_start(d["rel_ext"], ext[:]).then_inc(ext_stored, 16)
                sp.wait_ge(ext_stored, 16)
                toeplitz = bass.AP(d["rel_ext"].tensor, 0, [[1, P], [WIN + P, HEADS], [1, WIN]])
                sp.dma_start(bias_up[:], toeplitz).then_inc(bias_loaded, 16)

                def step(before, cur, after, p):
                    if after is not None:
                        wait_if(sp, s_done, HEADS * cur.t)
                        alone(sp) if not isinstance(cur.t, int) else None
                        load(after, 1 - p)

                def load_cache_v():
                    sp.wait_ge(pv_done, HEADS * 8)
                    sp.dma_start(v[:, 0:4, :], d["cache_v"].rearrange("(b p) w -> p b w", p=P)).then_inc(smp_loaded, 16)
                tiles(sp, step, load_cache_v)
                sp.wait_ge(rows_done, 5)
                sp.dma_start(d["prompt_k"].rearrange("(b p) w -> p b w", p=P), k_rows[:, 0:4, :]).then_inc(rows_stored, 16)
                sp.dma_start(d["sample_k"], k_rows[:NSMP, 4, :]).then_inc(rows_stored, 16)
                sp.wait_ge(rows_stored, 32)

            @block.gpsimd
            def _(pool):
                make_identity(pool, ident, zero_done, ident_done)
                pool.memset(flip[:], 0.0).then_inc(zero_done, 1)
                pool.wait_ge(zero_done, 2)
                pool.affine_select(out=flip[:], in_=flip[:], compare_op=ALU.not_equal, fill=1.0, base=1 - P,
                                   pattern=[[1, P]], channel_multiplier=1).then_inc(flip_done, 1)
                pool.wait_ge(bias_copied, HEADS)
                pool.memset(bias[0:64, :, WIN - 64:], MASKED)
                pool.memset(bias[64:P, :, 0:64], MASKED).then_inc(bias_done, 1)
                for k in range(CACHE // P):
                    for twice in range(2):
                        pool.dma_start(cache[:, k, :, twice, :], d["cache_k"][k * P:(k + 1) * P, :].rearrange(
                            "p (h f) -> p h f", h=HEADS)).then_inc(cache_loaded, 16)
                pool.dma_start(d["prompt_v"], d["v_rows"][SEQ - 512:SEQ, :]).then_inc(caches_stored, 16)
                pool.dma_start(d["sample_v"], d["v_rows"][SEQ:ROWS, :]).then_inc(caches_stored, 16)
                pool.dma_start(d["sample_gmlp_v"], d["uv_rows"][SEQ:ROWS, CW:]).then_inc(caches_stored, 16)

                def store_o(b, p):
                    pool.wait_ge(o_done, HEADS * (b.t + 1))
                    alone(pool)
                    pool.dma_start(d["mixed"][tile_rows(b.t), 0:AW], o[:b.nq, p, :]).then_inc(o_stored[p], 16)

                def step(before, cur, after, p):
                    if before is not None:
                        store_o(before, 1 - p)
                tiles(pool, step)
                store_o(Band(NT), 0)
                pool.wait_ge(o_stored[0], 16 * 9)
                pool.wait_ge(o_stored[1], 16 * 8)
                pool.wait_ge(caches_stored, 48)

            @block.vector
            def _(dve):
                dve.wait_ge(table_loaded, 16)
                lo, hi = WIN - P - 1, WIN - P - 1 + REL
                dve.tensor_copy(ext[:, 0:lo], ext[:, lo:lo + 1].to_broadcast([HEADS, lo]))
                dve.tensor_copy(ext[:, hi:], ext[:, hi - 1:hi].to_broadcast([HEADS, WIN + P - hi])).then_inc(ext_done, 1)
                dve.wait_ge(ident_done, 1)
                dve.tensor_copy(ident_r[:], ident[:, 0:HD]).then_inc(ident_r_done, 1)
                dve.wait_ge(bias_done, 1)

                def add_bias(x):
                    b, p, h = x
                    n, par = HEADS * b.t + h, h % 2
                    dve.wait_ge(s_done, n + 1)
                    if isinstance(n, int) and n - 3 < NO_REST:
                        wait_if(dve, turned, n - 2)
                    else:
                        dve.wait_ge(rest_turned, n - 2 - NO_REST)
                    alone(dve)
                    dve.tensor_tensor_reduce(out=s[:b.nq, h % 3, :b.width], in0=ps_s[:b.nq, par, :b.width],
                                             in1=bias[:b.nq, h, b.col0:b.col0 + b.width], scale=1.0, scalar=-3e38,
                                             op0=ALU.add, op1=ALU.max, accum_out=top[:b.nq, h:h + 1]).then_inc(biased, 1)
                    dve.wait_ge(biased, n + 1)
                    dve.tensor_scalar(ntop[:b.nq, h:h + 1], top[:b.nq, h:h + 1], -1.0, None,
                                      ALU.mult).then_inc(ntop_done, 1)

                def normalise(x):
                    b, p, h = x
                    n, par = HEADS * b.t + h, h % 2
                    if h == 0 and not (isinstance(b.t, int) and b.t < 2):
                        dve.wait_ge(o_stored[p], tile_count(b, p, 16))
                    dve.wait_ge(pv_done, n + 1)
                    dve.reciprocal(inv[:b.nq, h:h + 1], total[:b.nq, h:h + 1]).then_inc(inv_done, 1)
                    dve.wait_ge(inv_done, n + 1)
                    dve.tensor_scalar(o[:b.nq, p, h * HD:(h + 1) * HD], ps_o[:b.nq, par, 0:HD], inv[:b.nq, h:h + 1],
                                      None, ALU.mult).then_inc(o_done, 1)

                def take_rest(x):
                    b, p, h = x
                    n, par = HEADS * b.t + h, h % 2
                    if b.nb <= NFIRST:
                        return
                    dve.wait_ge(rest_turned, n - NO_REST + 1)
                    wait_if(dve, pv_done, n - 1)
                    if not b.smp:
                        nr = b.nb - NFIRST
                        alone(dve)
                        ins = dve.tensor_copy(pt[:, par, NFIRST:b.nb, :], ps_t[:, REST:REST + nr * P].rearrange("p (b c) -> p b c", b=nr))
                    else:
                        dve.tensor_copy(pt[:, par, NFIRST, :NSMP], ps_t[:, REST:REST + NSMP])
                        ins = dve.tensor_copy(pt[:NSMP, par, NFIRST + 1, :NSMP], ps_t[:NSMP, REST + P:REST + P + NSMP])
                    ins.then_inc(rest_done, 1)

                add_bias((Band(0), 0, 0))
                add_bias((Band(0), 0, 1))

                def step(prev, cur, nxt, nxt2):
                    if nxt2:
                        add_bias(nxt2)
                    take_rest(cur)
                    if prev:
                        normalise(prev)

                def cache_lo():
                    for h in range(HEADS):
                        dve.wait_ge(cache_hi_done, h + 1)
                        dve.tensor_tensor(k_lo[:, h, 0:CACHE], ps_o[:, h % 2, :], k_hi[:, h, 0:CACHE].bitcast(F32),
                                          ALU.subtract).then_inc(cache_lo_done, 1)
                heads(dve, step, cache_lo)
                normalise((Band(NT), 0, HEADS - 1))
                for b in range(5):
                    n = P if b < 4 else NSMP
                    dve.wait_ge(rows_turned, b + 1)
                    src = ps_s[:n, b // 2, (b % 2) * 512:(b % 2) * 512 + AW] if b < 4 else ps_t[:n, 0:AW]
                    dve.tensor_copy(k_rows[:n, b, :], src).then_inc(rows_done, 1)

            @block.scalar
            def _(act):
                def exp(x):
                    b, p, h = x
                    n, par = HEADS * b.t + h, h % 2
                    act.wait_ge(ntop_done, n + 1)
                    act.activation(s[:b.nq, h % 3, :b.width], s[:b.nq, h % 3, :b.width], ACT.Exp,
                                   bias=ntop[:b.nq, h:h + 1],
                                   accum_out=total[:b.nq, h:h + 1]).then_inc(exp_done, 1)

                def take_pt(x):
                    b, p, h = x
                    n, par = HEADS * b.t + h, h % 2
                    act.wait_ge(turned, n + 1)
                    wait_if(act, pv_done, n - 1)
                    nf = min(b.nb, NFIRST)
                    act.copy(pt[:, par, 0:nf, :b.nq],
                             ps_t[:, 0:nf * P].rearrange("p (b c) -> p b c", b=nf)[:, :, :b.nq]).then_inc(pt_done, 1)

                for h in range(HEADS):
                    act.wait_ge(bias_flipped, h + 1)
                    act.copy(bias[:, h, :], (ps_s[:, 0] if h % 2 == 0 else ps_t)[:, 0:WIN]).then_inc(bias_copied, 1)

                exp((Band(0), 0, 0))

                def step(prev, cur, nxt, nxt2):
                    if nxt:
                        exp(nxt)
                    take_pt(cur)

                def cache_hi():
                    for h in range(HEADS):
                        act.wait_ge(cache_turned, h + 1)
                        act.copy(k_hi[:, h, 0:CACHE], ps_o[:, h % 2, :]).then_inc(cache_hi_done, 1)
                heads(act, step, cache_hi)

            @block.tensor
            def _(pe):
                pe.wait_ge(ident_done, 1)
                pe.wait_ge(flip_done, 1)
                pe.wait_ge(bias_loaded, 16)
                for h in range(HEADS):
                    wait_if(pe, bias_copied, h - 1)
                    dst = ps_s[:, 0] if h % 2 == 0 else ps_t
                    pe.matmul(dst[:, 0:512], flip[:], bias_up[:, h, 0:512], start=True, stop=True)
                    pe.matmul(dst[:, 512:WIN], flip[:], bias_up[:, h, 512:], start=True, stop=True).then_inc(bias_flipped, 1)
                pe.wait_ge(bias_copied, HEADS)

                def score(x):
                    b, p, h = x
                    n, par = HEADS * b.t + h, h % 2
                    if h == 0:
                        if b.smp:
                            pe.wait_ge(smp_loaded, 16 * 8)
                        else:
                            pe.wait_ge(loaded[p], tile_count(b, p, 16 * 7, 1))
                    wait_if(pe, biased, n - 1)
                    queries = q_smp[:, h, :] if b.smp else q[:, p, h, :]
                    for c in range(0, b.width, 512):
                        w = min(512, b.width - c)
                        out = ps_s[:b.nq, par, c:c + w]
                        pe.matmul(out, queries, k_hi[:, h, b.key_cols(c, w)], start=True, stop=False)
                        last = pe.matmul(out, queries, k_lo[:, h, b.key_cols(c, w)], start=False, stop=True)
                    last.then_inc(s_done, 1)

                def turn(x):
                    b, p, h = x
                    n, par = HEADS * b.t + h, h % 2
                    pe.wait_ge(exp_done, n + 1)
                    wait_if(pe, pt_done, n)
                    for k in range(b.nb):
                        w = b.block_rows(k)
                        at = k * P if k < NFIRST else REST + (k - NFIRST) * P
                        if k == NFIRST:
                            last.then_inc(turned, 1)
                            wait_if(pe, rest_done, n - NO_REST)
                        last = pe.transpose(ps_t[:w, at:at + b.nq], s[:b.nq, h % 3, k * P:k * P + w],
                                            ident[:b.nq, :b.nq])
                    last.then_inc(turned if b.nb <= NFIRST else rest_turned, 1)

                def out(x):
                    b, p, h = x
                    n, par = HEADS * b.t + h, h % 2
                    pe.wait_ge(pt_done, n + 1)
                    if b.nb > NFIRST:
                        pe.wait_ge(rest_done, n - NO_REST + 1)
                    wait_if(pe, o_done, n - 1)
                    for k in range(b.nb):
                        w = b.block_rows(k)
                        blk = b.block(k)
                        blk = blk if isinstance(blk, int) else bass.ds(blk, 1)
                        vals = v[:w, blk, h * HD:(h + 1) * HD]
                        if not isinstance(blk, int):
                            vals = vals.rearrange("p a c -> p (a c)")
                        last = pe.matmul(ps_o[:b.nq, par, 0:HD], pt[:w, par, k, :b.nq], vals, start=(k == 0), stop=(k == b.nb - 1))
                    last.then_inc(pv_done, 1)

                score((Band(0), 0, 0))
                score((Band(0), 0, 1))

                def step(prev, cur, nxt, nxt2):
                    if nxt2:
                        score(nxt2)
                    turn(cur)
                    if prev:
                        out(prev)

                def turn_cache():
                    pe.wait_ge(cache_loaded, 16 * 8)
                    pe.wait_ge(o_done, HEADS * LOOP1 - 1)
                    for h in range(HEADS):
                        wait_if(pe, cache_lo_done, h - 1)
                        for k in range(CACHE // P):
                            twice = cache[:, k, h].rearrange("p a f -> p (a f)")
                            last = pe.transpose(ps_o[:, h % 2, k * P:(k + 1) * P], twice, ident[:])
                        last.then_inc(cache_turned, 1)
                    pe.wait_ge(cache_lo_done, HEADS)
                heads(pe, step, turn_cache)
                out((Band(NT), 0, HEADS - 1))
                pe.wait_ge(ident_r_done, 1)
                pe.wait_ge(pt_done, HEADS * (NT + 1))
                for b in range(5):
                    n = P if b < 4 else NSMP
                    dst = ps_s[:n, b // 2, (b % 2) * 512:(b % 2) * 512 + AW] if b < 4 else ps_t[:n, 0:AW]
                    cols = slice(SEQ - CACHE + b * P, SEQ - CACHE + b * P + n)
                    for h in range(HEADS):
                        c = slice(h * HD, (h + 1) * HD)
                        pe.matmul(dst[:, c], k_hi[:, h, cols], ident_r[:], start=True, stop=False)
                        last = pe.matmul(dst[:, c], k_lo[:, h, cols], ident_r[:], start=False, stop=True)
                    last.then_inc(rows_turned, 1)


def ssd_and_gmlp(nc, d):
    with nc.cleanup_on_exit(), ExitStack() as ctx:
        m = Stage(nc, ctx, "sg")
        NC_ = NT + 1
        ident, upper, ones = m.sb("ident", [P, P]), m.sb("upper", [P, P]), m.sb("ones", [P, P])
        dt = m.sb("dt", [P, NC_, HEADS])
        e, w2, num, den = m.sb("e", [P, NC_, HEADS]), m.sb("w2", [P, NC_, HEADS]), m.sb("num", [P, NC_, HEADS]), m.sb("den", [P, NC_, HEADS])
        dta, ncum, ecum, dts, etot = (m.sb("dta", [P, NC_, HEADS]), m.sb("ncum", [P, NC_, HEADS]), m.sb("ecum", [P, NC_, HEADS]),
                                      m.sb("dts", [P, NC_, HEADS]), m.sb("etot", [P, NC_, HEADS]))
        dt_bias, a_row, d_row = m.sb("dt_bias", [P, HEADS]), m.sb("a_row", [P, HEADS]), m.sb("d_row", [P, HEADS])
        ws, wt, gb = m.sb("ws", [P, CG, P]), m.sb("wt", [P, CG, P]), m.sb("gb", [P, CG])
        st_in, st_out = m.sb("st_in", [P, 3, P]), m.sb("st_out", [P, 2, 3, P])
        state = m.sb("state", [P, AW])
        decayed = m.sb("decayed", [P, AW])
        xbc = m.sb("xbc", [P, 4, NXBC, P])
        z, uv = m.sb("z", [P, 4, AW]), m.sb("uv", [P, 4, 2 * CW])
        dta_t, ncum_t = m.sb("dta_t", [P, 2, HEADS]), m.sb("ncum_t", [P, 2, HEADS])
        rows = m.sb("rows", [P, 2, AW + 2 * STATE])
        xdt, xds, xd = m.sb("xdt", [P, 2, AW]), m.sb("xds", [P, 2, AW]), m.sb("xd", [P, 2, AW])
        seg, cbm, mix = m.sb("seg", [P, 2, HEADS, P]), m.sb("cbm", [P, 2, 2, P]), m.sb("mix", [P, 2, HEADS, P])
        y1, y2, y3 = m.sb("y1", [P, AW]), m.sb("y2", [P, AW]), m.sb("y3", [P, AW])
        ob, oc = m.sb("ob", [P, 2, AW]), m.sb("oc", [P, 2, CW])
        ps_a, ps_r = m.ps("ps_a", [P, 1024]), m.ps("ps_r", [P, 1024])
        ps_c, ps_off, ps_diag, ps_st = m.ps("ps_c", [P, 512]), m.ps("ps_off", [P, 512]), m.ps("ps_diag", [P, 512]), m.ps("ps_st", [P, 512])

        zero_done, ident_done, const_done = m.sem("zero_done"), m.sem("ident_done"), m.sem("const_done")
        small_loaded, prep, prep_done, prep_act, prep_pe = (m.sem("small_loaded"), m.sem("prep"), m.sem("prep_done"), m.sem("prep_act"),
                                                           m.sem("prep_pe"))
        loaded = [m.sem(f"loaded{b}") for b in range(4)]
        dta_done, cum_done, rows_turned, cb_done = m.sem("dta_done"), m.sem("cum_done"), m.sem("rows_turned"), m.sem("cb_done")
        rows_done, seg_done, exp_done, cbm_done, mix_done = (m.sem("rows_done"), m.sem("seg_done"), 
                                                                        m.sem("exp_done"), m.sem("cbm_done"), m.sem("mix_done"))
        scaled, off_done, st_done, diag_done, gm_done = m.sem("scaled"), m.sem("off_done"), m.sem("st_done"), m.sem("diag_done"), m.sem("gm_done")
        y1_done, y2_done, y3_done, ob_done, oc_done = m.sem("y1_done"), m.sem("y2_done"), m.sem("y3_done"), m.sem("ob_done"), m.sem("oc_done")
        decayed_done, state_done = m.sem("decayed_done"), m.sem("state_done")
        o_stored = [m.sem("o_stored0"), m.sem("o_stored1")]
        ncum_done, dta_all_done = m.sem("ncum_done"), m.sem("dta_all_done")
        fin_turned, fin_done, fin_stored, init_turned = m.sem("fin_turned"), m.sem("fin_done"), m.sem("fin_stored"), m.sem("init_turned")

        def chunks(eng, step):
            for t in range(4):
                step(t, t, t % 2, 0)
            with eng.Fori(1, 3) as i:
                for b in range(4):
                    step(4 * i + b, b, b % 2, i)
            for t in range(12, NC_):
                step(t, t % 4, t % 2, t // 4)

        def col(t):
            return slice(t, t + 1) if isinstance(t, int) else bass.ds(t, 1)

        def per_head(a, t):
            return a[:, col(t), :].rearrange("p a h -> p (a h)").unsqueeze(2).to_broadcast([P, HEADS, HD])

        def by_head(a):
            return a.rearrange("p (h c) -> p h c", h=HEADS)

        with nc.Block() as block:
            @block.sync
            def _(sp):
                sp.dma_start(dt[:, 0:NT, :], d["dt_rows"][0:SEQ, :].rearrange("(t p) h -> p t h", p=P)).then_inc(small_loaded, 16)
                sp.dma_start(dt[:NSMP, NT, :], d["dt_rows"][SEQ:ROWS, :]).then_inc(small_loaded, 16)
                sp.dma_start(dt_bias[:], bc_row(d["ssm_dt_bias"], HEADS)).then_inc(small_loaded, 16)
                sp.dma_start(a_row[:], bc_row(d["ssm_a_log"], HEADS)).then_inc(small_loaded, 16)
                sp.dma_start(d_row[:], bc_row(d["ssm_d"], HEADS)).then_inc(small_loaded, 16)
                sp.dma_start(ws[:], d["gmlp_w"].rearrange("g i j -> i g j")).then_inc(small_loaded, 16)
                sp.dma_start(gb[:], d["gmlp_b"].rearrange("g i -> i g"), allow_slow_non_contiguous=True).then_inc(small_loaded, 16)
                sp.dma_start(st_in[:], d["state_ssm"].rearrange("(m p) n -> p m n", p=P)).then_inc(small_loaded, 16)

                def load(t, b):
                    n = n_rows(t)
                    sp.dma_start(xbc[:, b, :, :n], d["xbc_t"][:, :, tile_rows(t)]).then_inc(loaded[b], 16)
                    sp.dma_start(z[:n, b, :], d["z_rows"][tile_rows(t), :]).then_inc(loaded[b], 16)
                    sp.dma_start(uv[:n, b, :], d["uv_rows"][tile_rows(t), :]).then_inc(loaded[b], 16)

                for t in range(4):
                    load(t, t)

                def step(t, b, p, i):
                    n = n_rows(t)
                    sp.wait_ge(oc_done, t + 1)
                    alone(sp)
                    sp.dma_start(d["mixed"][tile_rows(t), 2 * AW:], oc[:n, p, :]).then_inc(o_stored[p], 16)
                    sp.wait_ge(ob_done, t + 1)
                    alone(sp)
                    sp.dma_start(d["mixed"][tile_rows(t), AW:2 * AW], ob[:n, p, :]).then_inc(o_stored[p], 16)
                    if not isinstance(t, int) or t + 4 <= NT:
                        load(t + 4, b)
                chunks(sp, step)
                sp.wait_ge(o_stored[0], 32 * 9)
                sp.wait_ge(o_stored[1], 32 * 8)

            @block.gpsimd
            def _(pool):
                make_identity(pool, ident, zero_done, ident_done)
                pool.memset(ones[:], 1.0).then_inc(zero_done, 1)
                pool.wait_ge(zero_done, 2)
                pool.affine_select(out=upper[:], in_=ones[:], compare_op=ALU.is_ge, fill=0.0, base=0,
                                   pattern=[[1, P]], channel_multiplier=-1).then_inc(const_done, 1)

                def scale(t, p):
                    n = n_rows(t)
                    pool.wait_ge(rows_done, t + 1)
                    if not (isinstance(t, int) and t < 2):
                        pool.wait_ge(diag_done, t - 1)
                        pool.wait_ge(y2_done, t - 1)
                        alone(pool)
                    x = by_head(rows[:n, p, 0:AW])
                    pool.tensor_tensor(by_head(xdt[:n, p, :]), x, per_head(dt, t)[:n], ALU.mult)
                    pool.tensor_tensor(by_head(xds[:n, p, :]), x, per_head(dts, t)[:n], ALU.mult)
                    pool.tensor_tensor(by_head(xd[:n, p, :]), x, d_row[:n, :].unsqueeze(2).to_broadcast([n, HEADS, HD]),
                                       ALU.mult).then_inc(scaled, 1)

                def back(t, b, p, i):
                    n = n_rows(t)
                    pool.wait_ge(state_done, NT + 2 if isinstance(t, int) and t == NT else t + 1)
                    pool.tensor_tensor(by_head(decayed[:]), by_head(state[:]), per_head(etot, t), ALU.mult).then_inc(decayed_done, 1)
                    pool.wait_ge(y1_done, t + 1)
                    wait_if(pool, y3_done, t)
                    pool.tensor_tensor(y2[:n, :], y1[:n, :], xd[:n, p, :], ALU.add).then_inc(y2_done, 1)
                    pool.wait_ge(y3_done, t + 1)
                    if not (isinstance(t, int) and t < 2):
                        pool.wait_ge(o_stored[p], 32 * (2 * i + b // 2))
                    pool.tensor_tensor(ob[:n, p, :], y3[:n, :], z[:n, b, :], ALU.mult).then_inc(ob_done, 1)

                pool.wait_ge(prep_done, 1)
                scale(0, 0)

                def step(t, b, p, i):
                    if not isinstance(t, int) or t + 1 <= NT:
                        scale(t + 1, 1 - p)
                    back(t, b, p, i)
                chunks(pool, step)
                pool.wait_ge(fin_done, 1)
                pool.dma_start(d["prompt_ssm"].rearrange("(m p) n -> p m n", p=P), st_out[:, 0]).then_inc(fin_stored, 16)
                pool.wait_ge(fin_done, 2)
                pool.dma_start(d["sample_ssm"].rearrange("(m p) n -> p m n", p=P), st_out[:, 1]).then_inc(fin_stored, 16)
                pool.wait_ge(fin_stored, 32)

            @block.scalar
            def _(act):
                act.wait_ge(small_loaded, 128)
                act.activation(a_row[:], a_row[:], ACT.Exp).then_inc(prep_act, 1)
                act.wait_ge(prep, 2)
                act.activation(e[:], e[:], ACT.Exp).then_inc(prep_act, 1)
                act.wait_ge(ncum_done, 2)
                act.activation(ecum[:], ncum[:], ACT.Exp, scale=-1.0)
                act.activation(etot[:], ps_r[:, 0:NC_ * HEADS].rearrange("p (t h) -> p t h", h=HEADS), ACT.Exp)
                act.activation(den[:], num[:], ACT.Exp).then_inc(prep_act, 1)
                act.wait_ge(prep_done, 1)

                def front(t, p):
                    n = n_rows(t)
                    act.wait_ge(rows_turned, t + 1)
                    if not (isinstance(t, int) and t < 2):
                        act.wait_ge(scaled, t - 1)
                        act.wait_ge(st_done, t - 1)
                    act.copy(rows[:n, p, :], ps_r[:n, 0:AW + 2 * STATE]).then_inc(rows_done, 1)
                    act.wait_ge(seg_done, t + 1)
                    act.activation(seg[:n, p, :, :n], seg[:n, p, :, :n], ACT.Exp).then_inc(exp_done, 1)

                front(0, 0)

                def step(t, b, p, i):
                    if not isinstance(t, int) or t + 1 <= NT:
                        front(t + 1, 1 - p)
                chunks(act, step)
                for f in range(2):
                    act.wait_ge(fin_turned, f + 1)
                    act.copy(st_out[:, f], ps_st[:, 0:AW].rearrange("p (m n) -> p m n", m=3)).then_inc(fin_done, 1)

            @block.vector
            def _(dve):
                count = [0]

                def link(ins):
                    count[0] += 1
                    ins.then_inc(prep, 1)
                    dve.wait_ge(prep, count[0])

                dve.memset(dt[NSMP:, NT, :], 0.0)
                dve.memset(state[:], 0.0).then_inc(state_done, 1)
                dve.wait_ge(state_done, 1)
                dve.wait_ge(small_loaded, 128)
                link(dve.tensor_tensor(dt[:], dt[:], dt_bias[:].unsqueeze(1).to_broadcast([P, NC_, HEADS]), ALU.add))
                link(dve.scalar_tensor_tensor(out=e[:], in0=dt[:], scalar=-1.0, in1=dt[:], op0=ALU.mult, op1=ALU.min))
                dve.wait_ge(prep_act, 2)
                link(dve.tensor_scalar(den[:], e[:], 2.0, None, ALU.add))
                link(dve.reciprocal(den[:], den[:]))
                link(dve.tensor_tensor(e[:], e[:], den[:], ALU.mult))
                link(dve.tensor_tensor(w2[:], e[:], e[:], ALU.mult))
                link(dve.tensor_scalar(num[:], w2[:], 1.0 / 17, None, ALU.mult))
                for k in (15, 13, 11, 9, 7, 5, 3):
                    link(dve.scalar_tensor_tensor(out=num[:], in0=num[:], scalar=1.0 / k, in1=w2[:], op0=ALU.add, op1=ALU.mult))
                link(dve.scalar_tensor_tensor(out=num[:], in0=num[:], scalar=1.0, in1=e[:], op0=ALU.add, op1=ALU.mult))
                link(dve.tensor_scalar(dt[:], dt[:], 0.0, None, ALU.max))
                link(dve.scalar_tensor_tensor(out=dt[:], in0=num[:], scalar=2.0, in1=dt[:], op0=ALU.mult, op1=ALU.add))
                link(dve.tensor_scalar(a_row[:], a_row[:], -1.0, None, ALU.mult))
                link(dve.tensor_tensor(dta[:], dt[:], a_row[:].unsqueeze(1).to_broadcast([P, NC_, HEADS]), ALU.mult))
                dve.memset(dta[NSMP:, NT, :], 0.0).then_inc(dta_all_done, 1)
                dve.wait_ge(dta_all_done, 1)
                dve.wait_ge(prep_pe, 1)
                dve.tensor_scalar(ncum[:], ps_a[:, 0:NC_ * HEADS].rearrange("p (t h) -> p t h", h=HEADS), -1.0, None,
                                  ALU.mult).then_inc(ncum_done, 1)
                dve.wait_ge(ncum_done, 1)
                dve.tensor_tensor(num[:], ncum[:], ps_r[:, 0:NC_ * HEADS].rearrange("p (t h) -> p t h", h=HEADS),
                                  ALU.add).then_inc(ncum_done, 1)
                dve.wait_ge(prep_pe, 2)
                dve.tensor_tensor(wt[:], ps_off[:].rearrange("p (g j) -> p g j", g=CG),
                                  upper[:].unsqueeze(1).to_broadcast([P, CG, P]), ALU.mult)
                dve.wait_ge(prep_act, 3)
                dve.tensor_tensor(dts[:], dt[:], den[:], ALU.mult).then_inc(prep_done, 1)

                def take_dta(t, p):
                    if not (isinstance(t, int) and t < 2):
                        dve.wait_ge(cum_done, t - 1)
                        dve.wait_ge(seg_done, t - 1)
                    dve.tensor_copy(ncum_t[:, p, :], ncum[:, col(t), :].rearrange("p a h -> p (a h)"))
                    dve.tensor_copy(dta_t[:, p, :], dta[:, col(t), :].rearrange("p a h -> p (a h)")).then_inc(dta_done, 1)

                def differences(t, p):
                    n = n_rows(t)
                    dve.wait_ge(cum_done, t + 1)
                    dve.wait_ge(dta_done, t + 1)
                    if not (isinstance(t, int) and t < 2):
                        dve.wait_ge(mix_done, t - 1)
                    for h in range(HEADS):
                        last = dve.tensor_scalar(seg[:n, p, h, :n], ps_a[:n, h * P:h * P + n], ncum_t[:n, p, h:h + 1], 0.0,
                                                 ALU.add, ALU.min)
                    last.then_inc(seg_done, 1)
                    dve.wait_ge(cb_done, t + 1)
                    dve.tensor_tensor(cbm[:n, p, :, :n], ps_c[:n, 0:2 * P].rearrange("p (g l) -> p g l", g=2)[:, :, :n],
                                      upper[:n, :n].unsqueeze(1).to_broadcast([n, 2, n]), ALU.mult).then_inc(cbm_done, 1)

                def mixing(t, p):
                    n = n_rows(t)
                    dve.wait_ge(exp_done, t + 1)
                    dve.wait_ge(cbm_done, t + 1)
                    if not (isinstance(t, int) and t < 2):
                        dve.wait_ge(diag_done, t - 1)
                    for g in range(2):
                        last = dve.tensor_tensor(mix[:n, p, 3 * g:3 * g + 3, :n], seg[:n, p, 3 * g:3 * g + 3, :n],
                                                 cbm[:n, p, g, :n].unsqueeze(1).to_broadcast([n, 3, n]), ALU.mult)
                    last.then_inc(mix_done, 1)

                take_dta(0, 0)
                take_dta(1, 1)
                differences(0, 0)
                mixing(0, 0)

                def step(t, b, p, i):
                    n = n_rows(t)
                    more = not isinstance(t, int) or t + 1 <= NT
                    if not isinstance(t, int) or t + 2 <= NT:
                        take_dta(t + 2, p)
                    if more:
                        differences(t + 1, 1 - p)
                    dve.wait_ge(off_done, t + 1)
                    wait_if(dve, y2_done, t)
                    dve.tensor_tensor(by_head(y1[:n, :]), by_head(ps_off[:n, 0:AW]), per_head(ecum, t)[:n], ALU.mult).then_inc(y1_done, 1)
                    dve.wait_ge(decayed_done, t + 1)
                    dve.tensor_tensor(state[:], decayed[:], ps_st[:, 0:AW], ALU.add).then_inc(state_done, 1)
                    if more:
                        mixing(t + 1, 1 - p)
                    dve.wait_ge(diag_done, t + 1)
                    dve.wait_ge(y2_done, t + 1)
                    wait_if(dve, ob_done, t)
                    dve.tensor_tensor(y3[:n, :], y2[:n, :], ps_diag[:n, 0:AW], ALU.add).then_inc(y3_done, 1)
                    dve.wait_ge(gm_done, t + 1)
                    if not (isinstance(t, int) and t < 2):
                        dve.wait_ge(o_stored[p], 32 * (2 * i + b // 2))
                    for g in range(CG):
                        c = slice(g * 64, g * 64 + 64)
                        last = dve.scalar_tensor_tensor(out=oc[:n, p, c], in0=ps_c[:n, 2 * P + g * 64:2 * P + g * 64 + 64],
                                                        scalar=gb[:n, g:g + 1], in1=uv[:n, b, c], op0=ALU.add, op1=ALU.mult)
                    last.then_inc(oc_done, 1)
                    if isinstance(t, int) and t == NT - 1:
                        dve.wait_ge(init_turned, 1)
                        dve.tensor_copy(state[:], ps_st[:, 0:AW]).then_inc(state_done, 1)
                chunks(dve, step)

            @block.tensor
            def _(pe):
                pe.wait_ge(const_done, 1)
                pe.wait_ge(ident_done, 1)
                pe.wait_ge(small_loaded, 128)
                for g in range(CG):
                    last = pe.transpose(ps_off[:, g * P:(g + 1) * P], ws[:, g, :], ident[:])
                pe.wait_ge(dta_all_done, 1)
                flat = dta[:].rearrange("p t h -> p (t h)")
                pe.matmul(ps_a[:, 0:NC_ * HEADS], upper[:], flat, start=True, stop=True)
                pe.matmul(ps_r[:, 0:NC_ * HEADS], ones[:], flat, start=True, stop=True).then_inc(prep_pe, 1)
                pe.transpose(ps_off[:, 3 * P:4 * P], ws[:, 3, :], ident[:]).then_inc(prep_pe, 1)

                def front(t, b, p, i):
                    n = n_rows(t)
                    pe.wait_ge(loaded[b], 48 * (i + 1))
                    if isinstance(t, int) and t == 0:
                        pe.wait_ge(prep_done, 1)
                    wait_if(pe, rows_done, t)
                    for j in range(5):
                        last = pe.transpose(ps_r[:n, j * P:(j + 1) * P], xbc[:, b, j, :n], ident[:])
                    last.then_inc(rows_turned, 1)
                    pe.wait_ge(dta_done, t + 1)
                    wait_if(pe, seg_done, t)
                    for h in range(HEADS):
                        last = pe.matmul(ps_a[:n, h * P:h * P + n], dta_t[:n, p, h:h + 1].to_broadcast([n, n]), upper[:n, :n],
                                         start=True, stop=True)
                    last.then_inc(cum_done, 1)
                    wait_if(pe, cbm_done, t)
                    wait_if(pe, oc_done, t - 1)
                    for g in range(2):
                        last = pe.matmul(ps_c[:n, g * P:g * P + n], xbc[:, b, 3 + g, :n], xbc[:, b, 5 + g, :n], start=True, stop=True)
                    last.then_inc(cb_done, 1)

                front(0, 0, 0, 0)

                def step(t, b, p, i):
                    n = n_rows(t)
                    more = not isinstance(t, int) or t + 1 <= NT
                    if more:
                        front(t + 1, (b + 1) % 4, 1 - p, i + (b + 1) // 4)
                    pe.wait_ge(scaled, t + 1)
                    pe.wait_ge(state_done, NT + 2 if isinstance(t, int) and t == NT else t + 1)
                    for g in range(2):
                        c = slice(3 * g * HD, 3 * (g + 1) * HD)
                        last = pe.matmul(ps_st[:, c], rows[:n, p, AW + g * P:AW + (g + 1) * P], xds[:n, p, c], start=True, stop=True)
                    last.then_inc(st_done, 1)
                    wait_if(pe, y1_done, t)
                    for g in range(2):
                        c = slice(3 * g * HD, 3 * (g + 1) * HD)
                        last = pe.matmul(ps_off[:n, c], xbc[:, b, 5 + g, :n], state[:, c], start=True, stop=True)
                    last.then_inc(off_done, 1)
                    pe.wait_ge(mix_done, t + 1)
                    wait_if(pe, y3_done, t)
                    for h in range(HEADS):
                        c = slice(h * HD, (h + 1) * HD)
                        last = pe.matmul(ps_diag[:n, c], mix[:n, p, h, :n], xdt[:n, p, c], start=True, stop=True)
                    last.then_inc(diag_done, 1)
                    if more:
                        pe.wait_ge(cbm_done, t + 2)
                    for g in range(CG):
                        last = pe.matmul(ps_c[:n, 2 * P + g * 64:2 * P + g * 64 + 64], wt[:n, g, :n],
                                         uv[:n, b, CW + g * 64:CW + (g + 1) * 64], start=True, stop=True)
                    last.then_inc(gm_done, 1)
                    if isinstance(t, int) and t == NT - 1:
                        turn_state(NT + 1)
                        pe.wait_ge(fin_done, 1)
                        for j in range(3):
                            last = pe.transpose(ps_st[:, j * P:(j + 1) * P], st_in[:, j, :], ident[:])
                        last.then_inc(init_turned, 1)

                def turn_state(value):
                    pe.wait_ge(state_done, value)
                    for j in range(3):
                        last = pe.transpose(ps_st[:, j * P:(j + 1) * P], state[:, j * P:(j + 1) * P], ident[:])
                    last.then_inc(fin_turned, 1)
                chunks(pe, step)
                turn_state(NT + 3)


def mix_out(nc, d):
    with nc.cleanup_on_exit(), ExitStack() as ctx:
        m = Stage(nc, ctx, "mo")
        segs = [(0, AW), (AW, AW), (2 * AW, CW)]
        w_raw = m.sb("w_raw", [P, 2, D])
        w_hi, w_lo = m.sb("w_hi", [P, KD, D], F32R), m.sb("w_lo", [P, KD, D], F32R)
        g_mix, g_ln, b_ln = m.sb("g_mix", [P, D]), m.sb("g_ln", [P, D]), m.sb("b_ln", [P, D])
        mx, x, y = m.sb("mx", [P, 2, D]), m.sb("x", [P, 2, D]), m.sb("y", [P, 2, D])
        sq, ss, rms, inv = m.sb("sq", [P, D]), m.sb("ss", [P, 3]), m.sb("rms", [P, 3]), m.sb("inv", [P, 3])
        mt_hi, mt_lo = m.sb("mt_hi", [P, 2, KD, P], F32R), m.sb("mt_lo", [P, 2, KD, P], F32R)
        yt_hi, yt_lo = m.sb("yt_hi", [P, 2, KD, P], F32R), m.sb("yt_lo", [P, 2, KD, P], F32R)
        stats, mv, sd, rs = m.sb("stats", [P, 2, 6]), m.sb("mv", [P, 2]), m.sb("sd", [P, 2]), m.sb("rs", [P, 1])
        ident = m.sb("ident", [P, P])
        ps_m, ps_y, ps_t = m.ps("ps_m", [P, KD, P]), m.ps("ps_y", [P, 2, D]), m.ps("ps_t", [P, KD, P])

        zero_done, ident_done = m.sem("zero_done"), m.sem("ident_done")
        w_loaded = [m.sem("w_loaded0"), m.sem("w_loaded1")]
        w_hi_done, w_lo_done, vec_loaded = m.sem("w_hi_done"), m.sem("w_lo_done"), m.sem("vec_loaded")
        mx_loaded, x_loaded = [m.sem("mx_loaded0"), m.sem("mx_loaded1")], [m.sem("x_loaded0"), m.sem("x_loaded1")]
        sq_done, ms_done, rms_done, inv_done, scaled, mx_done = (m.sem("sq_done"), m.sem("ms_done"), m.sem("rms_done"),
                                                                 m.sem("inv_done"), m.sem("scaled"), m.sem("mx_done"))
        m_turned, m_hi_done, m_lo_done, mm_done = m.sem("m_turned"), m.sem("m_hi_done"), m.sem("m_lo_done"), m.sem("mm_done")
        sum_done, bn_done, aggr_done, var_done, sd_done = (m.sem("sum_done"), m.sem("bn_done"), m.sem("aggr_done"), m.sem("var_done"),
                                                           m.sem("sd_done"))
        rs_done, xhat_done, gain_done, y_done = m.sem("rs_done"), m.sem("xhat_done"), m.sem("gain_done"), m.sem("y_done")
        y_turned, y_hi_done, y_lo_done = m.sem("y_turned"), m.sem("y_hi_done"), m.sem("y_lo_done")
        y_stored, yt_stored = [m.sem("y_stored0"), m.sem("y_stored1")], [m.sem("yt_stored0"), m.sem("yt_stored1")]

        def tiles(eng, step):
            step(0, 0, 0)
            step(1, 1, 0)
            with eng.Fori(1, 7) as i:
                step(2 * i, 0, i)
                step(2 * i + 1, 1, i)
            for t in (14, 15, 16):
                step(t, t % 2, t // 2)

        def early(t):
            return isinstance(t, int) and t < 2

        def exists(t, ahead):
            return not isinstance(t, int) or t + ahead <= NT

        with nc.Block() as block:
            @block.sync
            def _(sp):
                def load_mx(t, p):
                    n = n_rows(t)
                    if not early(t):
                        sp.wait_ge(m_turned, t - 1)
                    alone(sp) if not early(t) else None
                    sp.dma_start(mx[:n, p, :], d["mixed"][tile_rows(t), :]).then_inc(mx_loaded[p], 16)

                def load_x(t, p):
                    n = n_rows(t)
                    if not early(t):
                        sp.wait_ge(sum_done, t - 1)
                    alone(sp) if not early(t) else None
                    sp.dma_start(x[:n, p, :], d["x_rows"][tile_rows(t), :]).then_inc(x_loaded[p], 16)

                load_mx(0, 0)
                load_mx(1, 1)
                for k in range(KD):
                    if k >= 2:
                        sp.wait_ge(w_hi_done, k - 1)
                        sp.wait_ge(w_lo_done, k - 1)
                    sp.dma_start(w_raw[:, k % 2, :], d["w_out"][k * P:(k + 1) * P, :]).then_inc(w_loaded[k % 2], 16)
                load_x(0, 0)
                load_x(1, 1)

                def step(t, p, i):
                    if exists(t, 2):
                        load_mx(t + 2, p)
                    if exists(t, 2):
                        load_x(t + 2, p)
                tiles(sp, step)

            @block.gpsimd
            def _(pool):
                make_identity(pool, ident, zero_done, ident_done)
                pool.dma_start(g_mix[:], bc_row(d["mix_norm_g"], D)).then_inc(vec_loaded, 16)
                pool.dma_start(g_ln[:], bc_row(d["ln1_g"], D)).then_inc(vec_loaded, 16)
                pool.dma_start(b_ln[:], bc_row(d["ln1_b"], D)).then_inc(vec_loaded, 16)
                pool.wait_ge(vec_loaded, 48)

                def gain_mx(t, p):
                    n = n_rows(t)
                    pool.wait_ge(scaled, t + 1)
                    pool.tensor_tensor(mx[:n, p, :], mx[:n, p, :], g_mix[:n, :], ALU.mult).then_inc(mx_done, 1)

                def store_yt(t, p):
                    n = n_rows(t)
                    pool.wait_ge(y_hi_done, t + 1)
                    alone(pool)
                    pool.dma_start(d["x1t_hi"][:, :, tile_rows(t)], yt_hi[:, p, :, :n].bitcast(F32)).then_inc(yt_stored[p], 16)
                    pool.wait_ge(y_lo_done, t + 1)
                    alone(pool)
                    pool.dma_start(d["x1t_lo"][:, :, tile_rows(t)], yt_lo[:, p, :, :n].bitcast(F32)).then_inc(yt_stored[p], 16)

                gain_mx(0, 0)
                gain_mx(1, 1)

                def step(t, p, i):
                    n = n_rows(t)
                    if exists(t, 2):
                        gain_mx(t + 2, p)
                    pool.wait_ge(xhat_done, t + 1)
                    pool.tensor_tensor(y[:n, p, :], y[:n, p, :], g_ln[:n, :], ALU.mult).then_inc(gain_done, 1)
                    pool.wait_ge(gain_done, t + 1)
                    pool.tensor_tensor(y[:n, p, :], y[:n, p, :], b_ln[:n, :], ALU.add).then_inc(y_done, 1)
                    pool.wait_ge(y_done, t + 1)
                    alone(pool)
                    pool.dma_start(d["x1_rows"][tile_rows(t), :], y[:n, p, :]).then_inc(y_stored[p], 16)
                    if not (isinstance(t, int) and t == 0):
                        store_yt(t - 1, 1 - p)
                tiles(pool, step)
                store_yt(NT, 0)
                for p, count in ((0, 9), (1, 8)):
                    pool.wait_ge(y_stored[p], 16 * count)
                    pool.wait_ge(yt_stored[p], 32 * count)

            @block.scalar
            def _(act):
                def squares(t, p, i):
                    n = n_rows(t)
                    act.wait_ge(mx_loaded[p], 16 * (i + 1))
                    for s, (c, w) in enumerate(segs):
                        last = act.activation(sq[:n, c:c + w], mx[:n, p, c:c + w], ACT.Square, accum_out=ss[:n, s:s + 1])
                    last.then_inc(sq_done, 1)
                    act.wait_ge(ms_done, t + 1)
                    act.activation(rms[:n, :], ss[:n, :], ACT.Sqrt).then_inc(rms_done, 1)

                def hi_m(t, p):
                    n = n_rows(t)
                    act.wait_ge(m_turned, t + 1)
                    if not early(t):
                        act.wait_ge(mm_done, t - 1)
                    act.copy(mt_hi[:, p, :, :n], ps_m[:, :, :n]).then_inc(m_hi_done, 1)

                def hi_y(t, p, i):
                    n = n_rows(t)
                    act.wait_ge(y_turned, t + 1)
                    if not early(t):
                        act.wait_ge(yt_stored[p], 32 * i)
                    act.copy(yt_hi[:, p, :, :n], ps_t[:, :, :n]).then_inc(y_hi_done, 1)

                squares(0, 0, 0)
                for k in range(KD):
                    act.wait_ge(w_loaded[k % 2], 16 * (k // 2 + 1))
                    act.copy(w_hi[:, k, :], w_raw[:, k % 2, :]).then_inc(w_hi_done, 1)
                hi_m(0, 0)
                squares(1, 1, 0)

                def step(t, p, i):
                    n = n_rows(t)
                    if exists(t, 1):
                        hi_m(t + 1, 1 - p)
                    if exists(t, 2):
                        squares(t + 2, p, i + 1)
                    act.wait_ge(var_done, t + 1)
                    act.activation(sd[:n, 1:2], sd[:n, 0:1], ACT.Sqrt).then_inc(sd_done, 1)
                    if not (isinstance(t, int) and t == 0):
                        hi_y(t - 1, 1 - p, i - 1 + p)
                tiles(act, step)
                hi_y(NT, 0, NT // 2)

            @block.vector
            def _(dve):
                def scale(t, p):
                    n = n_rows(t)
                    dve.wait_ge(sq_done, t + 1)
                    dve.tensor_scalar(ss[:n, 0:2], ss[:n, 0:2], 1.0 / AW, EPS, ALU.mult, ALU.add)
                    dve.tensor_scalar(ss[:n, 2:3], ss[:n, 2:3], 1.0 / CW, EPS, ALU.mult, ALU.add).then_inc(ms_done, 1)
                    dve.wait_ge(rms_done, t + 1)
                    dve.reciprocal(inv[:n, :], rms[:n, :]).then_inc(inv_done, 1)
                    dve.wait_ge(inv_done, t + 1)
                    for s, (c, w) in enumerate(segs):
                        last = dve.tensor_scalar(mx[:n, p, c:c + w], mx[:n, p, c:c + w], inv[:n, s:s + 1], None, ALU.mult)
                    last.then_inc(scaled, 1)

                def lo_m(t, p):
                    n = n_rows(t)
                    dve.wait_ge(m_hi_done, t + 1)
                    dve.tensor_tensor(mt_lo[:, p, :, :n], ps_m[:, :, :n], mt_hi[:, p, :, :n].bitcast(F32),
                                      ALU.subtract).then_inc(m_lo_done, 1)

                def lo_y(t, p):
                    n = n_rows(t)
                    dve.wait_ge(y_hi_done, t + 1)
                    dve.tensor_tensor(yt_lo[:, p, :, :n], ps_t[:, :, :n], yt_hi[:, p, :, :n].bitcast(F32),
                                      ALU.subtract).then_inc(y_lo_done, 1)

                scale(0, 0)
                for k in range(KD):
                    dve.wait_ge(w_hi_done, k + 1)
                    dve.tensor_tensor(w_lo[:, k, :], w_raw[:, k % 2, :], w_hi[:, k, :].bitcast(F32),
                                      ALU.subtract).then_inc(w_lo_done, 1)
                lo_m(0, 0)
                scale(1, 1)

                def step(t, p, i):
                    n = n_rows(t)
                    if exists(t, 1):
                        lo_m(t + 1, 1 - p)
                    if exists(t, 2):
                        scale(t + 2, p)
                    dve.wait_ge(x_loaded[p], 16 * (i + 1))
                    dve.wait_ge(mm_done, t + 1)
                    if not early(t):
                        dve.wait_ge(y_stored[p], 16 * i)
                        dve.wait_ge(y_turned, t - 1)
                    dve.scalar_tensor_tensor(out=y[:n, p, :], in0=x[:n, p, :], scalar=ALPHA, in1=ps_y[:n, p, :],
                                             op0=ALU.mult, op1=ALU.add).then_inc(sum_done, 1)
                    dve.wait_ge(sum_done, t + 1)
                    for c in range(2):
                        last = dve.bn_stats(stats[:n, c, :], y[:n, p, c * 512:(c + 1) * 512])
                    last.then_inc(bn_done, 1)
                    dve.wait_ge(bn_done, t + 1)
                    alone(dve)
                    dve.bn_aggr(mv[:n, :], stats[:n].rearrange("p a b -> p (a b)")).then_inc(aggr_done, 1)
                    dve.wait_ge(aggr_done, t + 1)
                    dve.tensor_scalar(sd[:n, 0:1], mv[:n, 1:2], EPS, None, ALU.add).then_inc(var_done, 1)
                    dve.wait_ge(sd_done, t + 1)
                    dve.reciprocal(rs[:n, :], sd[:n, 1:2]).then_inc(rs_done, 1)
                    dve.wait_ge(rs_done, t + 1)
                    dve.tensor_scalar(y[:n, p, :], y[:n, p, :], mv[:n, 0:1], rs[:n, :], ALU.subtract,
                                      ALU.mult).then_inc(xhat_done, 1)
                    if not (isinstance(t, int) and t == 0):
                        lo_y(t - 1, 1 - p)
                tiles(dve, step)
                lo_y(NT, 0)

            @block.tensor
            def _(pe):
                pe.wait_ge(ident_done, 1)

                def turn_m(t, p):
                    n = n_rows(t)
                    pe.wait_ge(mx_done, t + 1)
                    wait_if(pe, m_lo_done, t)
                    for k in range(KD):
                        last = pe.transpose(ps_m[:, k, :n], mx[:n, p, k * P:(k + 1) * P], ident[:n, :n])
                    last.then_inc(m_turned, 1)

                def turn_y(t, p):
                    n = n_rows(t)
                    pe.wait_ge(y_done, t + 1)
                    wait_if(pe, y_lo_done, t)
                    for k in range(KD):
                        last = pe.transpose(ps_t[:, k, :n], y[:n, p, k * P:(k + 1) * P], ident[:n, :n])
                    last.then_inc(y_turned, 1)

                turn_m(0, 0)

                def step(t, p, i):
                    n = n_rows(t)
                    if exists(t, 1):
                        turn_m(t + 1, 1 - p)
                    pe.wait_ge(m_lo_done, t + 1)
                    if not early(t):
                        pe.wait_ge(sum_done, t - 1)
                    for c in range(0, D, 512):
                        for k in range(KD):
                            if isinstance(t, int) and t == 0 and c == 0:
                                pe.wait_ge(w_lo_done, k + 1)
                            last = products(pe, ps_y[:n, p, c:c + 512], mt_hi[:, p, k, :n], mt_lo[:, p, k, :n],
                                            w_hi[:, k, c:c + 512], w_lo[:, k, c:c + 512], k == 0, k == KD - 1)
                    last.then_inc(mm_done, 1)
                    if not (isinstance(t, int) and t == 0):
                        turn_y(t - 1, 1 - p)
                tiles(pe, step)
                turn_y(NT, 0)


def ffn_up(nc, d):
    with nc.cleanup_on_exit(), ExitStack() as ctx:
        m = Stage(nc, ctx, "fu")
        H = 2
        GW = 424
        NG = -(-ROWS // GW)
        REST = SEQ - (NG - 1) * GW
        LASTW = REST + NSMP
        U = 2 * NG
        MT = 2 * KF
        xt_hi, xt_lo = m.sb("xt_hi", [P, KD, H + ROWS], F32R), m.sb("xt_lo", [P, KD, H + ROWS], F32R)
        w_raw = m.sb("w_raw", [P, 2, KD, P])
        w_hi, w_lo = m.sb("w_hi", [P, 2, KD, P], F32R), m.sb("w_lo", [P, 2, KD, P], F32R)
        vec_rows, vecs = m.sb("vec_rows", [2 * MT, 3, P]), m.sb("vecs", [P, 6, MT])
        smp = m.sb("smp", [P, 2, H + NSMP])
        conv = m.sb("conv", [P, 2, GW])
        gate, h = m.sb("gate", [P, NG, GW]), m.sb("h", [P, 2, GW])
        states, states_t = m.sb("states", [P, 4, MT]), m.sb("states_t", [2 * MT, 2, P])
        ident = m.sb("ident", [P, P])
        ps_y = m.ps("ps_y", [P, 8, 512])

        zero_done, ident_done = m.sem("zero_done"), m.sem("ident_done")
        vec_loaded, vec_turned, vec_done, edge_done = m.sem("vec_loaded"), m.sem("vec_turned"), m.sem("vec_done"), m.sem("edge_done")
        xt_loaded = [m.sem(f"xt_loaded{g}") for g in range(NG)]
        w_loaded = [m.sem("w_loaded0"), m.sem("w_loaded1")]
        w_hi_done, w_lo_done = m.sem("w_hi_done"), m.sem("w_lo_done")
        mm_done, smp_done, tap0_done, smp_in_done, tap1_done, conv_done, gate_done, h_done = (
            m.sem("mm_done"), m.sem("smp_done"), m.sem("tap0_done"), m.sem("smp_in_done"), m.sem("tap1_done"), m.sem("conv_done"),
            m.sem("gate_done"), m.sem("h_done"))
        h_stored = [m.sem("h_stored0"), m.sem("h_stored1")]
        states_turned, states_done, states_stored = m.sem("states_turned"), m.sem("states_done"), m.sem("states_stored")

        def pairs(eng, step):
            step(0)
            with eng.Fori(1, KF) as j:
                step(j)

        def one(a, m_):
            return a[:, m_:m_ + 1] if isinstance(m_, int) else a[:, bass.ds(m_, 1)]

        def gwidth(g):
            return LASTW if g == NG - 1 else GW

        def stored_before(j, g):
            return ((NG + 1) // 2 if g % 2 == 0 else NG // 2) * j + g // 2

        with nc.Block() as block:
            @block.sync
            def _(sp):
                def load_w(j, half):
                    c = (j * P if isinstance(j, int) else j * P) + half * DFF
                    cols = slice(c, c + P) if isinstance(c, int) else bass.ds(c, P)
                    sp.dma_start(w_raw[:, half], d["ffn_w_in"][:, cols].rearrange("(k p) c -> p k c", p=P)).then_inc(w_loaded[half], 16)

                def load_xt(g):
                    c = slice(g * GW, g * GW + gwidth(g))
                    to = slice(H + g * GW, H + g * GW + gwidth(g))
                    sp.dma_start(xt_hi[:, :, to].bitcast(F32), d["x1t_hi"][:, :, c]).then_inc(xt_loaded[g], 16)
                    sp.dma_start(xt_lo[:, :, to].bitcast(F32), d["x1t_lo"][:, :, c]).then_inc(xt_loaded[g], 16)

                load_w(0, 0)
                load_xt(0)
                taps = d["ffn_conv_w"].rearrange("c (m p) -> (c m) p", p=P)
                sp.dma_start(vec_rows[:, 0, :], taps[0:2 * MT, :]).then_inc(vec_loaded, 16)
                sp.dma_start(vec_rows[0:MT, 1, :], taps[2 * MT:3 * MT, :]).then_inc(vec_loaded, 16)
                sp.dma_start(vec_rows[MT:2 * MT, 1, :], d["ffn_conv_b"].rearrange("(m p) -> m p", p=P)).then_inc(vec_loaded, 16)
                sp.dma_start(vec_rows[:, 2, :], d["state_ffn_conv"].rearrange("c (m p) -> (c m) p", p=P)).then_inc(vec_loaded, 16)
                load_w(0, 1)
                for g in range(1, NG):
                    load_xt(g)

                def step(j):
                    if isinstance(j, int):
                        for half in range(2):
                            sp.wait_ge(w_hi_done, half + 1)
                            sp.wait_ge(w_lo_done, half + 1)
                            load_w(j + 1, half)
                step(0)
                with sp.Fori(1, KF - 1) as j:
                    for half in range(2):
                        sp.wait_ge(w_hi_done, 2 * j + half + 1)
                        sp.wait_ge(w_lo_done, 2 * j + half + 1)
                        alone(sp)
                        load_w(j + 1, half)
                sp.wait_ge(states_done, 2)
                sp.dma_start(d["prompt_ffn_conv"].rearrange("c (m p) -> (c m) p", p=P), states_t[:, 0, :]).then_inc(states_stored, 16)
                sp.dma_start(d["sample_ffn_conv"].rearrange("c (m p) -> (c m) p", p=P), states_t[:, 1, :]).then_inc(states_stored, 16)
                sp.wait_ge(states_stored, 32)

            @block.gpsimd
            def _(pool):
                pool.memset(xt_hi[:, :, 0:H].bitcast(F32), 0.0)
                pool.memset(xt_lo[:, :, 0:H].bitcast(F32), 0.0).then_inc(edge_done, 1)
                make_identity(pool, ident, zero_done, ident_done)

                def step(j):
                    for g in range(NG):
                        n = gwidth(g)
                        pool.wait_ge(conv_done, U * j + NG + g + 1)
                        pool.wait_ge(gate_done, NG * j + g + 1)
                        if not (isinstance(j, int) and g < 2):
                            pool.wait_ge(h_stored[g % 2], 16 * stored_before(j, g))
                        v = NG + g
                        pool.tensor_tensor(h[:, g % 2, :n], conv[:, v % 2, :n], gate[:, g, :n], ALU.mult).then_inc(h_done, 1)
                        pool.wait_ge(h_done, NG * j + g + 1)
                        alone(pool)
                        k = slice(j, j + 1) if isinstance(j, int) else bass.ds(j, 1)
                        pool.dma_start(d["h_t"][:, k, g * GW:g * GW + n].rearrange("p a c -> p (a c)"),
                                       h[:, g % 2, :n]).then_inc(h_stored[g % 2], 16)
                pairs(pool, step)
                pool.wait_ge(h_stored[0], 16 * stored_before(KF, 0))
                pool.wait_ge(h_stored[1], 16 * stored_before(KF, 1))

            @block.scalar
            def _(act):
                def split_hi(j, half):
                    act.wait_ge(w_loaded[half], 16 * (j + 1))
                    wait_if(act, mm_done, U * (j - 1) + NG * (half + 1))
                    act.copy(w_hi[:, half], w_raw[:, half]).then_inc(w_hi_done, 1)

                split_hi(0, 0)
                act.wait_ge(vec_turned, 1)
                act.copy(vecs[:].rearrange("p a b -> p (a b)"), ps_y[:, 0, 0:6 * MT]).then_inc(vec_done, 1)
                act.wait_ge(vec_done, 1)
                split_hi(0, 1)

                def step(j):
                    for v in range(U):
                        half, g = v // NG, v % NG
                        u = U * j + v
                        mt = j + half * KF
                        n = REST if g == NG - 1 else GW
                        act.wait_ge(mm_done, u + 1)
                        if v >= NG:
                            if v - NG >= 2:
                                act.wait_ge(h_done, NG * j + v - NG - 1)
                        elif v < 2:
                            wait_if(act, h_done, NG * j - 1 + v)
                        if 2 <= v < NG + 2:
                            act.wait_ge(gate_done, NG * j + v - 1)
                        if g == NG - 1:
                            act.copy(smp[:, half, H:], ps_y[:, v % 8, H + REST:H + LASTW])
                            last2 = ps_y[:, v % 8, REST:REST + 2 * NSMP].rearrange("p (a b) -> p a b", b=NSMP)[:, :, 0:2]
                            act.copy(one_state(mt), last2).then_inc(smp_done, 1)
                        alone(act)
                        act.activation(conv[:, v % 2, :n], ps_y[:, v % 8, 0:n], ACT.Identity,
                                       bias=one(vecs[:, 3, :], mt), scale=one(vecs[:, 0, :], mt)).then_inc(tap0_done, 1)
                        if half == 0:
                            act.wait_ge(conv_done, u + 1)
                            wait_if(act, h_done, NG * (j - 1) + g + 1)
                            act.activation(gate[:, g, :gwidth(g)], conv[:, v % 2, :gwidth(g)], ACT.Silu).then_inc(gate_done, 1)
                        if v in (NG, U - 1):
                            nxt(j, 0 if v == NG else 1)

                def one_state(mt):
                    a = states[:, :, mt:mt + 1] if isinstance(mt, int) else states[:, :, bass.ds(mt, 1)]
                    return a.rearrange("p (x y) b -> p x (y b)", x=2)

                def nxt(j, half):
                    if peel[0]:
                        return
                    split_hi(j + 1, half)

                peel = [False]
                step(0)
                with act.Fori(1, KF - 1) as j:
                    step(j)
                peel[0] = True
                step(KF - 1)
                act.wait_ge(states_turned, 1)
                act.copy(states_t[:, 0, :], ps_y[0:2 * MT, 0, 0:P]).then_inc(states_done, 1)
                act.copy(states_t[:, 1, :], ps_y[0:2 * MT, 0, P:2 * P]).then_inc(states_done, 1)

            @block.vector
            def _(dve):
                def split_lo(j, half):
                    dve.wait_ge(w_hi_done, 2 * j + half + 1)
                    dve.tensor_tensor(w_lo[:, half], w_raw[:, half], w_hi[:, half].bitcast(F32), ALU.subtract).then_inc(w_lo_done, 1)

                split_lo(0, 0)
                split_lo(0, 1)
                dve.wait_ge(vec_done, 1)

                def step(j, more):
                    for v in range(U):
                        half, g = v // NG, v % NG
                        u = U * j + v
                        mt = j + half * KF
                        n = REST if g == NG - 1 else GW
                        c, y = conv[:, v % 2], ps_y[:, v % 8]
                        w0, w1, w2, b = (one(vecs[:, e, :], mt) for e in (0, 1, 2, 3))
                        dve.wait_ge(tap0_done, u + 1)
                        if g == NG - 1:
                            dve.wait_ge(smp_done, 2 * j + half + 1)
                            s = smp[:, half]
                            m_ = slice(mt, mt + 1) if isinstance(mt, int) else bass.ds(mt, 1)
                            dve.tensor_copy(s[:, 0:H], vecs[:, 4:6, m_].rearrange("p a b -> p (a b)")).then_inc(smp_in_done, 1)
                            dve.wait_ge(smp_in_done, 4 * (2 * j + half) + 1)
                            cs = c[:, REST:LASTW]
                            dve.tensor_scalar(cs, s[:, 0:NSMP], w0, b, ALU.mult, ALU.add).then_inc(smp_in_done, 1)
                            dve.wait_ge(smp_in_done, 4 * (2 * j + half) + 2)
                            dve.scalar_tensor_tensor(out=cs, in0=s[:, 1:1 + NSMP], scalar=w1, in1=cs, op0=ALU.mult,
                                                     op1=ALU.add).then_inc(smp_in_done, 1)
                            dve.wait_ge(smp_in_done, 4 * (2 * j + half) + 3)
                            dve.scalar_tensor_tensor(out=cs, in0=s[:, 2:2 + NSMP], scalar=w2, in1=cs, op0=ALU.mult,
                                                     op1=ALU.add).then_inc(smp_in_done, 1)
                        dve.scalar_tensor_tensor(out=c[:, :n], in0=y[:, 1:1 + n], scalar=w1, in1=c[:, :n], op0=ALU.mult,
                                                 op1=ALU.add).then_inc(tap1_done, 1)
                        dve.wait_ge(tap1_done, u + 1)
                        dve.scalar_tensor_tensor(out=c[:, :n], in0=y[:, 2:2 + n], scalar=w2, in1=c[:, :n], op0=ALU.mult,
                                                 op1=ALU.add).then_inc(conv_done, 1)
                        if more and v in (NG, U - 1):
                            split_lo(j + 1, 0 if v == NG else 1)
                step(0, True)
                with dve.Fori(1, KF - 1) as j:
                    step(j, True)
                step(KF - 1, False)

            @block.tensor
            def _(pe):
                pe.wait_ge(ident_done, 1)
                pe.wait_ge(vec_loaded, 64)
                for e in range(3):
                    last = pe.transpose(ps_y[:, 0, 2 * MT * e:2 * MT * (e + 1)], vec_rows[:, e, :], ident[0:2 * MT, 0:2 * MT])
                last.then_inc(vec_turned, 1)
                pe.wait_ge(vec_done, 1)
                pe.wait_ge(edge_done, 1)

                def step(j):
                    for v in range(U):
                        half, g = v // NG, v % NG
                        if isinstance(j, int) and j == 0 and half == 0:
                            pe.wait_ge(xt_loaded[g], 32)
                        if g == 0:
                            pe.wait_ge(w_lo_done, 2 * j + half + 1)
                        wait_if(pe, conv_done, U * j + v - 1)
                        n = H + gwidth(g)
                        for k in range(KD):
                            last = products(pe, ps_y[:, v % 8, :n], w_hi[:, half, k, :], w_lo[:, half, k, :],
                                            xt_hi[:, k, g * GW:g * GW + n], xt_lo[:, k, g * GW:g * GW + n],
                                            k == 0, k == KD - 1)
                        last.then_inc(mm_done, 1)
                pairs(pe, step)
                pe.wait_ge(conv_done, U * KF)
                for e in range(2):
                    last = pe.transpose(ps_y[0:2 * MT, 0, e * P:(e + 1) * P],
                                        states[:, 2 * e:2 * e + 2, :].rearrange("p a b -> p (a b)"), ident[:])
                last.then_inc(states_turned, 1)


def ffn_down(nc, d):
    with nc.cleanup_on_exit(), ExitStack() as ctx:
        m = Stage(nc, ctx, "fd")
        PK = 2
        NPC = KF // PK
        RING = 4
        w_hi, w_lo = m.sb("w_hi", [P, KF, D], F32R), m.sb("w_lo", [P, KF, D], F32R)
        h_raw = m.sb("h_raw", [P, RING, PK, P])
        h_hi, h_lo = m.sb("h_hi", [P, RING, PK, P], F32R), m.sb("h_lo", [P, RING, PK, P], F32R)
        y = m.sb("y", [P, 2, D])
        g_ln, b_ln = m.sb("g_ln", [P, D]), m.sb("b_ln", [P, D])
        stats, mv, sd, rs = m.sb("stats", [P, 2, 6]), m.sb("mv", [P, 2]), m.sb("sd", [P, 2]), m.sb("rs", [P, 1])
        ps_y = m.ps("ps_y", [P, 2, D])

        w_loaded = [m.sem("w_loaded0"), m.sem("w_loaded1")]
        w_hi_done, w_lo_done, vec_loaded = m.sem("w_hi_done"), m.sem("w_lo_done"), m.sem("vec_loaded")
        h_loaded = [m.sem(f"h_loaded{s}") for s in range(RING)]
        x_loaded = [m.sem("x_loaded0"), m.sem("x_loaded1")]
        h_hi_done, h_lo_done, piece_done = m.sem("h_hi_done"), m.sem("h_lo_done"), m.sem("piece_done")
        sum_done, bn_done, aggr_done, var_done, sd_done = (m.sem("sum_done"), m.sem("bn_done"), m.sem("aggr_done"), m.sem("var_done"),
                                                           m.sem("sd_done"))
        rs_done, xhat_done, gain_done, y_done = m.sem("rs_done"), m.sem("xhat_done"), m.sem("gain_done"), m.sem("y_done")
        y_stored = [m.sem("y_stored0"), m.sem("y_stored1")]

        def tiles(eng, step):
            step(0, 0, 0)
            step(1, 1, 0)
            with eng.Fori(1, NT // 2) as i:
                step(2 * i, 0, i)
                step(2 * i + 1, 1, i)
            step(NT, 0, NT // 2)

        def slot_loads(t, c):
            a_tile = len(range(c % RING, NPC, RING))
            return a_tile * t + c // RING + 1

        with nc.Block() as block:
            @block.sync
            def _(sp):
                for k in range(KF):
                    if k >= 2:
                        sp.wait_ge(w_hi_done, k - 1)
                        sp.wait_ge(w_lo_done, k - 1)
                    sp.dma_start(y[:, k % 2, :], d["ffn_w_out"][k * P:(k + 1) * P, :]).then_inc(w_loaded[k % 2], 16)
                sp.wait_ge(w_lo_done, KF)

                def step(t, p, i):
                    n = n_rows(t)
                    if not (isinstance(t, int) and t < 2):
                        sp.wait_ge(y_stored[p], 16 * i)
                    alone(sp)
                    sp.dma_start(y[:n, p, :], d["x1_rows"][tile_rows(t), :]).then_inc(x_loaded[p], 16)
                tiles(sp, step)

            @block.gpsimd
            def _(pool):
                pool.dma_start(g_ln[:], bc_row(d["ln2_g"], D)).then_inc(vec_loaded, 16)
                pool.dma_start(b_ln[:], bc_row(d["ln2_b"], D)).then_inc(vec_loaded, 16)

                def load_piece(t, c):
                    n = n_rows(t)
                    wait_if(pool, h_lo_done, NPC * t + c - 2)
                    alone(pool) if not isinstance(t, int) else None
                    pool.dma_start(h_raw[:, c % RING, :, :n], d["h_t"][:, PK * c:PK * (c + 1), tile_rows(t)]).then_inc(h_loaded[c % RING], 16)

                def finish(t, p):
                    n = n_rows(t)
                    pool.wait_ge(xhat_done, t + 1)
                    pool.tensor_tensor(y[:n, p, :], y[:n, p, :], g_ln[:n, :], ALU.mult).then_inc(gain_done, 1)
                    pool.wait_ge(gain_done, t + 1)
                    pool.tensor_tensor(y[:n, p, :], y[:n, p, :], b_ln[:n, :], ALU.add).then_inc(y_done, 1)
                    pool.wait_ge(y_done, t + 1)
                    alone(pool)
                    if isinstance(t, int) and t == NT:
                        pool.dma_start(d["y_sample"], y[:n, p, :]).then_inc(y_stored[p], 16)
                    else:
                        pool.dma_start(d["y_prompt"][tile_rows(t), :], y[:n, p, :]).then_inc(y_stored[p], 16)

                def step(t, p, i):
                    for c in range(NPC):
                        load_piece(t, c)
                        if c == NPC - 3 and not (isinstance(t, int) and t == 0):
                            finish(t - 1, 1 - p)
                    if isinstance(t, int) and t == 0:
                        pool.wait_ge(vec_loaded, 32)
                tiles(pool, step)
                finish(NT, 0)
                pool.wait_ge(y_stored[0], 16 * 9)
                pool.wait_ge(y_stored[1], 16 * 8)

            @block.scalar
            def _(act):
                def hi(t, c):
                    n = n_rows(t)
                    act.wait_ge(h_loaded[c % RING], 16 * slot_loads(t, c))
                    wait_if(act, piece_done, NPC * t + c - 2)
                    act.copy(h_hi[:, c % RING, :, :n], h_raw[:, c % RING, :, :n]).then_inc(h_hi_done, 1)

                def split_w(k):
                    act.wait_ge(w_loaded[k % 2], 16 * (k // 2 + 1))
                    act.copy(w_hi[:, k, :], y[:, k % 2, :]).then_inc(w_hi_done, 1)

                def step(t, p, i):
                    n = n_rows(t)
                    for c in range(NPC):
                        if isinstance(t, int) and t == 0:
                            split_w(2 * c)
                            split_w(2 * c + 1)
                        hi(t, c)
                        if c == 4 and not (isinstance(t, int) and t == 0):
                            root(t - 1)

                def root(t):
                    n = n_rows(t)
                    act.wait_ge(var_done, t + 1)
                    act.activation(sd[:n, 1:2], sd[:n, 0:1], ACT.Sqrt).then_inc(sd_done, 1)
                tiles(act, step)
                root(NT)

            @block.vector
            def _(dve):
                def lo(t, c):
                    n = n_rows(t)
                    dve.wait_ge(h_hi_done, NPC * t + c + 1)
                    dve.tensor_tensor(h_lo[:, c % RING, :, :n], h_raw[:, c % RING, :, :n], h_hi[:, c % RING, :, :n].bitcast(F32),
                                      ALU.subtract).then_inc(h_lo_done, 1)

                def norm(t, p, i):
                    n = n_rows(t)
                    dve.wait_ge(x_loaded[p], 16 * (i + 1))
                    dve.wait_ge(piece_done, NPC * (t + 1))
                    dve.scalar_tensor_tensor(out=y[:n, p, :], in0=y[:n, p, :], scalar=ALPHA, in1=ps_y[:n, p, :],
                                             op0=ALU.mult, op1=ALU.add).then_inc(sum_done, 1)
                    dve.wait_ge(sum_done, t + 1)
                    for c in range(2):
                        last = dve.bn_stats(stats[:n, c, :], y[:n, p, c * 512:(c + 1) * 512])
                    last.then_inc(bn_done, 1)
                    dve.wait_ge(bn_done, t + 1)
                    alone(dve)
                    dve.bn_aggr(mv[:n, :], stats[:n].rearrange("p a b -> p (a b)")).then_inc(aggr_done, 1)
                    dve.wait_ge(aggr_done, t + 1)
                    dve.tensor_scalar(sd[:n, 0:1], mv[:n, 1:2], EPS, None, ALU.add).then_inc(var_done, 1)

                def finish(t, p):
                    n = n_rows(t)
                    dve.wait_ge(sd_done, t + 1)
                    dve.reciprocal(rs[:n, :], sd[:n, 1:2]).then_inc(rs_done, 1)
                    dve.wait_ge(rs_done, t + 1)
                    dve.tensor_scalar(y[:n, p, :], y[:n, p, :], mv[:n, 0:1], rs[:n, :], ALU.subtract,
                                      ALU.mult).then_inc(xhat_done, 1)

                def step(t, p, i):
                    for c in range(NPC):
                        if isinstance(t, int) and t == 0:
                            for k in (2 * c, 2 * c + 1):
                                dve.wait_ge(w_hi_done, k + 1)
                                dve.tensor_tensor(w_lo[:, k, :], y[:, k % 2, :], w_hi[:, k, :].bitcast(F32),
                                                  ALU.subtract).then_inc(w_lo_done, 1)
                        lo(t, c)
                        if not (isinstance(t, int) and t == 0):
                            if c == 2:
                                norm(t - 1, 1 - p, i - 1 + p)
                            if c == 5:
                                finish(t - 1, 1 - p)
                tiles(dve, step)
                norm(NT, 0, NT // 2)
                finish(NT, 0)

            @block.tensor
            def _(pe):
                def step(t, p, i):
                    n = n_rows(t)
                    if not (isinstance(t, int) and t < 2):
                        pe.wait_ge(sum_done, t - 1)
                    for c in range(NPC):
                        if isinstance(t, int) and t == 0:
                            pe.wait_ge(w_lo_done, PK * (c + 1))
                        pe.wait_ge(h_lo_done, NPC * t + c + 1)
                        for e in range(PK):
                            k = PK * c + e
                            for col in range(0, D, 512):
                                last = products(pe, ps_y[:n, p, col:col + 512], h_hi[:, c % RING, e, :n], h_lo[:, c % RING, e, :n],
                                                w_hi[:, k, col:col + 512], w_lo[:, k, col:col + 512], k == 0, k == KF - 1)
                        last.then_inc(piece_done, 1)
                tiles(pe, step)


INPUTS = [
    ("x_prompt", (SEQ, D)), ("x_sample", (NSMP, D)), ("cache_k", (CACHE, AW)), ("cache_v", (CACHE, AW)),
    ("state_ssm", (AW, STATE)), ("state_ssm_conv", (3, XBC)), ("state_ffn_conv", (2, 2 * DFF)),
    ("ln_in_g", (D,)), ("ln_in_b", (D,)), ("w_in", (D, N_IN)), ("rel_bias", (HEADS, REL)),
    ("ssm_conv_w", (4, XBC)), ("ssm_conv_b", (XBC,)), ("ssm_dt_bias", (HEADS,)), ("ssm_a_log", (HEADS,)), ("ssm_d", (HEADS,)),
    ("gmlp_w", (CG, P, P)), ("gmlp_b", (CG, P)), ("mix_norm_g", (D,)), ("w_out", (D, D)), ("ln1_g", (D,)), ("ln1_b", (D,)),
    ("ffn_w_in", (D, 2 * DFF)), ("ffn_conv_w", (3, 2 * DFF)), ("ffn_conv_b", (2 * DFF,)), ("ffn_w_out", (DFF, D)),
    ("ln2_g", (D,)), ("ln2_b", (D,)),
]
ARGUMENT = {"cache_k": "cache_attn_k", "cache_v": "cache_attn_v", "rel_bias": "attn_rel_bias"}
OUTPUTS = [
    ("y_prompt", (SEQ, D), (1, SEQ, D)), ("y_sample", (NSMP, D), (1, NSMP, D)),
    ("prompt_k", (CACHE, AW), (1, 1, CACHE, HEADS, HD)), ("prompt_v", (CACHE, AW), (1, 1, CACHE, HEADS, HD)),
    ("prompt_ssm", (AW, STATE), (1, 1, HEADS, HD, STATE)), ("prompt_ssm_conv", (3, XBC), (1, 1, 3, XBC)),
    ("prompt_ffn_conv", (2, 2 * DFF), (1, 1, 2, 2 * DFF)),
    ("sample_k", (NSMP, AW), (1, 1, NSMP, HEADS, HD)), ("sample_v", (NSMP, AW), (1, 1, NSMP, HEADS, HD)),
    ("sample_ssm", (AW, STATE), (1, 1, HEADS, HD, STATE)), ("sample_ssm_conv", (3, XBC), (1, 1, 3, XBC)),
    ("sample_gmlp_v", (NSMP, CW), (1, 1, NSMP, CW)), ("sample_ffn_conv", (2, 2 * DFF), (1, 1, 2, 2 * DFF)),
]
SCRATCH = [
    ("x_rows", (ROWS, D), F32), ("xt_hi", (P, KD, ROWS), F32), ("xt_lo", (P, KD, ROWS), F32),
    ("v_rows", (ROWS, AW), F32), ("z_rows", (ROWS, AW), F32), ("dt_rows", (ROWS, HEADS), F32), ("uv_rows", (ROWS, 2 * CW), F32),
    ("qk_hi", (2 * AW, ROWS), F32), ("qk_lo", (2 * AW, ROWS), F32), ("xbc_t", (P, NXBC, ROWS), F32), ("rel_ext", (HEADS, WIN + P), F32),
    ("mixed", (ROWS, D), F32), ("x1_rows", (ROWS, D), F32), ("x1t_hi", (P, KD, ROWS), F32), ("x1t_lo", (P, KD, ROWS), F32),
    ("h_t", (P, KF, ROWS), F32),
]


def build(nc):
    d = {name: nc.dram_tensor(name, shape, F32, kind="ExternalInput").ap() for name, shape in INPUTS}
    d.update({name: nc.dram_tensor(name, shape, F32, kind="ExternalOutput").ap() for name, shape, _ in OUTPUTS})
    d.update({name: nc.dram_tensor(name, shape, dt, kind="Internal").ap() for name, shape, dt in SCRATCH})
    for stage in STAGES:
        stage(nc, d)


STAGES = (project_rows, project_features, attention, ssd_and_gmlp, mix_out, ffn_up, ffn_down)


def kernel(**inputs):
    import numpy as np
    import concourse.bacc as bacc
    from concourse.bass_utils import run_bass_kernel_spmd

    nc = bacc.Bacc("TRN2", target_bir_lowering=False, num_devices=1)
    build(nc)
    arrays = {name: np.ascontiguousarray(inputs[ARGUMENT.get(name, name)]).reshape(shape) for name, shape in INPUTS}
    r = run_bass_kernel_spmd(nc, [arrays], core_ids=[0])
    return tuple(r.results[0][name].reshape(shape) for name, _, shape in OUTPUTS)
```

```python
from contextlib import ExitStack

import concourse.bass as bass
from concourse import mybir

F32 = mybir.dt.float32
F32R = mybir.dt.float32r
ALU = mybir.AluOpType
ACT = mybir.ActivationFunctionType

P = 128
D = 1024
KD = D // P
SEQ = 2048
NSMP = 64
ROWS = SEQ + NSMP
NT = SEQ // P
CACHE = 512
HEADS = 6
HD = 64
AW = HEADS * HD
STATE = 128
XBC = AW + 4 * STATE
NXBC = XBC // P
CW = 256
CG = 4
DFF = 2816
KF = DFF // P
ALPHA = 2.0 ** 0.25
EPS = 1e-5
MASKED = -1e30
REL = 192
WIN = CACHE + P
V0, Z0, X0, DT0, U0 = 2 * AW, 3 * AW, 4 * AW, 4 * AW + XBC, 4 * AW + XBC + HEADS
G0 = U0 + CW
N_IN = G0 + CW


def wait_if(eng, sem, value):
    if not isinstance(value, int) or value > 0:
        eng.wait_ge(sem, value)


def alone(eng):
    eng.nop(nofuse=True)


def tile_rows(t):
    if isinstance(t, int):
        return slice(t * P, t * P + (NSMP if t == NT else P))
    return bass.ds(t * P, P)


def n_rows(t):
    return NSMP if isinstance(t, int) and t == NT else P


class Place:

    def __init__(self, nc, ctx, stage):
        self.nc, self.ctx, self.stage = nc, ctx, stage

    def sb(self, name, shape, dt=F32):
        return self.ctx.enter_context(self.nc.sbuf_tensor(f"{self.stage}_{name}", shape, dt))

    def ps(self, name, shape):
        return self.ctx.enter_context(self.nc.psum_tensor(f"{self.stage}_{name}", shape, F32))

    def sem(self, name):
        return self.nc.alloc_semaphore(f"{self.stage}_{name}")


def bc_row(ap1d, n):
    return ap1d.rearrange("(a n) -> a n", a=1).to_broadcast([P, n])


def products(pe, out, lhs_hi, lhs_lo, rhs_hi, rhs_lo, first, last):
    pe.matmul(out, lhs_hi, rhs_hi, start=first, stop=False)
    pe.matmul(out, lhs_hi, rhs_lo, start=False, stop=False)
    return pe.matmul(out, lhs_lo, rhs_hi, start=False, stop=last)


def make_identity(pool, ident, zero_done, ident_done):
    pool.memset(ident[:], 0.0).then_inc(zero_done, 1)
    pool.wait_ge(zero_done, 1)
    pool.affine_select(out=ident[:], in_=ident[:], compare_op=ALU.not_equal, fill=1.0, base=0,
                       pattern=[[-1, P]], channel_multiplier=1).then_inc(ident_done, 1)


def project_rows(nc, d):
    with nc.cleanup_on_exit(), ExitStack() as ctx:
        m = Place(nc, ctx, "pr")
        cols = [(V0, 512), (V0 + 512, 256), (G0, CW), (DT0, HEADS + CW)]
        at = [0, 512, 768, 1024]
        NW = 1024 + HEADS + CW
        w_raw = m.sb("w_raw", [P, KD, NW])
        w_hi, w_lo = m.sb("w_hi", [P, KD, NW], F32R), m.sb("w_lo", [P, KD, NW], F32R)
        x = m.sb("x", [P, 2, D])
        xr = m.sb("xr", [P, 2, D])
        xt_hi, xt_lo = m.sb("xt_hi", [P, 2, KD, P], F32R), m.sb("xt_lo", [P, 2, KD, P], F32R)
        xt = m.sb("xt", [P, 2, KD, P])
        g_bc, b_bc = m.sb("g_bc", [P, D]), m.sb("b_bc", [P, D])
        stats, mv, sd, rs = m.sb("stats", [P, 2, 6]), m.sb("mv", [P, 2]), m.sb("sd", [P, 2]), m.sb("rs", [P, 1])
        ident = m.sb("ident", [P, P])
        v_out, z_out = m.sb("v_out", [P, 2, AW]), m.sb("z_out", [P, 2, AW])
        uv_out, dt_out = m.sb("uv_out", [P, 2, 2 * CW]), m.sb("dt_out", [P, 2, 8])
        ps_y, ps_t = m.ps("ps_y", [P, 2, 3, 512]), m.ps("ps_t", [P, KD, P])

        zero_done, ident_done = m.sem("zero_done"), m.sem("ident_done")
        w_loaded = [m.sem(f"w_loaded{k}") for k in range(KD)]
        w_hi_done, w_lo_done = m.sem("w_hi_done"), m.sem("w_lo_done")
        gb_loaded = m.sem("gb_loaded")
        x_loaded = [m.sem("x_loaded0"), m.sem("x_loaded1")]
        first_x_loaded = m.sem("first_x_loaded")
        bn_done, aggr_done, var_done, sd_done = m.sem("bn_done"), m.sem("aggr_done"), m.sem("var_done"), m.sem("sd_done")
        rs_done, xg_done, xr_done = m.sem("rs_done"), m.sem("xg_done"), m.sem("xr_done")
        t_done, xt_done, hi_done, lo_done, y_done = m.sem("t_done"), m.sem("xt_done"), m.sem("hi_done"), m.sem("lo_done"), m.sem("y_done")
        vdt_done, act_out_done = m.sem("vdt_done"), m.sem("act_out_done")
        xr_stored = [m.sem("xr_stored0"), m.sem("xr_stored1")]
        xt_stored = [m.sem("xt_stored0"), m.sem("xt_stored1")]
        y_stored = [m.sem("y_stored0"), m.sem("y_stored1")]

        def half(t):
            return t // 2

        def tiles(eng, step):
            step(0, 0, 0)
            step(1, 1, 0)
            with eng.Fori(1, 7) as i:
                step(2 * i, 0, i)
                step(2 * i + 1, 1, i)
            for t in (14, 15, 16):
                step(t, t % 2, t // 2)

        with nc.Block() as block:
            @block.sync
            def _(sp):
                sp.dma_start(x[:, 0, :], d["x_prompt"][0:P, :]).then_inc(first_x_loaded, 16)
                for k in range(KD):
                    if k == 1:
                        sp.dma_start(g_bc[:], bc_row(d["ln_in_g"], D)).then_inc(gb_loaded, 16)
                        sp.dma_start(b_bc[:], bc_row(d["ln_in_b"], D)).then_inc(gb_loaded, 16)
                    for (c, n), a in zip(cols, at):
                        sp.dma_start(w_raw[:, k, a:a + n], d["w_in"][k * P:(k + 1) * P, c:c + n]).then_inc(w_loaded[k], 16)
                def step(t, p, i):
                    n = n_rows(t)
                    sp.wait_ge(xr_done, t + 1)
                    alone(sp)
                    sp.dma_start(d["x_rows"][tile_rows(t), :], xr[:n, p, :]).then_inc(xr_stored[p], 16)
                    sp.wait_ge(xt_done, t + 1)
                    alone(sp)
                    sp.dma_start(d["xt"][:, :, tile_rows(t)], xt[:, p, :, :n]).then_inc(xt_stored[p], 16)
                    sp.wait_ge(vdt_done, t + 1)
                    alone(sp)
                    sp.dma_start(d["v_rows"][tile_rows(t), :], v_out[:n, p, :]).then_inc(y_stored[p], 16)
                    sp.dma_start(d["dt_rows"][tile_rows(t), :], dt_out[:n, p, :HEADS]).then_inc(y_stored[p], 16)
                    sp.wait_ge(act_out_done, t + 1)
                    alone(sp)
                    sp.dma_start(d["z_rows"][tile_rows(t), :], z_out[:n, p, :]).then_inc(y_stored[p], 16)
                    sp.dma_start(d["uv_rows"][tile_rows(t), :], uv_out[:n, p, :]).then_inc(y_stored[p], 16)
                tiles(sp, step)
                for p, count in ((0, 9), (1, 8)):
                    sp.wait_ge(xr_stored[p], 16 * count)
                    sp.wait_ge(xt_stored[p], 16 * count)
                    sp.wait_ge(y_stored[p], 64 * count)

            @block.gpsimd
            def _(pool):
                make_identity(pool, ident, zero_done, ident_done)

                def load_x(t, p):
                    if isinstance(t, int) and t == NT:
                        pool.dma_start(x[:NSMP, p, :], d["x_sample"]).then_inc(x_loaded[p], 16)
                    else:
                        pool.dma_start(x[:, p, :], d["x_prompt"][tile_rows(t), :]).then_inc(x_loaded[p], 16)

                pool.wait_ge(w_hi_done, 1)
                load_x(1, 1)

                def step(t, p, i):
                    if not isinstance(t, int) or t + 2 <= NT:
                        pool.wait_ge(xg_done, t + 1)
                        alone(pool)
                        load_x(t + 2, p)
                tiles(pool, step)

            @block.scalar
            def _(act):
                def weights_hi(ks):
                    for k in ks:
                        act.wait_ge(w_loaded[k], 64)
                        act.copy(w_hi[:, k, :], w_raw[:, k, :]).then_inc(w_hi_done, 1)

                def root(t):
                    n = n_rows(t)
                    act.wait_ge(var_done, t + 1)
                    act.activation(sd[:n, 1:2], sd[:n, 0:1], ACT.Sqrt).then_inc(sd_done, 1)

                def hi(t, p, i):
                    n = n_rows(t)
                    act.wait_ge(t_done, t + 1)
                    if not (isinstance(t, int) and t < 2):
                        act.wait_ge(xt_stored[p], 16 * i)
                        act.wait_ge(lo_done, t - 1)
                        act.wait_ge(y_done, t - 1)
                    act.copy(xt[:, p, :, :n], ps_t[:, :, :n]).then_inc(xt_done, 1)
                    act.wait_ge(xt_done, t + 1)
                    act.copy(xt_hi[:, p, :, :n], xt[:, p, :, :n]).then_inc(hi_done, 1)

                root(0)
                weights_hi(range(0, 3))
                hi(0, 0, 0)
                weights_hi(range(3, 5))
                root(1)
                weights_hi(range(5, KD))

                def step(t, p, i):
                    n = n_rows(t)
                    if not isinstance(t, int) or t + 1 <= NT:
                        hi(t + 1, 1 - p, i + p)
                    if not isinstance(t, int) or t + 2 <= NT:
                        root(t + 2)
                    act.wait_ge(y_done, t + 1)
                    if not (isinstance(t, int) and t < 2):
                        act.wait_ge(y_stored[p], 64 * i)
                    y = ps_y[:, p]
                    act.activation(z_out[:n, p, 0:128], y[:n, 0, AW:512], ACT.Silu)
                    act.activation(z_out[:n, p, 128:AW], y[:n, 1, 0:256], ACT.Silu)
                    act.activation(uv_out[:n, p, CW:], y[:n, 1, 256:512], ACT.Gelu_apprx_tanh)
                    act.activation(uv_out[:n, p, :CW], y[:n, 2, HEADS:HEADS + CW],
                                   ACT.Gelu_apprx_tanh).then_inc(act_out_done, 1)
                tiles(act, step)

            @block.vector
            def _(dve):
                def weights_lo(ks):
                    for k in ks:
                        dve.wait_ge(w_hi_done, k + 1)
                        dve.tensor_tensor(w_lo[:, k, :], w_raw[:, k, :], w_hi[:, k, :].bitcast(F32),
                                          ALU.subtract).then_inc(w_lo_done, 1)

                def norm(t, p, i):
                    n = n_rows(t)
                    if isinstance(t, int) and t == 0:
                        dve.wait_ge(first_x_loaded, 16)
                    else:
                        dve.wait_ge(x_loaded[p], 16 * (i + p))
                    for c in range(2):
                        last = dve.bn_stats(stats[:n, c, :], x[:n, p, c * 512:(c + 1) * 512])
                    last.then_inc(bn_done, 1)
                    dve.wait_ge(bn_done, t + 1)
                    alone(dve)
                    dve.bn_aggr(mv[:n, :], stats[:n].rearrange("p a b -> p (a b)")).then_inc(aggr_done, 1)
                    dve.wait_ge(aggr_done, t + 1)
                    dve.tensor_scalar(sd[:n, 0:1], mv[:n, 1:2], EPS, None, ALU.add).then_inc(var_done, 1)
                    dve.wait_ge(sd_done, t + 1)
                    dve.reciprocal(rs[:n, :], sd[:n, 1:2]).then_inc(rs_done, 1)
                    dve.wait_ge(rs_done, t + 1)
                    if isinstance(t, int) and t == 0:
                        dve.wait_ge(gb_loaded, 32)
                    if not (isinstance(t, int) and t < 2):
                        dve.wait_ge(xr_stored[p], 16 * i)
                        dve.wait_ge(t_done, t - 1)
                    dve.scalar_tensor_tensor(out=xr[:n, p, :], in0=x[:n, p, :], scalar=mv[:n, 0:1], in1=g_bc[:n, :],
                                             op0=ALU.subtract, op1=ALU.mult).then_inc(xg_done, 1)
                    dve.wait_ge(xg_done, t + 1)
                    dve.scalar_tensor_tensor(out=xr[:n, p, :], in0=xr[:n, p, :], scalar=rs[:n, :], in1=b_bc[:n, :],
                                             op0=ALU.mult, op1=ALU.add).then_inc(xr_done, 1)

                def lo(t, p):
                    n = n_rows(t)
                    dve.wait_ge(hi_done, t + 1)
                    dve.tensor_tensor(xt_lo[:, p, :, :n], xt[:, p, :, :n], xt_hi[:, p, :, :n].bitcast(F32),
                                      ALU.subtract).then_inc(lo_done, 1)

                norm(0, 0, 0)
                weights_lo(range(0, 3))
                lo(0, 0)
                weights_lo(range(3, 5))
                norm(1, 1, 0)
                weights_lo(range(5, KD))

                def step(t, p, i):
                    n = n_rows(t)
                    if not isinstance(t, int) or t + 1 <= NT:
                        lo(t + 1, 1 - p)
                    if not isinstance(t, int) or t + 2 <= NT:
                        norm(t + 2, p, i + 1)
                    dve.wait_ge(y_done, t + 1)
                    dve.wait_ge(act_out_done, t + 1)
                    if not (isinstance(t, int) and t < 2):
                        dve.wait_ge(y_stored[p], 64 * i)
                    dve.tensor_copy(v_out[:n, p, :], ps_y[:n, p, 0, 0:AW])
                    dve.tensor_copy(dt_out[:n, p, :HEADS], ps_y[:n, p, 2, 0:HEADS]).then_inc(vdt_done, 1)
                tiles(dve, step)

            @block.tensor
            def _(pe):
                pe.wait_ge(ident_done, 1)

                def turn(t, p):
                    n = n_rows(t)
                    pe.wait_ge(xr_done, t + 1)
                    wait_if(pe, xt_done, t)
                    for k in range(KD):
                        last = pe.transpose(ps_t[:, k, :n], xr[:n, p, k * P:(k + 1) * P], ident[:n, :n])
                    last.then_inc(t_done, 1)

                turn(0, 0)

                def step(t, p, i):
                    n = n_rows(t)
                    first = isinstance(t, int) and t == 0
                    if not first and (not isinstance(t, int) or t + 1 <= NT):
                        turn(t + 1, 1 - p)
                    pe.wait_ge(lo_done, t + 1)
                    if not (isinstance(t, int) and t < 2):
                        pe.wait_ge(vdt_done, t - 1)
                    outs = [(ps_y[:n, p, b, 0:w], 512 * b, w) for b, w in enumerate((512, 512, HEADS + CW))]

                    def product(k, x):
                        out, a, w = x
                        return products(pe, out, xt_hi[:, p, k, :n], xt_lo[:, p, k, :n],
                                        w_hi[:, k, a:a + w], w_lo[:, k, a:a + w], k == 0, k == KD - 1)
                    if first:
                        for k in range(KD):
                            if k == 6:
                                turn(1, 1)
                            pe.wait_ge(w_lo_done, k + 1)
                            for x in outs:
                                last = product(k, x)
                    else:
                        for x in outs:
                            for k in range(KD):
                                last = product(k, x)
                    last.then_inc(y_done, 1)
                tiles(pe, step)


def project_features(nc, d):
    with nc.cleanup_on_exit(), ExitStack() as ctx:
        m = Place(nc, ctx, "pf")
        GN = 304
        NG = ROWS // GN
        TAIL = SEQ - NG * GN
        NM = (2 * AW + XBC) // P
        NQK = 2 * AW // P
        W = 2 * AW + XBC
        w_raw = m.sb("w_raw", [P, 4, W])
        w_hi, w_lo = m.sb("w_hi", [P, KD, W], F32R), m.sb("w_lo", [P, KD, W], F32R)
        xt = m.sb("xt", [P, 2, KD, GN])
        xt_hi, xt_lo = m.sb("xt_hi", [P, 2, KD, GN], F32R), m.sb("xt_lo", [P, 2, KD, GN], F32R)
        qk_hi, qk_lo = m.sb("qk_hi", [P, 2, GN], F32R), m.sb("qk_lo", [P, 2, GN], F32R)
        cin = m.sb("cin", [P, 2, 3 + GN])
        conv, conv_out = m.sb("conv", [P, 2, GN]), m.sb("conv_out", [P, 2, GN])
        halo, halo_smp = m.sb("halo", [P, NXBC, 3]), m.sb("halo_smp", [P, NXBC, 3])
        taps, shift = m.sb("taps", [P, NXBC, 4]), m.sb("shift", [P, NXBC])
        ext = m.sb("ext", [HEADS, WIN + P])
        ps_y = m.ps("ps_y", [P, 8, 512])

        w_loaded = [m.sem(f"w_loaded{k}") for k in range(4)]
        w_hi_done, w_lo_done = m.sem("w_hi_done"), m.sem("w_lo_done")
        small_loaded, halo_zeroed = m.sem("small_loaded"), m.sem("halo_zeroed")
        xt_loaded = [m.sem("xt_loaded0"), m.sem("xt_loaded1")]
        first_xt_loaded = [m.sem("first_xt_loaded0"), m.sem("first_xt_loaded1")]
        xt_hi_done, xt_lo_done = m.sem("xt_hi_done"), m.sem("xt_lo_done")
        y_done, evac_done, qk_lo_done = m.sem("y_done"), m.sem("evac_done"), m.sem("qk_lo_done")
        halo_in_done, conv_done, tap_done, silu_done = m.sem("halo_in_done"), m.sem("conv_done"), m.sem("tap_done"), m.sem("silu_done")
        qk_stored = [m.sem("qk_stored0"), m.sem("qk_stored1")]
        xbc_stored = [m.sem("xbc_stored0"), m.sem("xbc_stored1")]
        state_stored = m.sem("state_stored")
        table_loaded, ext_done, ext_stored = m.sem("table_loaded"), m.sem("ext_done"), m.sem("ext_stored")

        def width(g):
            return ROWS - NG * GN if isinstance(g, int) and g == NG else GN

        def gcols(g):
            if isinstance(g, int):
                return slice(g * GN, g * GN + width(g))
            return bass.ds(g * GN, GN)

        def groups(eng, step):
            step(0, 0, 0)
            step(1, 1, 0)
            with eng.Fori(1, NG // 2) as i:
                step(2 * i, 0, i)
                step(2 * i + 1, 1, i)
            step(NG, 0, NG // 2)

        def half_features(e):
            return slice(e * KD // 2, (e + 1) * KD // 2)

        def scale(j):
            return HD ** -0.5 if j < NQK // 2 else 1.0

        def tail(g):
            return isinstance(g, int) and g == NG

        def xbc_count(g, j):
            return (NXBC + 1 - j % 2) // 2 * g + j // 2

        with nc.Block() as block:
            @block.sync
            def _(sp):
                for k in range(KD):
                    if k in (1, 3):
                        ks = half_features(k // 2)
                        sp.dma_start(xt[:, 0, ks, :], d["xt"][:, ks, 0:GN]).then_inc(first_xt_loaded[k // 2], 16)
                    if k >= 4:
                        sp.wait_ge(w_hi_done, k - 3)
                        sp.wait_ge(w_lo_done, k - 3)
                    rows = slice(k * P, (k + 1) * P)
                    sp.dma_start(w_raw[:, k % 4, 0:2 * AW], d["w_in"][rows, 0:2 * AW]).then_inc(w_loaded[k % 4], 16)
                    sp.dma_start(w_raw[:, k % 4, 2 * AW:], d["w_in"][rows, X0:X0 + XBC]).then_inc(w_loaded[k % 4], 16)

                def step(g, p, i):
                    n = width(g)
                    for j in range(NQK):
                        sp.wait_ge(qk_lo_done, NQK * g + j + 1)
                        alone(sp)
                        rows = slice(j * P, (j + 1) * P)
                        sp.dma_start(d["qk_hi"][rows, gcols(g)], qk_hi[:, j % 2, :n].bitcast(F32)).then_inc(qk_stored[j % 2], 16)
                        sp.dma_start(d["qk_lo"][rows, gcols(g)], qk_lo[:, j % 2, :n].bitcast(F32)).then_inc(qk_stored[j % 2], 16)
                    for j in range(NXBC):
                        sp.wait_ge(silu_done, NXBC * g + j + 1)
                        alone(sp)
                        sp.dma_start(d["xbc_t"][:, j, gcols(g)], conv_out[:, j % 2, :n]).then_inc(xbc_stored[j % 2], 16)
                groups(sp, step)
                sp.wait_ge(conv_done, NXBC * (NG + 1))
                for c in range(3):
                    sp.dma_start(d["prompt_ssm_conv"][c].rearrange("(m p) -> p m", p=P), halo[:, :, c], allow_slow_non_contiguous=True).then_inc(state_stored, 16)
                for c in range(3):
                    sp.dma_start(d["sample_ssm_conv"][c].rearrange("(m p) -> p m", p=P), halo_smp[:, :, c], allow_slow_non_contiguous=True).then_inc(state_stored, 16)
                sp.wait_ge(state_stored, 16 * 6)
                for p in range(2):
                    sp.wait_ge(qk_stored[p], 32 * (NQK // 2) * (NG + 1))
                    sp.wait_ge(xbc_stored[p], 16 * xbc_count(NG + 1, p))

            @block.gpsimd
            def _(pool):
                def load_xt(g, p):
                    n = width(g)
                    pool.dma_start(xt[:, p, :, :n], d["xt"][:, :, gcols(g)]).then_inc(xt_loaded[p], 16)

                for c in range(4):
                    pool.dma_start(taps[:, :, c], d["ssm_conv_w"][c].rearrange("(m p) -> p m", p=P),
                                   allow_slow_non_contiguous=True).then_inc(small_loaded, 16)
                pool.dma_start(shift[:], d["ssm_conv_b"].rearrange("(m p) -> p m", p=P), allow_slow_non_contiguous=True).then_inc(small_loaded, 16)
                for c in range(3):
                    pool.dma_start(halo_smp[:, :, c], d["state_ssm_conv"][c].rearrange("(m p) -> p m", p=P),
                                   allow_slow_non_contiguous=True).then_inc(small_loaded, 16)
                pool.memset(halo[:], 0.0).then_inc(halo_zeroed, 1)
                pool.wait_ge(w_hi_done, KD - 1)
                load_xt(1, 1)
                back = bass.AP(d["rel_bias"].tensor, REL - 1, [[REL, HEADS], [-1, REL]])
                pool.dma_start(ext[:, WIN - P - 1:WIN - P - 1 + REL], back, allow_slow_non_contiguous=True).then_inc(table_loaded, 16)
                pool.wait_ge(table_loaded, 16)
                lo, hi = WIN - P - 1, WIN - P - 1 + REL
                pool.tensor_copy(ext[:, 0:lo], ext[:, lo:lo + 1].to_broadcast([HEADS, lo]))
                pool.tensor_copy(ext[:, hi:], ext[:, hi - 1:hi].to_broadcast([HEADS, WIN + P - hi])).then_inc(ext_done, 1)
                pool.wait_ge(ext_done, 1)
                pool.dma_start(d["rel_ext"], ext[:]).then_inc(ext_stored, 16)
                pool.wait_ge(ext_stored, 16)

                def step(g, p, i):
                    if not isinstance(g, int) or g + 2 <= NG:
                        pool.wait_ge(xt_lo_done, g + 2)
                        alone(pool)
                        load_xt(g + 2, p)
                step(0, 0, 0)
                step(1, 1, 0)
                with pool.Fori(1, NG // 2 - 1) as i:
                    step(2 * i, 0, i)
                    step(2 * i + 1, 1, i)
                step(NG - 2, 0, NG // 2 - 1)

            @block.scalar
            def _(act):
                for k in range(KD):
                    act.wait_ge(w_loaded[k % 4], 32 * (k // 4 + 1))
                    act.copy(w_hi[:, k, :], w_raw[:, k % 4, :]).then_inc(w_hi_done, 1)
                    if k in (0, 3):
                        ks = half_features(k // 3)
                        act.wait_ge(first_xt_loaded[k // 3], 16)
                        act.copy(xt_hi[:, 0, ks, :], xt[:, 0, ks, :]).then_inc(xt_hi_done, 1)

                def split_hi(g, p, i):
                    n = width(g)
                    act.wait_ge(xt_loaded[p], 16 * (i + p))
                    wait_if(act, y_done, NM * (g - 1))
                    act.copy(xt_hi[:, p, :, :n], xt[:, p, :, :n]).then_inc(xt_hi_done, 1)

                def step(g, p, i):
                    n = width(g)
                    for j in range(NQK):
                        if not (isinstance(g, int) and g == 0 and j < 2):
                            act.wait_ge(qk_stored[j % 2], 32 * (NQK // 2 * g + j // 2))
                        act.wait_ge(y_done, NM * g + j + 1)
                        act.mul(qk_hi[:, j % 2, :n], ps_y[:, j, :n], scale(j)).then_inc(evac_done, 1)
                    if not tail(g):
                        split_hi(g + 1, 1 - p, i + p)

                    def silu(j):
                        if not (isinstance(g, int) and g == 0 and j < 2):
                            act.wait_ge(xbc_stored[j % 2], 16 * xbc_count(g, j))
                        act.wait_ge(conv_done, NXBC * g + j + 1)
                        if tail(g):
                            act.activation(conv_out[:, j % 2, :TAIL], conv[:, j % 2, :TAIL], ACT.Silu)
                            act.activation(conv_out[:, j % 2, TAIL:n], conv[:, j % 2, TAIL + 3:n + 3], ACT.Silu).then_inc(silu_done, 1)
                        else:
                            act.activation(conv_out[:, j % 2, :n], conv[:, j % 2, :n], ACT.Silu).then_inc(silu_done, 1)

                    for j in range(NXBC):
                        wait_if(act, conv_done, NXBC * g + j - (1 if j != 0 else 0) if j != 1 else NXBC * g)
                        act.wait_ge(y_done, NM * g + NQK + j + 1)
                        y = ps_y[:, (NQK + j) % 8, :n]
                        if tail(g):
                            act.copy(cin[:, j % 2, 3:3 + TAIL], y[:, :TAIL])
                            act.copy(cin[:, j % 2, TAIL + 6:n + 6], y[:, TAIL:]).then_inc(evac_done, 1)
                        else:
                            act.copy(cin[:, j % 2, 3:3 + n], y).then_inc(evac_done, 1)
                        if j >= 1:
                            silu(j - 1)
                    silu(NXBC - 1)
                groups(act, step)

            @block.vector
            def _(dve):
                for k in range(KD):
                    dve.wait_ge(w_hi_done, k + 1)
                    dve.tensor_tensor(w_lo[:, k, :], w_raw[:, k % 4, :], w_hi[:, k, :].bitcast(F32),
                                      ALU.subtract).then_inc(w_lo_done, 1)
                    if k in (0, 3):
                        ks = half_features(k // 3)
                        dve.wait_ge(xt_hi_done, k // 3 + 1)
                        dve.tensor_tensor(xt_lo[:, 0, ks, :], xt[:, 0, ks, :], xt_hi[:, 0, ks, :].bitcast(F32),
                                          ALU.subtract).then_inc(xt_lo_done, 1)

                def split_lo(g, p):
                    n = width(g)
                    dve.wait_ge(xt_hi_done, g + 2)
                    dve.tensor_tensor(xt_lo[:, p, :, :n], xt[:, p, :, :n], xt_hi[:, p, :, :n].bitcast(F32),
                                      ALU.subtract).then_inc(xt_lo_done, 1)

                dve.wait_ge(small_loaded, 128)
                dve.wait_ge(halo_zeroed, 1)

                def step(g, p, i):
                    n = width(g)
                    for j in range(NQK):
                        if not (isinstance(g, int) and g == 0 and j < 2):
                            dve.wait_ge(qk_stored[j % 2], 32 * (NQK // 2 * g + j // 2))
                        dve.wait_ge(evac_done, NM * g + j + 1)
                        alone(dve)
                        dve.scalar_tensor_tensor(out=qk_lo[:, j % 2, :n], in0=ps_y[:, j, :n], scalar=scale(j),
                                                 in1=qk_hi[:, j % 2, :n].bitcast(F32), op0=ALU.mult,
                                                 op1=ALU.subtract).then_inc(qk_lo_done, 1)
                    if not tail(g):
                        split_lo(g + 1, 1 - p)
                    for j in range(NXBC):
                        u, b = NXBC * g + j, j % 2
                        c = cin[:, b]
                        nc_ = n + 3 if tail(g) else n
                        y = conv[:, b, :nc_]
                        dve.wait_ge(evac_done, NM * g + NQK + j + 1)
                        if tail(g):
                            dve.tensor_copy(c[:, TAIL + 3:TAIL + 6], halo_smp[:, j, :])
                        dve.tensor_copy(c[:, 0:3], halo[:, j, :]).then_inc(halo_in_done, 1)
                        if not (isinstance(g, int) and g == 0 and j < 2):
                            dve.wait_ge(silu_done, u if j == 0 else u - 1)
                        dve.wait_ge(halo_in_done, u + 1)
                        dve.tensor_scalar(y, c[:, 0:nc_], taps[:, j, 0:1], shift[:, j:j + 1], ALU.mult,
                                          ALU.add).then_inc(tap_done, 1)
                        for e in (1, 2):
                            dve.wait_ge(tap_done, 3 * u + e)
                            dve.scalar_tensor_tensor(out=y, in0=c[:, e:e + nc_], scalar=taps[:, j, e:e + 1], in1=y,
                                                     op0=ALU.mult, op1=ALU.add).then_inc(tap_done, 1)
                        if tail(g):
                            dve.tensor_copy(halo_smp[:, j, :], c[:, n + 3:n + 6])
                            dve.tensor_copy(halo[:, j, :], c[:, TAIL:TAIL + 3])
                        else:
                            dve.tensor_copy(halo[:, j, :], c[:, n:n + 3])
                        dve.wait_ge(tap_done, 3 * u + 3)
                        dve.scalar_tensor_tensor(out=y, in0=c[:, 3:3 + nc_], scalar=taps[:, j, 3:4], in1=y,
                                                 op0=ALU.mult, op1=ALU.add).then_inc(conv_done, 1)
                groups(dve, step)

            @block.tensor
            def _(pe):
                def step(g, p, i):
                    n = width(g)
                    if not (isinstance(g, int) and g == 0):
                        pe.wait_ge(xt_lo_done, g + 2)

                    def product(j, k):
                        c = slice(j * P, (j + 1) * P)
                        last = products(pe, ps_y[:, j % 8, :n], w_hi[:, k, c], w_lo[:, k, c],
                                        xt_hi[:, p, k, :n], xt_lo[:, p, k, :n], k == 0, k == KD - 1)
                        if k == KD - 1:
                            last.then_inc(y_done, 1)

                    first = isinstance(g, int) and g == 0
                    if first:
                        for k in range(KD):
                            if k % (KD // 2) == 0:
                                pe.wait_ge(xt_lo_done, k // (KD // 2) + 1)
                            pe.wait_ge(w_lo_done, k + 1)
                            for j in range(8):
                                product(j, k)
                    for j in range(8 if first else 0, NM):
                        wait_if(pe, evac_done, NM * g + j - 4)
                        if j == NQK - 1:
                            wait_if(pe, qk_lo_done, NQK * g)
                        if j >= 8:
                            pe.wait_ge(qk_lo_done, NQK * g + j - 7)
                        for k in range(KD):
                            product(j, k)
                groups(pe, step)


class Band:

    def __init__(self, t):
        self.t = t
        self.smp = isinstance(t, int) and t == NT
        self.nb = min(t + 1, 5) if isinstance(t, int) else 5
        self.nq = NSMP if self.smp else P
        self.width = CACHE + NSMP if self.smp else self.nb * P
        self.col0 = 0 if self.smp else WIN - self.width

    def block_rows(self, k):
        return min(P, self.width - k * P)

    def first(self):
        return self.t + 1 - self.nb

    def block(self, k):
        return (k if k < CACHE // P else NT) if self.smp else self.first() + k

    def key_cols(self, c, n):
        if self.smp:
            return slice(c, c + n) if c < CACHE else slice(SEQ + c - CACHE, SEQ + c - CACHE + n)
        at = self.first() * P + c
        return slice(at, at + n) if isinstance(at, int) else bass.ds(at, n)


def attention(nc, d):
    with nc.cleanup_on_exit(), ExitStack() as ctx:
        m = Place(nc, ctx, "at")
        k_hi, k_lo, v = m.sb("k_hi", [P, HEADS, ROWS], F32R), m.sb("k_lo", [P, HEADS, ROWS], F32R), m.sb("v", [P, NT + 1, AW])
        q, q_smp = m.sb("q", [P, 2, HEADS, P], F32R), m.sb("q_smp", [P, HEADS, NSMP], F32R)
        cache = m.sb("cache", [P, 4, HEADS, 2, HD])
        bias, bias_up = m.sb("bias", [P, HEADS, WIN]), m.sb("bias_up", [P, HEADS, WIN])
        ident, flip, ident_r = m.sb("ident", [P, P]), m.sb("flip", [P, P]), m.sb("ident_r", [P, HD], F32R)
        s = m.sb("s", [P, 3, WIN])
        pt = m.sb("pt", [P, 2, 5, P])
        top, ntop, total, inv = (m.sb("top", [P, HEADS]), m.sb("ntop", [P, HEADS]), m.sb("total", [P, HEADS]), m.sb("inv", [P, HEADS]))
        o = m.sb("o", [P, 2, AW])
        k_rows = m.sb("k_rows", [P, 5, AW])
        ps_s, ps_t, ps_o = m.ps("ps_s", [P, 2, 1024]), m.ps("ps_t", [P, 1024]), m.ps("ps_o", [P, 2, 512])
        NFIRST, REST = 3, 512
        NO_REST = HEADS * NFIRST

        zero_done, ident_done, ident_r_done = m.sem("zero_done"), m.sem("ident_done"), m.sem("ident_r_done")
        bias_loaded, bias_done = m.sem("bias_loaded"), m.sem("bias_done")
        flip_done, bias_flipped, bias_copied = m.sem("flip_done"), m.sem("bias_flipped"), m.sem("bias_copied")
        cache_loaded, cache_turned, cache_hi_done, cache_lo_done = (
            m.sem("cache_loaded"), m.sem("cache_turned"), m.sem("cache_hi_done"), m.sem("cache_lo_done"))
        loaded = [m.sem("loaded0"), m.sem("loaded1")]
        smp_loaded = m.sem("smp_loaded")
        s_done, biased, ntop_done, exp_done = m.sem("s_done"), m.sem("biased"), m.sem("ntop_done"), m.sem("exp_done")
        turned, pt_done = m.sem("turned"), m.sem("pt_done")
        rest_turned, rest_done = m.sem("rest_turned"), m.sem("rest_done")
        pv_done, inv_done, o_done = m.sem("pv_done"), m.sem("inv_done"), m.sem("o_done")
        o_stored = [m.sem("o_stored0"), m.sem("o_stored1")]
        rows_turned, rows_done, rows_stored = m.sem("rows_turned"), m.sem("rows_done"), m.sem("rows_stored")
        caches_stored = m.sem("caches_stored")

        LOOP0, LOOP1 = 6, 14

        def tiles(eng, step, before_last=None):
            def straight(t):
                step(Band(t - 1) if t else None, Band(t), Band(t + 1) if t < NT else None, t % 2)
            for t in range(LOOP0):
                straight(t)
            with eng.Fori(LOOP0 // 2, LOOP1 // 2) as i:
                for p in range(2):
                    t = 2 * i + p
                    step(Band(t - 1), Band(t), Band(t + 1), p)
            if before_last:
                before_last()
            for t in range(LOOP1, NT + 1):
                straight(t)

        def heads(eng, step, before_last=None):
            def tile_step(before, cur, after, p):
                for h in range(HEADS):
                    prev = (cur, p, h - 1) if h else (before, 1 - p, HEADS - 1) if before else None
                    nxt, nxt2 = [(cur, p, x) if x < HEADS else (after, 1 - p, x - HEADS) if after else None
                                 for x in (h + 1, h + 2)]
                    step(prev, (cur, p, h), nxt, nxt2)
            tiles(eng, tile_step, before_last)

        def tile_count(b, p, each, ahead=0):
            return each * (b.t // 2 + ahead) if isinstance(b.t, int) else each // 2 * (b.t - p) + each * ahead

        with nc.Block() as block:
            @block.sync
            def _(sp):
                toeplitz = bass.AP(d["rel_ext"].tensor, 0, [[1, P], [WIN + P, HEADS], [1, WIN]])
                sp.dma_start(bias_up[:], toeplitz).then_inc(bias_loaded, 16)
                by_head = {name: d[name].rearrange("(h f) c -> f h c", f=HD) for name in ("qk_hi", "qk_lo")}

                def load(b, p):
                    done = smp_loaded if b.smp else loaded[p]
                    n = b.nq
                    cols = tile_rows(b.t)
                    for part, at in (("qk_hi", 0), ("qk_lo", HD)):
                        dst = q_smp[at:at + HD, :, :] if b.smp else q[at:at + HD, p, :, :]
                        sp.dma_start(dst.bitcast(F32), by_head[part][:, 0:HEADS, cols]).then_inc(done, 16)
                    for part, k_part in (("qk_hi", k_hi), ("qk_lo", k_lo)):
                        for at in (0, HD):
                            sp.dma_start(k_part[at:at + HD, :, cols].bitcast(F32), by_head[part][:, HEADS:, cols]).then_inc(done, 16)
                    blk = slice(b.t, b.t + 1) if isinstance(b.t, int) else bass.ds(b.t, 1)
                    sp.dma_start(v[:n, blk, :], d["v_rows"][cols, :].rearrange("(a p) w -> p a w", a=1)).then_inc(done, 16)

                load(Band(0), 0)

                def step(before, cur, after, p):
                    if after is not None:
                        wait_if(sp, s_done, HEADS * cur.t)
                        alone(sp) if not isinstance(cur.t, int) else None
                        load(after, 1 - p)

                def load_cache_v():
                    sp.wait_ge(pv_done, HEADS * 8)
                    sp.dma_start(v[:, 0:4, :], d["cache_v"].rearrange("(b p) w -> p b w", p=P)).then_inc(smp_loaded, 16)
                tiles(sp, step, load_cache_v)
                sp.wait_ge(rows_done, 5)
                sp.dma_start(d["prompt_k"].rearrange("(b p) w -> p b w", p=P), k_rows[:, 0:4, :]).then_inc(rows_stored, 16)
                sp.dma_start(d["sample_k"], k_rows[:NSMP, 4, :]).then_inc(rows_stored, 16)
                sp.wait_ge(rows_stored, 32)

            @block.gpsimd
            def _(pool):
                make_identity(pool, ident, zero_done, ident_done)
                pool.memset(flip[:], 0.0).then_inc(zero_done, 1)
                pool.wait_ge(zero_done, 2)
                pool.affine_select(out=flip[:], in_=flip[:], compare_op=ALU.not_equal, fill=1.0, base=1 - P,
                                   pattern=[[1, P]], channel_multiplier=1).then_inc(flip_done, 1)
                pool.wait_ge(bias_copied, HEADS)
                pool.memset(bias[0:64, :, WIN - 64:], MASKED)
                pool.memset(bias[64:P, :, 0:64], MASKED).then_inc(bias_done, 1)
                for k in range(CACHE // P):
                    for twice in range(2):
                        pool.dma_start(cache[:, k, :, twice, :], d["cache_k"][k * P:(k + 1) * P, :].rearrange(
                            "p (h f) -> p h f", h=HEADS)).then_inc(cache_loaded, 16)
                pool.dma_start(d["prompt_v"], d["v_rows"][SEQ - 512:SEQ, :]).then_inc(caches_stored, 16)
                pool.dma_start(d["sample_v"], d["v_rows"][SEQ:ROWS, :]).then_inc(caches_stored, 16)
                pool.dma_start(d["sample_gmlp_v"], d["uv_rows"][SEQ:ROWS, CW:]).then_inc(caches_stored, 16)

                def store_o(b, p):
                    pool.wait_ge(o_done, HEADS * (b.t + 1))
                    alone(pool)
                    pool.dma_start(d["mixed"][tile_rows(b.t), 0:AW], o[:b.nq, p, :]).then_inc(o_stored[p], 16)

                def step(before, cur, after, p):
                    if before is not None:
                        store_o(before, 1 - p)
                tiles(pool, step)
                store_o(Band(NT), 0)
                pool.wait_ge(o_stored[0], 16 * 9)
                pool.wait_ge(o_stored[1], 16 * 8)
                pool.wait_ge(caches_stored, 48)

            @block.vector
            def _(dve):
                dve.wait_ge(ident_done, 1)
                dve.tensor_copy(ident_r[:], ident[:, 0:HD]).then_inc(ident_r_done, 1)
                dve.wait_ge(bias_done, 1)

                def add_bias(x):
                    b, p, h = x
                    n, par = HEADS * b.t + h, h % 2
                    dve.wait_ge(s_done, n + 1)
                    if isinstance(n, int) and n - 3 < NO_REST:
                        wait_if(dve, turned, n - 2)
                    else:
                        dve.wait_ge(rest_turned, n - 2 - NO_REST)
                    alone(dve)
                    dve.tensor_tensor_reduce(out=s[:b.nq, h % 3, :b.width], in0=ps_s[:b.nq, par, :b.width],
                                             in1=bias[:b.nq, h, b.col0:b.col0 + b.width], scale=1.0, scalar=-3e38,
                                             op0=ALU.add, op1=ALU.max, accum_out=top[:b.nq, h:h + 1]).then_inc(biased, 1)
                    dve.wait_ge(biased, n + 1)
                    dve.tensor_scalar(ntop[:b.nq, h:h + 1], top[:b.nq, h:h + 1], -1.0, None,
                                      ALU.mult).then_inc(ntop_done, 1)

                def normalise(x):
                    b, p, h = x
                    n, par = HEADS * b.t + h, h % 2
                    if h == 0 and not (isinstance(b.t, int) and b.t < 2):
                        dve.wait_ge(o_stored[p], tile_count(b, p, 16))
                    dve.wait_ge(pv_done, n + 1)
                    dve.reciprocal(inv[:b.nq, h:h + 1], total[:b.nq, h:h + 1]).then_inc(inv_done, 1)
                    dve.wait_ge(inv_done, n + 1)
                    dve.tensor_scalar(o[:b.nq, p, h * HD:(h + 1) * HD], ps_o[:b.nq, par, 0:HD], inv[:b.nq, h:h + 1],
                                      None, ALU.mult).then_inc(o_done, 1)

                def take_rest(x):
                    b, p, h = x
                    n, par = HEADS * b.t + h, h % 2
                    if b.nb <= NFIRST:
                        return
                    dve.wait_ge(rest_turned, n - NO_REST + 1)
                    wait_if(dve, pv_done, n - 1)
                    if not b.smp:
                        nr = b.nb - NFIRST
                        alone(dve)
                        ins = dve.tensor_copy(pt[:, par, NFIRST:b.nb, :], ps_t[:, REST:REST + nr * P].rearrange("p (b c) -> p b c", b=nr))
                    else:
                        dve.tensor_copy(pt[:, par, NFIRST, :NSMP], ps_t[:, REST:REST + NSMP])
                        ins = dve.tensor_copy(pt[:NSMP, par, NFIRST + 1, :NSMP], ps_t[:NSMP, REST + P:REST + P + NSMP])
                    ins.then_inc(rest_done, 1)

                add_bias((Band(0), 0, 0))
                add_bias((Band(0), 0, 1))

                def step(prev, cur, nxt, nxt2):
                    if nxt2:
                        add_bias(nxt2)
                    take_rest(cur)
                    if prev:
                        normalise(prev)

                def cache_lo():
                    for h in range(HEADS):
                        dve.wait_ge(cache_hi_done, h + 1)
                        dve.tensor_tensor(k_lo[:, h, 0:CACHE], ps_o[:, h % 2, :], k_hi[:, h, 0:CACHE].bitcast(F32),
                                          ALU.subtract).then_inc(cache_lo_done, 1)
                heads(dve, step, cache_lo)
                normalise((Band(NT), 0, HEADS - 1))
                for b in range(5):
                    n = P if b < 4 else NSMP
                    dve.wait_ge(rows_turned, b + 1)
                    src = ps_s[:n, b // 2, (b % 2) * 512:(b % 2) * 512 + AW] if b < 4 else ps_t[:n, 0:AW]
                    dve.tensor_copy(k_rows[:n, b, :], src).then_inc(rows_done, 1)

            @block.scalar
            def _(act):
                def exp(x):
                    b, p, h = x
                    n, par = HEADS * b.t + h, h % 2
                    act.wait_ge(ntop_done, n + 1)
                    act.activation(s[:b.nq, h % 3, :b.width], s[:b.nq, h % 3, :b.width], ACT.Exp,
                                   bias=ntop[:b.nq, h:h + 1],
                                   accum_out=total[:b.nq, h:h + 1]).then_inc(exp_done, 1)

                def take_pt(x):
                    b, p, h = x
                    n, par = HEADS * b.t + h, h % 2
                    act.wait_ge(turned, n + 1)
                    wait_if(act, pv_done, n - 1)
                    nf = min(b.nb, NFIRST)
                    act.copy(pt[:, par, 0:nf, :b.nq],
                             ps_t[:, 0:nf * P].rearrange("p (b c) -> p b c", b=nf)[:, :, :b.nq]).then_inc(pt_done, 1)

                for h in range(HEADS):
                    act.wait_ge(bias_flipped, h + 1)
                    act.copy(bias[:, h, :], (ps_s[:, 0] if h % 2 == 0 else ps_t)[:, 0:WIN]).then_inc(bias_copied, 1)

                exp((Band(0), 0, 0))

                def step(prev, cur, nxt, nxt2):
                    if nxt:
                        exp(nxt)
                    take_pt(cur)

                def cache_hi():
                    for h in range(HEADS):
                        act.wait_ge(cache_turned, h + 1)
                        act.copy(k_hi[:, h, 0:CACHE], ps_o[:, h % 2, :]).then_inc(cache_hi_done, 1)
                heads(act, step, cache_hi)

            @block.tensor
            def _(pe):
                pe.wait_ge(ident_done, 1)
                pe.wait_ge(flip_done, 1)
                pe.wait_ge(bias_loaded, 16)
                for h in range(HEADS):
                    wait_if(pe, bias_copied, h - 1)
                    dst = ps_s[:, 0] if h % 2 == 0 else ps_t
                    pe.matmul(dst[:, 0:512], flip[:], bias_up[:, h, 0:512], start=True, stop=True)
                    pe.matmul(dst[:, 512:WIN], flip[:], bias_up[:, h, 512:], start=True, stop=True).then_inc(bias_flipped, 1)
                pe.wait_ge(bias_copied, HEADS)

                def score(x):
                    b, p, h = x
                    n, par = HEADS * b.t + h, h % 2
                    if h == 0:
                        if b.smp:
                            pe.wait_ge(smp_loaded, 16 * 8)
                        else:
                            pe.wait_ge(loaded[p], tile_count(b, p, 16 * 7, 1))
                    wait_if(pe, biased, n - 1)
                    queries = q_smp[:, h, :] if b.smp else q[:, p, h, :]
                    for c in range(0, b.width, 512):
                        w = min(512, b.width - c)
                        out = ps_s[:b.nq, par, c:c + w]
                        pe.matmul(out, queries, k_hi[:, h, b.key_cols(c, w)], start=True, stop=False)
                        last = pe.matmul(out, queries, k_lo[:, h, b.key_cols(c, w)], start=False, stop=True)
                    last.then_inc(s_done, 1)

                def turn(x):
                    b, p, h = x
                    n, par = HEADS * b.t + h, h % 2
                    pe.wait_ge(exp_done, n + 1)
                    wait_if(pe, pt_done, n)
                    for k in range(b.nb):
                        w = b.block_rows(k)
                        at = k * P if k < NFIRST else REST + (k - NFIRST) * P
                        if k == NFIRST:
                            last.then_inc(turned, 1)
                            wait_if(pe, rest_done, n - NO_REST)
                        last = pe.transpose(ps_t[:w, at:at + b.nq], s[:b.nq, h % 3, k * P:k * P + w],
                                            ident[:b.nq, :b.nq])
                    last.then_inc(turned if b.nb <= NFIRST else rest_turned, 1)

                def out(x):
                    b, p, h = x
                    n, par = HEADS * b.t + h, h % 2
                    pe.wait_ge(pt_done, n + 1)
                    if b.nb > NFIRST:
                        pe.wait_ge(rest_done, n - NO_REST + 1)
                    wait_if(pe, o_done, n - 1)
                    for k in range(b.nb):
                        w = b.block_rows(k)
                        blk = b.block(k)
                        blk = blk if isinstance(blk, int) else bass.ds(blk, 1)
                        vals = v[:w, blk, h * HD:(h + 1) * HD]
                        if not isinstance(blk, int):
                            vals = vals.rearrange("p a c -> p (a c)")
                        last = pe.matmul(ps_o[:b.nq, par, 0:HD], pt[:w, par, k, :b.nq], vals, start=(k == 0), stop=(k == b.nb - 1))
                    last.then_inc(pv_done, 1)

                score((Band(0), 0, 0))
                score((Band(0), 0, 1))

                def step(prev, cur, nxt, nxt2):
                    if nxt2:
                        score(nxt2)
                    turn(cur)
                    if prev:
                        out(prev)

                def turn_cache():
                    pe.wait_ge(cache_loaded, 16 * 8)
                    pe.wait_ge(o_done, HEADS * LOOP1 - 1)
                    for h in range(HEADS):
                        wait_if(pe, cache_lo_done, h - 1)
                        for k in range(CACHE // P):
                            twice = cache[:, k, h].rearrange("p a f -> p (a f)")
                            last = pe.transpose(ps_o[:, h % 2, k * P:(k + 1) * P], twice, ident[:])
                        last.then_inc(cache_turned, 1)
                    pe.wait_ge(cache_lo_done, HEADS)
                heads(pe, step, turn_cache)
                out((Band(NT), 0, HEADS - 1))
                pe.wait_ge(ident_r_done, 1)
                pe.wait_ge(pt_done, HEADS * (NT + 1))
                for b in range(5):
                    n = P if b < 4 else NSMP
                    dst = ps_s[:n, b // 2, (b % 2) * 512:(b % 2) * 512 + AW] if b < 4 else ps_t[:n, 0:AW]
                    cols = slice(SEQ - CACHE + b * P, SEQ - CACHE + b * P + n)
                    for h in range(HEADS):
                        c = slice(h * HD, (h + 1) * HD)
                        pe.matmul(dst[:, c], k_hi[:, h, cols], ident_r[:], start=True, stop=False)
                        last = pe.matmul(dst[:, c], k_lo[:, h, cols], ident_r[:], start=False, stop=True)
                    last.then_inc(rows_turned, 1)


def ssd_and_gmlp(nc, d):
    with nc.cleanup_on_exit(), ExitStack() as ctx:
        m = Place(nc, ctx, "sg")
        NC_ = NT + 1
        ident, upper, ones = m.sb("ident", [P, P]), m.sb("upper", [P, P]), m.sb("ones", [P, P])
        dt = m.sb("dt", [P, NC_, HEADS])
        e, w2, num, den = m.sb("e", [P, NC_, HEADS]), m.sb("w2", [P, NC_, HEADS]), m.sb("num", [P, NC_, HEADS]), m.sb("den", [P, NC_, HEADS])
        dta, ncum, ecum, dts, etot = (m.sb("dta", [P, NC_, HEADS]), m.sb("ncum", [P, NC_, HEADS]), m.sb("ecum", [P, NC_, HEADS]),
                                      m.sb("dts", [P, NC_, HEADS]), m.sb("etot", [P, NC_, HEADS]))
        dt_bias, a_row, d_row = m.sb("dt_bias", [P, HEADS]), m.sb("a_row", [P, HEADS]), m.sb("d_row", [P, HEADS])
        ws, wt, gb = m.sb("ws", [P, CG, P]), m.sb("wt", [P, CG, P]), m.sb("gb", [P, CG])
        st_in, st_out = m.sb("st_in", [P, 3, P]), m.sb("st_out", [P, 2, 3, P])
        state = m.sb("state", [P, AW])
        decayed = m.sb("decayed", [P, AW])
        xbc = m.sb("xbc", [P, 4, NXBC, P])
        z, uv = m.sb("z", [P, 4, AW]), m.sb("uv", [P, 4, 2 * CW])
        dta_t, ncum_t = m.sb("dta_t", [P, 2, HEADS]), m.sb("ncum_t", [P, 2, HEADS])
        rows = m.sb("rows", [P, 2, AW + 2 * STATE])
        xdt, xds, xd = m.sb("xdt", [P, 2, AW]), m.sb("xds", [P, 2, AW]), m.sb("xd", [P, 2, AW])
        seg, cbm, mix = m.sb("seg", [P, 2, HEADS, P]), m.sb("cbm", [P, 2, 2, P]), m.sb("mix", [P, 2, HEADS, P])
        y1, y2, y3 = m.sb("y1", [P, AW]), m.sb("y2", [P, AW]), m.sb("y3", [P, AW])
        ob, oc = m.sb("ob", [P, 2, AW]), m.sb("oc", [P, 2, CW])
        ps_a, ps_r = m.ps("ps_a", [P, 1024]), m.ps("ps_r", [P, 1024])
        ps_c, ps_off, ps_diag, ps_st = m.ps("ps_c", [P, 512]), m.ps("ps_off", [P, 512]), m.ps("ps_diag", [P, 512]), m.ps("ps_st", [P, 512])

        zero_done, ident_done, const_done = m.sem("zero_done"), m.sem("ident_done"), m.sem("const_done")
        small_loaded, prep, prep_done, prep_act, prep_pe = (m.sem("small_loaded"), m.sem("prep"), m.sem("prep_done"), m.sem("prep_act"),
                                                           m.sem("prep_pe"))
        loaded = [m.sem(f"loaded{b}") for b in range(4)]
        dta_done, cum_done, rows_turned, cb_done = m.sem("dta_done"), m.sem("cum_done"), m.sem("rows_turned"), m.sem("cb_done")
        rows_done, seg_done, exp_done, cbm_done, mix_done = (m.sem("rows_done"), m.sem("seg_done"), 
                                                                        m.sem("exp_done"), m.sem("cbm_done"), m.sem("mix_done"))
        scaled, off_done, st_done, diag_done, gm_done = m.sem("scaled"), m.sem("off_done"), m.sem("st_done"), m.sem("diag_done"), m.sem("gm_done")
        y1_done, y2_done, y3_done, ob_done, oc_done = m.sem("y1_done"), m.sem("y2_done"), m.sem("y3_done"), m.sem("ob_done"), m.sem("oc_done")
        decayed_done, state_done = m.sem("decayed_done"), m.sem("state_done")
        o_stored = [m.sem("o_stored0"), m.sem("o_stored1")]
        ncum_done, dta_all_done = m.sem("ncum_done"), m.sem("dta_all_done")
        fin_turned, fin_done, fin_stored, init_turned = m.sem("fin_turned"), m.sem("fin_done"), m.sem("fin_stored"), m.sem("init_turned")

        def chunks(eng, step):
            for t in range(4):
                step(t, t, t % 2, 0)
            with eng.Fori(1, 3) as i:
                for b in range(4):
                    step(4 * i + b, b, b % 2, i)
            for t in range(12, NC_):
                step(t, t % 4, t % 2, t // 4)

        def col(t):
            return slice(t, t + 1) if isinstance(t, int) else bass.ds(t, 1)

        def per_head(a, t):
            return a[:, col(t), :].rearrange("p a h -> p (a h)").unsqueeze(2).to_broadcast([P, HEADS, HD])

        def by_head(a):
            return a.rearrange("p (h c) -> p h c", h=HEADS)

        with nc.Block() as block:
            @block.sync
            def _(sp):
                sp.dma_start(dt[:, 0:NT, :], d["dt_rows"][0:SEQ, :].rearrange("(t p) h -> p t h", p=P)).then_inc(small_loaded, 16)
                sp.dma_start(dt[:NSMP, NT, :], d["dt_rows"][SEQ:ROWS, :]).then_inc(small_loaded, 16)
                sp.dma_start(dt_bias[:], bc_row(d["ssm_dt_bias"], HEADS)).then_inc(small_loaded, 16)
                sp.dma_start(a_row[:], bc_row(d["ssm_a_log"], HEADS)).then_inc(small_loaded, 16)
                sp.dma_start(d_row[:], bc_row(d["ssm_d"], HEADS)).then_inc(small_loaded, 16)
                sp.dma_start(ws[:], d["gmlp_w"].rearrange("g i j -> i g j")).then_inc(small_loaded, 16)
                sp.dma_start(gb[:], d["gmlp_b"].rearrange("g i -> i g"), allow_slow_non_contiguous=True).then_inc(small_loaded, 16)
                sp.dma_start(st_in[:], d["state_ssm"].rearrange("(m p) n -> p m n", p=P)).then_inc(small_loaded, 16)

                def load(t, b):
                    n = n_rows(t)
                    sp.dma_start(xbc[:, b, :, :n], d["xbc_t"][:, :, tile_rows(t)]).then_inc(loaded[b], 16)
                    sp.dma_start(z[:n, b, :], d["z_rows"][tile_rows(t), :]).then_inc(loaded[b], 16)
                    sp.dma_start(uv[:n, b, :], d["uv_rows"][tile_rows(t), :]).then_inc(loaded[b], 16)

                for t in range(4):
                    load(t, t)

                def step(t, b, p, i):
                    n = n_rows(t)
                    sp.wait_ge(oc_done, t + 1)
                    alone(sp)
                    sp.dma_start(d["mixed"][tile_rows(t), 2 * AW:], oc[:n, p, :]).then_inc(o_stored[p], 16)
                    sp.wait_ge(ob_done, t + 1)
                    alone(sp)
                    sp.dma_start(d["mixed"][tile_rows(t), AW:2 * AW], ob[:n, p, :]).then_inc(o_stored[p], 16)
                    if not isinstance(t, int) or t + 4 <= NT:
                        load(t + 4, b)
                chunks(sp, step)
                sp.wait_ge(o_stored[0], 32 * 9)
                sp.wait_ge(o_stored[1], 32 * 8)

            @block.gpsimd
            def _(pool):
                make_identity(pool, ident, zero_done, ident_done)
                pool.memset(ones[:], 1.0).then_inc(zero_done, 1)
                pool.wait_ge(zero_done, 2)
                pool.affine_select(out=upper[:], in_=ones[:], compare_op=ALU.is_ge, fill=0.0, base=0,
                                   pattern=[[1, P]], channel_multiplier=-1).then_inc(const_done, 1)

                def scale(t, p):
                    n = n_rows(t)
                    pool.wait_ge(rows_done, t + 1)
                    if not (isinstance(t, int) and t < 2):
                        pool.wait_ge(diag_done, t - 1)
                        pool.wait_ge(y2_done, t - 1)
                        alone(pool)
                    x = by_head(rows[:n, p, 0:AW])
                    pool.tensor_tensor(by_head(xdt[:n, p, :]), x, per_head(dt, t)[:n], ALU.mult)
                    pool.tensor_tensor(by_head(xds[:n, p, :]), x, per_head(dts, t)[:n], ALU.mult)
                    pool.tensor_tensor(by_head(xd[:n, p, :]), x, d_row[:n, :].unsqueeze(2).to_broadcast([n, HEADS, HD]),
                                       ALU.mult).then_inc(scaled, 1)

                def back(t, b, p, i):
                    n = n_rows(t)
                    pool.wait_ge(state_done, NT + 2 if isinstance(t, int) and t == NT else t + 1)
                    pool.tensor_tensor(by_head(decayed[:]), by_head(state[:]), per_head(etot, t), ALU.mult).then_inc(decayed_done, 1)
                    pool.wait_ge(y1_done, t + 1)
                    wait_if(pool, y3_done, t)
                    pool.tensor_tensor(y2[:n, :], y1[:n, :], xd[:n, p, :], ALU.add).then_inc(y2_done, 1)
                    pool.wait_ge(y3_done, t + 1)
                    if not (isinstance(t, int) and t < 2):
                        pool.wait_ge(o_stored[p], 32 * (2 * i + b // 2))
                    pool.tensor_tensor(ob[:n, p, :], y3[:n, :], z[:n, b, :], ALU.mult).then_inc(ob_done, 1)

                pool.wait_ge(prep_done, 1)
                scale(0, 0)

                def step(t, b, p, i):
                    if not isinstance(t, int) or t + 1 <= NT:
                        scale(t + 1, 1 - p)
                    back(t, b, p, i)
                chunks(pool, step)
                pool.wait_ge(fin_done, 1)
                pool.dma_start(d["prompt_ssm"].rearrange("(m p) n -> p m n", p=P), st_out[:, 0]).then_inc(fin_stored, 16)
                pool.wait_ge(fin_done, 2)
                pool.dma_start(d["sample_ssm"].rearrange("(m p) n -> p m n", p=P), st_out[:, 1]).then_inc(fin_stored, 16)
                pool.wait_ge(fin_stored, 32)

            @block.scalar
            def _(act):
                act.wait_ge(small_loaded, 128)
                act.activation(a_row[:], a_row[:], ACT.Exp).then_inc(prep_act, 1)
                act.wait_ge(prep, 2)
                act.activation(e[:], e[:], ACT.Exp).then_inc(prep_act, 1)
                act.wait_ge(ncum_done, 2)
                act.activation(ecum[:], ncum[:], ACT.Exp, scale=-1.0)
                act.activation(etot[:], ps_r[:, 0:NC_ * HEADS].rearrange("p (t h) -> p t h", h=HEADS), ACT.Exp)
                act.activation(den[:], num[:], ACT.Exp).then_inc(prep_act, 1)
                act.wait_ge(prep_done, 1)

                def front(t, p):
                    n = n_rows(t)
                    act.wait_ge(rows_turned, t + 1)
                    if not (isinstance(t, int) and t < 2):
                        act.wait_ge(scaled, t - 1)
                        act.wait_ge(st_done, t - 1)
                    act.copy(rows[:n, p, :], ps_r[:n, 0:AW + 2 * STATE]).then_inc(rows_done, 1)
                    act.wait_ge(seg_done, t + 1)
                    act.activation(seg[:n, p, :, :n], seg[:n, p, :, :n], ACT.Exp).then_inc(exp_done, 1)

                front(0, 0)

                def step(t, b, p, i):
                    if not isinstance(t, int) or t + 1 <= NT:
                        front(t + 1, 1 - p)
                chunks(act, step)
                for f in range(2):
                    act.wait_ge(fin_turned, f + 1)
                    act.copy(st_out[:, f], ps_st[:, 0:AW].rearrange("p (m n) -> p m n", m=3)).then_inc(fin_done, 1)

            @block.vector
            def _(dve):
                count = [0]

                def link(ins):
                    count[0] += 1
                    ins.then_inc(prep, 1)
                    dve.wait_ge(prep, count[0])

                dve.memset(dt[NSMP:, NT, :], 0.0)
                dve.memset(state[:], 0.0).then_inc(state_done, 1)
                dve.wait_ge(state_done, 1)
                dve.wait_ge(small_loaded, 128)
                link(dve.tensor_tensor(dt[:], dt[:], dt_bias[:].unsqueeze(1).to_broadcast([P, NC_, HEADS]), ALU.add))
                link(dve.scalar_tensor_tensor(out=e[:], in0=dt[:], scalar=-1.0, in1=dt[:], op0=ALU.mult, op1=ALU.min))
                dve.wait_ge(prep_act, 2)
                link(dve.tensor_scalar(den[:], e[:], 2.0, None, ALU.add))
                link(dve.reciprocal(den[:], den[:]))
                link(dve.tensor_tensor(e[:], e[:], den[:], ALU.mult))
                link(dve.tensor_tensor(w2[:], e[:], e[:], ALU.mult))
                link(dve.tensor_scalar(num[:], w2[:], 1.0 / 17, None, ALU.mult))
                for k in (15, 13, 11, 9, 7, 5, 3):
                    link(dve.scalar_tensor_tensor(out=num[:], in0=num[:], scalar=1.0 / k, in1=w2[:], op0=ALU.add, op1=ALU.mult))
                link(dve.scalar_tensor_tensor(out=num[:], in0=num[:], scalar=1.0, in1=e[:], op0=ALU.add, op1=ALU.mult))
                link(dve.tensor_scalar(dt[:], dt[:], 0.0, None, ALU.max))
                link(dve.scalar_tensor_tensor(out=dt[:], in0=num[:], scalar=2.0, in1=dt[:], op0=ALU.mult, op1=ALU.add))
                link(dve.tensor_scalar(a_row[:], a_row[:], -1.0, None, ALU.mult))
                link(dve.tensor_tensor(dta[:], dt[:], a_row[:].unsqueeze(1).to_broadcast([P, NC_, HEADS]), ALU.mult))
                dve.memset(dta[NSMP:, NT, :], 0.0).then_inc(dta_all_done, 1)
                dve.wait_ge(dta_all_done, 1)
                dve.wait_ge(prep_pe, 1)
                dve.tensor_scalar(ncum[:], ps_a[:, 0:NC_ * HEADS].rearrange("p (t h) -> p t h", h=HEADS), -1.0, None,
                                  ALU.mult).then_inc(ncum_done, 1)
                dve.wait_ge(ncum_done, 1)
                dve.tensor_tensor(num[:], ncum[:], ps_r[:, 0:NC_ * HEADS].rearrange("p (t h) -> p t h", h=HEADS),
                                  ALU.add).then_inc(ncum_done, 1)
                dve.wait_ge(prep_pe, 2)
                dve.tensor_tensor(wt[:], ps_off[:].rearrange("p (g j) -> p g j", g=CG),
                                  upper[:].unsqueeze(1).to_broadcast([P, CG, P]), ALU.mult)
                dve.wait_ge(prep_act, 3)
                dve.tensor_tensor(dts[:], dt[:], den[:], ALU.mult).then_inc(prep_done, 1)

                def take_dta(t, p):
                    if not (isinstance(t, int) and t < 2):
                        dve.wait_ge(cum_done, t - 1)
                        dve.wait_ge(seg_done, t - 1)
                    dve.tensor_copy(ncum_t[:, p, :], ncum[:, col(t), :].rearrange("p a h -> p (a h)"))
                    dve.tensor_copy(dta_t[:, p, :], dta[:, col(t), :].rearrange("p a h -> p (a h)")).then_inc(dta_done, 1)

                def differences(t, p):
                    n = n_rows(t)
                    dve.wait_ge(cum_done, t + 1)
                    dve.wait_ge(dta_done, t + 1)
                    if not (isinstance(t, int) and t < 2):
                        dve.wait_ge(mix_done, t - 1)
                    for h in range(HEADS):
                        last = dve.tensor_scalar(seg[:n, p, h, :n], ps_a[:n, h * P:h * P + n], ncum_t[:n, p, h:h + 1], 0.0,
                                                 ALU.add, ALU.min)
                    last.then_inc(seg_done, 1)
                    dve.wait_ge(cb_done, t + 1)
                    dve.tensor_tensor(cbm[:n, p, :, :n], ps_c[:n, 0:2 * P].rearrange("p (g l) -> p g l", g=2)[:, :, :n],
                                      upper[:n, :n].unsqueeze(1).to_broadcast([n, 2, n]), ALU.mult).then_inc(cbm_done, 1)

                def mixing(t, p):
                    n = n_rows(t)
                    dve.wait_ge(exp_done, t + 1)
                    dve.wait_ge(cbm_done, t + 1)
                    if not (isinstance(t, int) and t < 2):
                        dve.wait_ge(diag_done, t - 1)
                    for g in range(2):
                        last = dve.tensor_tensor(mix[:n, p, 3 * g:3 * g + 3, :n], seg[:n, p, 3 * g:3 * g + 3, :n],
                                                 cbm[:n, p, g, :n].unsqueeze(1).to_broadcast([n, 3, n]), ALU.mult)
                    last.then_inc(mix_done, 1)

                take_dta(0, 0)
                take_dta(1, 1)
                differences(0, 0)
                mixing(0, 0)

                def step(t, b, p, i):
                    n = n_rows(t)
                    more = not isinstance(t, int) or t + 1 <= NT
                    if not isinstance(t, int) or t + 2 <= NT:
                        take_dta(t + 2, p)
                    if more:
                        differences(t + 1, 1 - p)
                    dve.wait_ge(off_done, t + 1)
                    wait_if(dve, y2_done, t)
                    dve.tensor_tensor(by_head(y1[:n, :]), by_head(ps_off[:n, 0:AW]), per_head(ecum, t)[:n], ALU.mult).then_inc(y1_done, 1)
                    dve.wait_ge(decayed_done, t + 1)
                    dve.tensor_tensor(state[:], decayed[:], ps_st[:, 0:AW], ALU.add).then_inc(state_done, 1)
                    if more:
                        mixing(t + 1, 1 - p)
                    dve.wait_ge(diag_done, t + 1)
                    dve.wait_ge(y2_done, t + 1)
                    wait_if(dve, ob_done, t)
                    dve.tensor_tensor(y3[:n, :], y2[:n, :], ps_diag[:n, 0:AW], ALU.add).then_inc(y3_done, 1)
                    dve.wait_ge(gm_done, t + 1)
                    if not (isinstance(t, int) and t < 2):
                        dve.wait_ge(o_stored[p], 32 * (2 * i + b // 2))
                    for g in range(CG):
                        c = slice(g * 64, g * 64 + 64)
                        last = dve.scalar_tensor_tensor(out=oc[:n, p, c], in0=ps_c[:n, 2 * P + g * 64:2 * P + g * 64 + 64],
                                                        scalar=gb[:n, g:g + 1], in1=uv[:n, b, c], op0=ALU.add, op1=ALU.mult)
                    last.then_inc(oc_done, 1)
                    if isinstance(t, int) and t == NT - 1:
                        dve.wait_ge(init_turned, 1)
                        dve.tensor_copy(state[:], ps_st[:, 0:AW]).then_inc(state_done, 1)
                chunks(dve, step)

            @block.tensor
            def _(pe):
                pe.wait_ge(const_done, 1)
                pe.wait_ge(ident_done, 1)
                pe.wait_ge(small_loaded, 128)
                for g in range(CG):
                    last = pe.transpose(ps_off[:, g * P:(g + 1) * P], ws[:, g, :], ident[:])
                pe.wait_ge(dta_all_done, 1)
                flat = dta[:].rearrange("p t h -> p (t h)")
                pe.matmul(ps_a[:, 0:NC_ * HEADS], upper[:], flat, start=True, stop=True)
                pe.matmul(ps_r[:, 0:NC_ * HEADS], ones[:], flat, start=True, stop=True).then_inc(prep_pe, 1)
                pe.transpose(ps_off[:, 3 * P:4 * P], ws[:, 3, :], ident[:]).then_inc(prep_pe, 1)

                def front(t, b, p, i):
                    n = n_rows(t)
                    pe.wait_ge(loaded[b], 48 * (i + 1))
                    if isinstance(t, int) and t == 0:
                        pe.wait_ge(prep_done, 1)
                    wait_if(pe, rows_done, t)
                    for j in range(5):
                        last = pe.transpose(ps_r[:n, j * P:(j + 1) * P], xbc[:, b, j, :n], ident[:])
                    last.then_inc(rows_turned, 1)
                    pe.wait_ge(dta_done, t + 1)
                    wait_if(pe, seg_done, t)
                    for h in range(HEADS):
                        last = pe.matmul(ps_a[:n, h * P:h * P + n], dta_t[:n, p, h:h + 1].to_broadcast([n, n]), upper[:n, :n],
                                         start=True, stop=True)
                    last.then_inc(cum_done, 1)
                    wait_if(pe, cbm_done, t)
                    wait_if(pe, oc_done, t - 1)
                    for g in range(2):
                        last = pe.matmul(ps_c[:n, g * P:g * P + n], xbc[:, b, 3 + g, :n], xbc[:, b, 5 + g, :n], start=True, stop=True)
                    last.then_inc(cb_done, 1)

                front(0, 0, 0, 0)

                def step(t, b, p, i):
                    n = n_rows(t)
                    more = not isinstance(t, int) or t + 1 <= NT
                    if more:
                        front(t + 1, (b + 1) % 4, 1 - p, i + (b + 1) // 4)
                    pe.wait_ge(scaled, t + 1)
                    pe.wait_ge(state_done, NT + 2 if isinstance(t, int) and t == NT else t + 1)
                    for g in range(2):
                        c = slice(3 * g * HD, 3 * (g + 1) * HD)
                        last = pe.matmul(ps_st[:, c], rows[:n, p, AW + g * P:AW + (g + 1) * P], xds[:n, p, c], start=True, stop=True)
                    last.then_inc(st_done, 1)
                    wait_if(pe, y1_done, t)
                    for g in range(2):
                        c = slice(3 * g * HD, 3 * (g + 1) * HD)
                        last = pe.matmul(ps_off[:n, c], xbc[:, b, 5 + g, :n], state[:, c], start=True, stop=True)
                    last.then_inc(off_done, 1)
                    pe.wait_ge(mix_done, t + 1)
                    wait_if(pe, y3_done, t)
                    for h in range(HEADS):
                        c = slice(h * HD, (h + 1) * HD)
                        last = pe.matmul(ps_diag[:n, c], mix[:n, p, h, :n], xdt[:n, p, c], start=True, stop=True)
                    last.then_inc(diag_done, 1)
                    if more:
                        pe.wait_ge(cbm_done, t + 2)
                    for g in range(CG):
                        last = pe.matmul(ps_c[:n, 2 * P + g * 64:2 * P + g * 64 + 64], wt[:n, g, :n],
                                         uv[:n, b, CW + g * 64:CW + (g + 1) * 64], start=True, stop=True)
                    last.then_inc(gm_done, 1)
                    if isinstance(t, int) and t == NT - 1:
                        turn_state(NT + 1)
                        pe.wait_ge(fin_done, 1)
                        for j in range(3):
                            last = pe.transpose(ps_st[:, j * P:(j + 1) * P], st_in[:, j, :], ident[:])
                        last.then_inc(init_turned, 1)

                def turn_state(value):
                    pe.wait_ge(state_done, value)
                    for j in range(3):
                        last = pe.transpose(ps_st[:, j * P:(j + 1) * P], state[:, j * P:(j + 1) * P], ident[:])
                    last.then_inc(fin_turned, 1)
                chunks(pe, step)
                turn_state(NT + 3)


def mix_out(nc, d):
    with nc.cleanup_on_exit(), ExitStack() as ctx:
        m = Place(nc, ctx, "mo")
        segs = [(0, AW), (AW, AW), (2 * AW, CW)]
        w_raw = m.sb("w_raw", [P, KD, D])
        w_hi, w_lo = m.sb("w_hi", [P, KD, D], F32R), m.sb("w_lo", [P, KD, D], F32R)
        g_mix, g_ln, b_ln = m.sb("g_mix", [P, D]), m.sb("g_ln", [P, D]), m.sb("b_ln", [P, D])
        mx, x, y = m.sb("mx", [P, 2, D]), m.sb("x", [P, 2, D]), m.sb("y", [P, 2, D])
        sq, ss, rms, inv = m.sb("sq", [P, D]), m.sb("ss", [P, 3]), m.sb("rms", [P, 3]), m.sb("inv", [P, 3])
        mt_hi, mt_lo = m.sb("mt_hi", [P, 2, KD, P], F32R), m.sb("mt_lo", [P, 2, KD, P], F32R)
        yt = m.sb("yt", [P, 2, KD, P])
        stats, mv, sd, rs = m.sb("stats", [P, 2, 6]), m.sb("mv", [P, 2]), m.sb("sd", [P, 2]), m.sb("rs", [P, 1])
        ident = m.sb("ident", [P, P])
        ps_m, ps_y, ps_t = m.ps("ps_m", [P, KD, P]), m.ps("ps_y", [P, 2, D]), m.ps("ps_t", [P, KD, P])

        zero_done, ident_done = m.sem("zero_done"), m.sem("ident_done")
        w_loaded = [m.sem(f"w_loaded{k}") for k in range(KD)]
        w_hi_done, w_lo_done, vec_loaded, g_mix_loaded = m.sem("w_hi_done"), m.sem("w_lo_done"), m.sem("vec_loaded"), m.sem("g_mix_loaded")
        mx_loaded, x_loaded = [m.sem("mx_loaded0"), m.sem("mx_loaded1")], [m.sem("x_loaded0"), m.sem("x_loaded1")]
        sq_done, ms_done, rms_done, inv_done, mx_done = (m.sem("sq_done"), m.sem("ms_done"), m.sem("rms_done"),
                                                                 m.sem("inv_done"), m.sem("mx_done"))
        m_turned, m_hi_done, m_lo_done, mm_done = m.sem("m_turned"), m.sem("m_hi_done"), m.sem("m_lo_done"), m.sem("mm_done")
        sum_done, bn_done, aggr_done, var_done, sd_done = (m.sem("sum_done"), m.sem("bn_done"), m.sem("aggr_done"), m.sem("var_done"),
                                                           m.sem("sd_done"))
        rs_done, gain_done, y_done = m.sem("rs_done"), m.sem("gain_done"), m.sem("y_done")
        y_turned, yt_done = m.sem("y_turned"), m.sem("yt_done")
        smp_stored = m.sem("smp_stored")
        y_stored, yt_stored = [m.sem("y_stored0"), m.sem("y_stored1")], [m.sem("yt_stored0"), m.sem("yt_stored1")]

        def tiles(eng, step):
            step(0, 0, 0)
            step(1, 1, 0)
            with eng.Fori(1, 7) as i:
                step(2 * i, 0, i)
                step(2 * i + 1, 1, i)
            for t in (14, 15, 16):
                step(t, t % 2, t // 2)

        def early(t):
            return isinstance(t, int) and t < 2

        def exists(t, ahead):
            return not isinstance(t, int) or t + ahead <= NT

        with nc.Block() as block:
            @block.sync
            def _(sp):
                def load_mx(t, p):
                    n = n_rows(t)
                    if not early(t):
                        sp.wait_ge(m_turned, t - 1)
                    alone(sp) if not early(t) else None
                    sp.dma_start(mx[:n, p, :], d["mixed"][tile_rows(t), :]).then_inc(mx_loaded[p], 16)

                def load_x(t, p):
                    n = n_rows(t)
                    if not early(t):
                        sp.wait_ge(sum_done, t - 1)
                    alone(sp) if not early(t) else None
                    sp.dma_start(x[:n, p, :], d["x_rows"][tile_rows(t), :]).then_inc(x_loaded[p], 16)

                load_mx(0, 0)
                load_mx(1, 1)
                for k in range(KD):
                    sp.dma_start(w_raw[:, k, :], d["w_out"][k * P:(k + 1) * P, :]).then_inc(w_loaded[k], 16)
                load_x(0, 0)
                load_x(1, 1)

                def step(t, p, i):
                    if exists(t, 2):
                        load_mx(t + 2, p)
                    if exists(t, 2):
                        load_x(t + 2, p)
                tiles(sp, step)
                rows = slice(SEQ, ROWS)
                sp.wait_ge(y_done, NT + 1)
                sp.dma_start(d["x1_rows"][rows, :], y[:NSMP, 0, :]).then_inc(smp_stored, 16)
                sp.wait_ge(yt_done, NT + 1)
                sp.dma_start(d["x1t"][:, :, rows], yt[:, 0, :, :NSMP]).then_inc(smp_stored, 16)
                sp.wait_ge(smp_stored, 32)

            @block.gpsimd
            def _(pool):
                make_identity(pool, ident, zero_done, ident_done)
                pool.dma_start(g_mix[:], bc_row(d["mix_norm_g"], D)).then_inc(g_mix_loaded, 16)
                pool.dma_start(g_ln[:], bc_row(d["ln1_g"], D)).then_inc(vec_loaded, 16)
                pool.dma_start(b_ln[:], bc_row(d["ln1_b"], D)).then_inc(vec_loaded, 16)

                def store_yt(t, p):
                    n = n_rows(t)
                    pool.wait_ge(yt_done, t + 1)
                    alone(pool)
                    pool.dma_start(d["x1t"][:, :, tile_rows(t)], yt[:, p, :, :n]).then_inc(yt_stored[p], 16)

                def step(t, p, i):
                    n = n_rows(t)
                    if not (isinstance(t, int) and t == NT):
                        pool.wait_ge(y_done, t + 1)
                        alone(pool)
                        pool.dma_start(d["x1_rows"][tile_rows(t), :], y[:n, p, :]).then_inc(y_stored[p], 16)
                    if not (isinstance(t, int) and t == 0):
                        store_yt(t - 1, 1 - p)
                tiles(pool, step)
                for p in range(2):
                    pool.wait_ge(y_stored[p], 16 * 8)
                    pool.wait_ge(yt_stored[p], 16 * 8)

            @block.scalar
            def _(act):
                def squares(t, p, i):
                    n = n_rows(t)
                    act.wait_ge(mx_loaded[p], 16 * (i + 1))
                    for s, (c, w) in enumerate(segs):
                        last = act.activation(sq[:n, c:c + w], mx[:n, p, c:c + w], ACT.Square, accum_out=ss[:n, s:s + 1])
                    last.then_inc(sq_done, 1)
                    act.wait_ge(ms_done, t + 1)
                    act.activation(rms[:n, :], ss[:n, :], ACT.Sqrt).then_inc(rms_done, 1)

                def hi_m(t, p):
                    n = n_rows(t)
                    act.wait_ge(m_turned, t + 1)
                    if not early(t):
                        act.wait_ge(mm_done, t - 1)
                    act.copy(mt_hi[:, p, :, :n], ps_m[:, :, :n]).then_inc(m_hi_done, 1)

                def take_yt(t, p, i):
                    n = n_rows(t)
                    act.wait_ge(y_turned, t + 1)
                    if not early(t):
                        act.wait_ge(yt_stored[p], 16 * i)
                    act.copy(yt[:, p, :, :n], ps_t[:, :, :n]).then_inc(yt_done, 1)

                def weights_hi(ks):
                    for k in ks:
                        act.wait_ge(w_loaded[k], 16)
                        act.copy(w_hi[:, k, :], w_raw[:, k, :]).then_inc(w_hi_done, 1)

                squares(0, 0, 0)
                weights_hi(range(0, 3))
                hi_m(0, 0)
                weights_hi(range(3, 5))
                squares(1, 1, 0)
                weights_hi(range(5, KD))

                def step(t, p, i):
                    n = n_rows(t)
                    if exists(t, 1):
                        hi_m(t + 1, 1 - p)
                    if exists(t, 2):
                        squares(t + 2, p, i + 1)
                    act.wait_ge(var_done, t + 1)
                    act.activation(sd[:n, 1:2], sd[:n, 0:1], ACT.Sqrt).then_inc(sd_done, 1)
                    if not (isinstance(t, int) and t == 0):
                        take_yt(t - 1, 1 - p, i - 1 + p)
                tiles(act, step)
                take_yt(NT, 0, NT // 2)

            @block.vector
            def _(dve):
                def scale(t, p):
                    n = n_rows(t)
                    dve.wait_ge(sq_done, t + 1)
                    dve.tensor_scalar(ss[:n, 0:2], ss[:n, 0:2], 1.0 / AW, EPS, ALU.mult, ALU.add)
                    dve.tensor_scalar(ss[:n, 2:3], ss[:n, 2:3], 1.0 / CW, EPS, ALU.mult, ALU.add).then_inc(ms_done, 1)
                    dve.wait_ge(rms_done, t + 1)
                    dve.reciprocal(inv[:n, :], rms[:n, :]).then_inc(inv_done, 1)
                    dve.wait_ge(inv_done, t + 1)
                    if isinstance(t, int) and t == 0:
                        dve.wait_ge(g_mix_loaded, 16)
                    for s, (c, w) in enumerate(segs):
                        last = dve.scalar_tensor_tensor(out=mx[:n, p, c:c + w], in0=mx[:n, p, c:c + w], scalar=inv[:n, s:s + 1],
                                                        in1=g_mix[:n, c:c + w], op0=ALU.mult, op1=ALU.mult)
                    last.then_inc(mx_done, 1)

                def lo_m(t, p):
                    n = n_rows(t)
                    dve.wait_ge(m_hi_done, t + 1)
                    dve.tensor_tensor(mt_lo[:, p, :, :n], ps_m[:, :, :n], mt_hi[:, p, :, :n].bitcast(F32),
                                      ALU.subtract).then_inc(m_lo_done, 1)

                def weights_lo(ks):
                    for k in ks:
                        dve.wait_ge(w_hi_done, k + 1)
                        dve.tensor_tensor(w_lo[:, k, :], w_raw[:, k, :], w_hi[:, k, :].bitcast(F32),
                                          ALU.subtract).then_inc(w_lo_done, 1)

                scale(0, 0)
                weights_lo(range(0, 3))
                lo_m(0, 0)
                weights_lo(range(3, 5))
                scale(1, 1)
                weights_lo(range(5, KD))

                def step(t, p, i):
                    n = n_rows(t)
                    if exists(t, 1):
                        lo_m(t + 1, 1 - p)
                    if exists(t, 2):
                        scale(t + 2, p)
                    dve.wait_ge(x_loaded[p], 16 * (i + 1))
                    dve.wait_ge(mm_done, t + 1)
                    if not early(t):
                        dve.wait_ge(y_stored[p], 16 * i)
                        dve.wait_ge(y_turned, t - 1)
                    dve.scalar_tensor_tensor(out=y[:n, p, :], in0=x[:n, p, :], scalar=ALPHA, in1=ps_y[:n, p, :],
                                             op0=ALU.mult, op1=ALU.add).then_inc(sum_done, 1)
                    dve.wait_ge(sum_done, t + 1)
                    for c in range(2):
                        last = dve.bn_stats(stats[:n, c, :], y[:n, p, c * 512:(c + 1) * 512])
                    last.then_inc(bn_done, 1)
                    dve.wait_ge(bn_done, t + 1)
                    alone(dve)
                    dve.bn_aggr(mv[:n, :], stats[:n].rearrange("p a b -> p (a b)")).then_inc(aggr_done, 1)
                    dve.wait_ge(aggr_done, t + 1)
                    dve.tensor_scalar(sd[:n, 0:1], mv[:n, 1:2], EPS, None, ALU.add).then_inc(var_done, 1)
                    dve.wait_ge(sd_done, t + 1)
                    dve.reciprocal(rs[:n, :], sd[:n, 1:2]).then_inc(rs_done, 1)
                    dve.wait_ge(rs_done, t + 1)
                    if isinstance(t, int) and t == 0:
                        dve.wait_ge(vec_loaded, 32)
                    dve.scalar_tensor_tensor(out=y[:n, p, :], in0=y[:n, p, :], scalar=mv[:n, 0:1], in1=g_ln[:n, :],
                                             op0=ALU.subtract, op1=ALU.mult).then_inc(gain_done, 1)
                    dve.wait_ge(gain_done, t + 1)
                    dve.scalar_tensor_tensor(out=y[:n, p, :], in0=y[:n, p, :], scalar=rs[:n, :], in1=b_ln[:n, :],
                                             op0=ALU.mult, op1=ALU.add).then_inc(y_done, 1)
                tiles(dve, step)

            @block.tensor
            def _(pe):
                pe.wait_ge(ident_done, 1)

                def turn_m(t, p):
                    n = n_rows(t)
                    pe.wait_ge(mx_done, t + 1)
                    wait_if(pe, m_lo_done, t)
                    for k in range(KD):
                        last = pe.transpose(ps_m[:, k, :n], mx[:n, p, k * P:(k + 1) * P], ident[:n, :n])
                    last.then_inc(m_turned, 1)

                def turn_y(t, p):
                    n = n_rows(t)
                    pe.wait_ge(y_done, t + 1)
                    wait_if(pe, yt_done, t)
                    for k in range(KD):
                        last = pe.transpose(ps_t[:, k, :n], y[:n, p, k * P:(k + 1) * P], ident[:n, :n])
                    last.then_inc(y_turned, 1)

                turn_m(0, 0)

                def step(t, p, i):
                    n = n_rows(t)
                    first = isinstance(t, int) and t == 0
                    if exists(t, 1) and not first:
                        turn_m(t + 1, 1 - p)
                    pe.wait_ge(m_lo_done, t + 1)
                    if not early(t):
                        pe.wait_ge(sum_done, t - 1)

                    def product(c, k):
                        return products(pe, ps_y[:n, p, c:c + 512], mt_hi[:, p, k, :n], mt_lo[:, p, k, :n],
                                        w_hi[:, k, c:c + 512], w_lo[:, k, c:c + 512], k == 0, k == KD - 1)
                    if first:
                        for k in range(KD):
                            if k == 6:
                                turn_m(1, 1)
                            pe.wait_ge(w_lo_done, k + 1)
                            for c in range(0, D, 512):
                                last = product(c, k)
                    else:
                        for c in range(0, D, 512):
                            for k in range(KD):
                                last = product(c, k)
                    last.then_inc(mm_done, 1)
                    if not (isinstance(t, int) and t == 0):
                        turn_y(t - 1, 1 - p)
                tiles(pe, step)
                turn_y(NT, 0)


def ffn_up(nc, d):
    with nc.cleanup_on_exit(), ExitStack() as ctx:
        m = Place(nc, ctx, "fu")
        H = 2
        GW = 424
        NG = -(-ROWS // GW)
        REST = SEQ - (NG - 1) * GW
        LASTW = REST + NSMP
        U = 2 * NG
        MT = 2 * KF
        xt_hi, xt_lo = m.sb("xt_hi", [P, KD, H + ROWS], F32R), m.sb("xt_lo", [P, KD, H + ROWS], F32R)
        xt = m.sb("xt", [P, 2, KD, GW])
        w_raw = m.sb("w_raw", [P, 2, KD, P])
        w_hi, w_lo = m.sb("w_hi", [P, 2, KD, P], F32R), m.sb("w_lo", [P, 2, KD, P], F32R)
        vec_rows, vecs = m.sb("vec_rows", [2 * MT, 3, P]), m.sb("vecs", [P, 6, MT])
        smp = m.sb("smp", [P, 2, H + NSMP])
        conv = m.sb("conv", [P, 2, GW])
        gate, h = m.sb("gate", [P, NG, GW]), m.sb("h", [P, 2, GW])
        states, states_t = m.sb("states", [P, 4, MT]), m.sb("states_t", [2 * MT, 2, P])
        ident = m.sb("ident", [P, P])
        ps_y = m.ps("ps_y", [P, 8, 512])

        zero_done, ident_done = m.sem("zero_done"), m.sem("ident_done")
        vec_loaded, vec_turned, vec_done, edge_done = m.sem("vec_loaded"), m.sem("vec_turned"), m.sem("vec_done"), m.sem("edge_done")
        xt_loaded = [m.sem(f"xt_loaded{g}") for g in range(NG)]
        second_xt_loaded = m.sem("second_xt_loaded")
        xt_hi_done, xt_lo_done = m.sem("xt_hi_done"), m.sem("xt_lo_done")
        w_loaded = [m.sem("w_loaded0"), m.sem("w_loaded1")]
        w_hi_done, w_lo_done = m.sem("w_hi_done"), m.sem("w_lo_done")
        mm_done, smp_done, tap0_done, smp_in_done, tap1_done, conv_done, gate_done, h_done = (
            m.sem("mm_done"), m.sem("smp_done"), m.sem("tap0_done"), m.sem("smp_in_done"), m.sem("tap1_done"), m.sem("conv_done"),
            m.sem("gate_done"), m.sem("h_done"))
        h_stored = [m.sem("h_stored0"), m.sem("h_stored1")]
        states_turned, states_done, states_stored = m.sem("states_turned"), m.sem("states_done"), m.sem("states_stored")

        def pairs(eng, step):
            step(0, True)
            with eng.Fori(1, KF - 1) as j:
                step(j, True)
            step(KF - 1, False)

        def half_features(e):
            return slice(e * KD // 2, (e + 1) * KD // 2)

        def split_parts(e):
            g = max(e - 1, 0)
            ks = half_features(e) if e < 2 else slice(0, KD)
            return g, ks, slice(H + g * GW, H + g * GW + gwidth(g))

        def group(j, v):
            return (v % 2, v // 2) if isinstance(j, int) and j == 0 else (v // NG, v % NG)

        def place(j, half, g):
            return 2 * g + half if isinstance(j, int) and j == 0 else NG * half + g

        def split_next(j, v):
            if isinstance(j, int) and j == 0:
                return {U - 2: 0, U - 1: 1}.get(v)
            return {NG: 0, U - 1: 1}.get(v)

        def one(a, m_):
            return a[:, m_:m_ + 1] if isinstance(m_, int) else a[:, bass.ds(m_, 1)]

        def gwidth(g):
            return LASTW if g == NG - 1 else GW

        def stored_before(j, g):
            return ((NG + 1) // 2 if g % 2 == 0 else NG // 2) * j + g // 2

        with nc.Block() as block:
            @block.sync
            def _(sp):
                def load_w(j, half):
                    c = j * P + half * DFF
                    cols = slice(c, c + P) if isinstance(c, int) else bass.ds(c, P)
                    sp.dma_start(w_raw[:, half], d["ffn_w_in"][:, cols].rearrange("(k p) c -> p k c", p=P)).then_inc(w_loaded[half], 16)

                def load_xt(g):
                    if g >= 2:
                        sp.wait_ge(xt_lo_done, g)
                    n = gwidth(g)
                    sp.dma_start(xt[:, g % 2, :, :n], d["x1t"][:, :, g * GW:g * GW + n]).then_inc(xt_loaded[g], 16)

                taps = d["ffn_conv_w"].rearrange("c (m p) -> (c m) p", p=P)
                sp.dma_start(vec_rows[:, 0, :], taps[0:2 * MT, :]).then_inc(vec_loaded, 16)
                sp.dma_start(vec_rows[0:MT, 1, :], taps[2 * MT:3 * MT, :]).then_inc(vec_loaded, 16)
                sp.dma_start(vec_rows[MT:2 * MT, 1, :], d["ffn_conv_b"].rearrange("(m p) -> m p", p=P)).then_inc(vec_loaded, 16)
                sp.dma_start(vec_rows[:, 2, :], d["state_ffn_conv"].rearrange("c (m p) -> (c m) p", p=P)).then_inc(vec_loaded, 16)
                load_w(0, 0)
                for ks, done in ((half_features(0), xt_loaded[0]), (half_features(1), second_xt_loaded)):
                    sp.dma_start(xt[:, 0, ks, :], d["x1t"][:, ks, 0:GW]).then_inc(done, 16)
                load_w(0, 1)
                for g in range(1, NG):
                    load_xt(g)

                def step(j, more):
                    for half in range(2 if more else 0):
                        sp.wait_ge(w_hi_done, 2 * j + half + 1)
                        sp.wait_ge(w_lo_done, 2 * j + half + 1)
                        alone(sp)
                        load_w(j + 1, half)
                    for g in range(NG):
                        sp.wait_ge(h_done, NG * j + g + 1)
                        alone(sp)
                        k = slice(j, j + 1) if isinstance(j, int) else bass.ds(j, 1)
                        sp.dma_start(d["h_t"][:, k, g * GW:g * GW + gwidth(g)].rearrange("p a c -> p (a c)"),
                                     h[:, g % 2, :gwidth(g)]).then_inc(h_stored[g % 2], 16)
                pairs(sp, step)
                sp.wait_ge(h_stored[0], 16 * stored_before(KF, 0))
                sp.wait_ge(h_stored[1], 16 * stored_before(KF, 1))
                sp.wait_ge(states_done, 2)
                sp.dma_start(d["prompt_ffn_conv"].rearrange("c (m p) -> (c m) p", p=P), states_t[:, 0, :]).then_inc(states_stored, 16)
                sp.dma_start(d["sample_ffn_conv"].rearrange("c (m p) -> (c m) p", p=P), states_t[:, 1, :]).then_inc(states_stored, 16)
                sp.wait_ge(states_stored, 32)

            @block.gpsimd
            def _(pool):
                pool.memset(xt_hi[:, :, 0:H].bitcast(F32), 0.0)
                pool.memset(xt_lo[:, :, 0:H].bitcast(F32), 0.0).then_inc(edge_done, 1)
                make_identity(pool, ident, zero_done, ident_done)

                def step(j, more):
                    for g in range(NG):
                        n = gwidth(g)
                        v = place(j, 1, g)
                        pool.wait_ge(conv_done, U * j + v + 1)
                        pool.wait_ge(gate_done, NG * j + g + 1)
                        if not (isinstance(j, int) and j == 0 and g < 2):
                            pool.wait_ge(h_stored[g % 2], 16 * stored_before(j, g))
                        pool.tensor_tensor(h[:, g % 2, :n], conv[:, v % 2, :n], gate[:, g, :n], ALU.mult).then_inc(h_done, 1)
                pairs(pool, step)

            @block.scalar
            def _(act):
                def split_hi(j, half):
                    act.wait_ge(w_loaded[half], 16 * (j + 1))
                    if isinstance(j, int) and j == 1:
                        act.wait_ge(mm_done, place(0, half, NG - 1) + 1)
                    else:
                        wait_if(act, mm_done, U * (j - 1) + NG * (half + 1))
                    act.copy(w_hi[:, half], w_raw[:, half]).then_inc(w_hi_done, 1)

                def split_xt_hi(e):
                    g, ks, cols = split_parts(e)
                    act.wait_ge(second_xt_loaded if e == 1 else xt_loaded[g], 16)
                    act.copy(xt_hi[:, ks, cols], xt[:, g % 2, ks, :gwidth(g)]).then_inc(xt_hi_done, 1)

                act.wait_ge(vec_turned, 1)
                act.copy(vecs[:].rearrange("p a b -> p (a b)"), ps_y[:, 0, 0:6 * MT]).then_inc(vec_done, 1)
                act.wait_ge(vec_done, 1)
                split_hi(0, 0)
                split_xt_hi(0)
                split_xt_hi(1)
                split_hi(0, 1)

                def step(j, more):
                    for v in range(U):
                        half, g = group(j, v)
                        u = U * j + v
                        mt = j + half * KF
                        n = REST if g == NG - 1 else GW
                        if isinstance(j, int) and j == 0 and half == 0 and g + 1 < NG:
                            split_xt_hi(g + 2)
                        act.wait_ge(mm_done, u + 1)
                        if isinstance(j, int) and j == 0:
                            wait_if(act, (gate_done, h_done)[half], g)
                        else:
                            if v < 2:
                                act.wait_ge(h_done, NG * j)
                            if v >= NG + 2:
                                act.wait_ge(h_done, NG * j + v - NG - 1)
                            if 2 <= v < NG + 2:
                                act.wait_ge(gate_done, NG * j + v - 1)
                        if g == NG - 1:
                            act.copy(smp[:, half, H:], ps_y[:, v % 8, H + REST:H + LASTW])
                            last2 = ps_y[:, v % 8, REST:REST + 2 * NSMP].rearrange("p (a b) -> p a b", b=NSMP)[:, :, 0:2]
                            act.copy(one_state(mt), last2).then_inc(smp_done, 1)
                        alone(act)
                        act.activation(conv[:, v % 2, :n], ps_y[:, v % 8, 0:n], ACT.Identity,
                                       bias=one(vecs[:, 3, :], mt), scale=one(vecs[:, 0, :], mt)).then_inc(tap0_done, 1)
                        if half == 0:
                            act.wait_ge(conv_done, u + 1)
                            wait_if(act, h_done, NG * (j - 1) + g + 1)
                            act.activation(gate[:, g, :gwidth(g)], conv[:, v % 2, :gwidth(g)], ACT.Silu).then_inc(gate_done, 1)
                        if more and split_next(j, v) is not None:
                            split_hi(j + 1, split_next(j, v))

                def one_state(mt):
                    a = states[:, :, mt:mt + 1] if isinstance(mt, int) else states[:, :, bass.ds(mt, 1)]
                    return a.rearrange("p (x y) b -> p x (y b)", x=2)

                pairs(act, step)
                act.wait_ge(states_turned, 1)
                act.copy(states_t[:, 0, :], ps_y[0:2 * MT, 0, 0:P]).then_inc(states_done, 1)
                act.copy(states_t[:, 1, :], ps_y[0:2 * MT, 0, P:2 * P]).then_inc(states_done, 1)

            @block.vector
            def _(dve):
                def split_lo(j, half):
                    dve.wait_ge(w_hi_done, 2 * j + half + 1)
                    dve.tensor_tensor(w_lo[:, half], w_raw[:, half], w_hi[:, half].bitcast(F32), ALU.subtract).then_inc(w_lo_done, 1)

                def split_xt_lo(e):
                    g, ks, cols = split_parts(e)
                    dve.wait_ge(xt_hi_done, e + 1)
                    dve.tensor_tensor(xt_lo[:, ks, cols], xt[:, g % 2, ks, :gwidth(g)], xt_hi[:, ks, cols].bitcast(F32),
                                      ALU.subtract).then_inc(xt_lo_done, 1)

                split_lo(0, 0)
                split_xt_lo(0)
                split_xt_lo(1)
                split_lo(0, 1)
                dve.wait_ge(vec_done, 1)

                def step(j, more):
                    for v in range(U):
                        half, g = group(j, v)
                        u = U * j + v
                        mt = j + half * KF
                        n = REST if g == NG - 1 else GW
                        c, y = conv[:, v % 2], ps_y[:, v % 8]
                        if isinstance(j, int) and j == 0 and half == 0 and g + 1 < NG:
                            split_xt_lo(g + 2)
                        w0, w1, w2, b = (one(vecs[:, e, :], mt) for e in (0, 1, 2, 3))
                        dve.wait_ge(tap0_done, u + 1)
                        if g == NG - 1:
                            dve.wait_ge(smp_done, 2 * j + half + 1)
                            s = smp[:, half]
                            m_ = slice(mt, mt + 1) if isinstance(mt, int) else bass.ds(mt, 1)
                            dve.tensor_copy(s[:, 0:H], vecs[:, 4:6, m_].rearrange("p a b -> p (a b)")).then_inc(smp_in_done, 1)
                            dve.wait_ge(smp_in_done, 4 * (2 * j + half) + 1)
                            cs = c[:, REST:LASTW]
                            dve.tensor_scalar(cs, s[:, 0:NSMP], w0, b, ALU.mult, ALU.add).then_inc(smp_in_done, 1)
                            dve.wait_ge(smp_in_done, 4 * (2 * j + half) + 2)
                            dve.scalar_tensor_tensor(out=cs, in0=s[:, 1:1 + NSMP], scalar=w1, in1=cs, op0=ALU.mult,
                                                     op1=ALU.add).then_inc(smp_in_done, 1)
                            dve.wait_ge(smp_in_done, 4 * (2 * j + half) + 3)
                            dve.scalar_tensor_tensor(out=cs, in0=s[:, 2:2 + NSMP], scalar=w2, in1=cs, op0=ALU.mult,
                                                     op1=ALU.add).then_inc(smp_in_done, 1)
                        dve.scalar_tensor_tensor(out=c[:, :n], in0=y[:, 1:1 + n], scalar=w1, in1=c[:, :n], op0=ALU.mult,
                                                 op1=ALU.add).then_inc(tap1_done, 1)
                        dve.wait_ge(tap1_done, u + 1)
                        dve.scalar_tensor_tensor(out=c[:, :n], in0=y[:, 2:2 + n], scalar=w2, in1=c[:, :n], op0=ALU.mult,
                                                 op1=ALU.add).then_inc(conv_done, 1)
                        if more and split_next(j, v) is not None:
                            split_lo(j + 1, split_next(j, v))
                pairs(dve, step)

            @block.tensor
            def _(pe):
                pe.wait_ge(ident_done, 1)
                pe.wait_ge(vec_loaded, 64)
                for e in range(3):
                    last = pe.transpose(ps_y[:, 0, 2 * MT * e:2 * MT * (e + 1)], vec_rows[:, e, :], ident[0:2 * MT, 0:2 * MT])
                last.then_inc(vec_turned, 1)
                pe.wait_ge(vec_done, 1)
                pe.wait_ge(edge_done, 1)

                def step(j, more):
                    for v in range(U):
                        half, g = group(j, v)
                        if isinstance(j, int) and j == 0 and half == 0:
                            pe.wait_ge(xt_lo_done, g + 2 if g else 1)
                        if g == 0:
                            pe.wait_ge(w_lo_done, 2 * j + half + 1)
                        wait_if(pe, conv_done, U * j + v - 1)
                        n = H + gwidth(g)
                        for k in range(KD):
                            if isinstance(j, int) and j == 0 and v == 0 and k == KD // 2:
                                pe.wait_ge(xt_lo_done, 2)
                            last = products(pe, ps_y[:, v % 8, :n], w_hi[:, half, k, :], w_lo[:, half, k, :],
                                            xt_hi[:, k, g * GW:g * GW + n], xt_lo[:, k, g * GW:g * GW + n],
                                            k == 0, k == KD - 1)
                        last.then_inc(mm_done, 1)
                pairs(pe, step)
                pe.wait_ge(conv_done, U * KF)
                for e in range(2):
                    last = pe.transpose(ps_y[0:2 * MT, 0, e * P:(e + 1) * P],
                                        states[:, 2 * e:2 * e + 2, :].rearrange("p a b -> p (a b)"), ident[:])
                last.then_inc(states_turned, 1)


def ffn_down(nc, d):
    with nc.cleanup_on_exit(), ExitStack() as ctx:
        m = Place(nc, ctx, "fd")
        PK = 2
        NPC = KF // PK
        RING = 4
        w_hi, w_lo = m.sb("w_hi", [P, KF, D], F32R), m.sb("w_lo", [P, KF, D], F32R)
        h_raw = m.sb("h_raw", [P, RING, PK, P])
        h_hi, h_lo = m.sb("h_hi", [P, RING, PK, P], F32R), m.sb("h_lo", [P, RING, PK, P], F32R)
        NRAW = 4
        raw = m.sb("raw", [P, NRAW, D])
        y, g_ln, b_ln = raw[:, 0:2], raw[:, 2], raw[:, 3]
        stats, mv, sd, rs = m.sb("stats", [P, 2, 6]), m.sb("mv", [P, 2]), m.sb("sd", [P, 2]), m.sb("rs", [P, 1])
        ps_y = m.ps("ps_y", [P, 4, D])

        w_loaded = [m.sem(f"w_loaded{k}") for k in range(NRAW)]
        w_hi_done, w_lo_done, vec_loaded = m.sem("w_hi_done"), m.sem("w_lo_done"), m.sem("vec_loaded")
        h_loaded = [m.sem(f"h_loaded{s}") for s in range(RING)]
        x_loaded = [m.sem("x_loaded0"), m.sem("x_loaded1")]
        h_hi_done, h_lo_done, piece_done = m.sem("h_hi_done"), m.sem("h_lo_done"), m.sem("piece_done")
        sum_done, bn_done, aggr_done, var_done, sd_done = (m.sem("sum_done"), m.sem("bn_done"), m.sem("aggr_done"), m.sem("var_done"),
                                                           m.sem("sd_done"))
        rs_done, gain_done, y_done = m.sem("rs_done"), m.sem("gain_done"), m.sem("y_done")
        y_stored = [m.sem("y_stored0"), m.sem("y_stored1")]

        def tiles(eng, step):
            step(2, 0, 1)
            step(3, 1, 1)
            with eng.Fori(2, NT // 2) as i:
                step(2 * i, 0, i)
                step(2 * i + 1, 1, i)
            step(NT, 0, NT // 2)

        def is_tile(t, value):
            return isinstance(t, int) and t == value

        class Piece:

            def __init__(self, t, c):
                self.c, self.n = c, n_rows(t)
                if isinstance(t, int) and t < 2:
                    self.number = 2 * c + t
                    self.slot = (self.number + 2) % RING
                    self.loads = self.number // RING + 1
                else:
                    self.number = NPC * t + c
                    self.slot = c % RING
                    pair = len(range((self.slot + 2) % RING, 2 * NPC, RING))
                    each = len(range(self.slot, NPC, RING))
                    self.loads = each * t + (pair - 2 * each + c // RING + 1)

        def first_pieces():
            for c in range(NPC):
                yield range(PK * c, PK * (c + 1)), (Piece(0, c), Piece(1, c))

        with nc.Block() as block:
            @block.sync
            def _(sp):
                def load_w(k):
                    if k >= NRAW:
                        sp.wait_ge(w_hi_done, k - NRAW + 1)
                        sp.wait_ge(w_lo_done, k - NRAW + 1)
                    sp.dma_start(raw[:, k % NRAW, :], d["ffn_w_out"][k * P:(k + 1) * P, :]).then_inc(w_loaded[k % NRAW], 16)

                def load_piece(t, c):
                    x = Piece(t, c)
                    wait_if(sp, h_lo_done, x.number - 2)
                    alone(sp) if not isinstance(t, int) else None
                    sp.dma_start(h_raw[:, x.slot, :, :x.n], d["h_t"][:, PK * c:PK * (c + 1), tile_rows(t)]).then_inc(h_loaded[x.slot], 16)

                def load_x(t, p):
                    sp.dma_start(y[:n_rows(t), p, :], d["x1_rows"][tile_rows(t), :]).then_inc(x_loaded[p], 16)

                for k in range(2):
                    load_w(k)
                for c in range(NPC):
                    load_piece(0, c)
                    load_piece(1, c)
                    for k in range(PK * (c + 1), min(PK * (c + 2), KF)):
                        load_w(k)
                sp.wait_ge(w_lo_done, KF)
                load_x(0, 0)
                load_x(1, 1)
                sp.dma_start(g_ln, bc_row(d["ln2_g"], D)).then_inc(vec_loaded, 16)
                sp.dma_start(b_ln, bc_row(d["ln2_b"], D)).then_inc(vec_loaded, 16)

                def step(t, p, i):
                    for c in range(NPC):
                        load_piece(t, c)
                        if c == 8:
                            sp.wait_ge(y_stored[p], 16 * i)
                            alone(sp)
                            load_x(t, p)
                tiles(sp, step)

            @block.gpsimd
            def _(pool):
                def store(t, p):
                    n = n_rows(t)
                    pool.wait_ge(y_done, t + 1)
                    alone(pool)
                    if isinstance(t, int) and t == NT:
                        pool.dma_start(d["y_sample"], y[:n, p, :]).then_inc(y_stored[p], 16)
                    else:
                        pool.dma_start(d["y_prompt"][tile_rows(t), :], y[:n, p, :]).then_inc(y_stored[p], 16)

                store(0, 0)

                def step(t, p, i):
                    store(t - 1, 1 - p)
                tiles(pool, step)
                store(NT, 0)
                pool.wait_ge(y_stored[0], 16 * 9)
                pool.wait_ge(y_stored[1], 16 * 8)

            @block.scalar
            def _(act):
                def hi(x):
                    act.wait_ge(h_loaded[x.slot], 16 * x.loads)
                    wait_if(act, piece_done, x.number - 2)
                    act.copy(h_hi[:, x.slot, :, :x.n], h_raw[:, x.slot, :, :x.n]).then_inc(h_hi_done, 1)

                for ks, pieces in first_pieces():
                    for k in ks:
                        act.wait_ge(w_loaded[k % NRAW], 16 * (k // NRAW + 1))
                        act.copy(w_hi[:, k, :], raw[:, k % NRAW, :]).then_inc(w_hi_done, 1)
                    for x in pieces:
                        hi(x)

                def step(t, p, i):
                    for c in range(NPC):
                        hi(Piece(t, c))
                        if c == 1 and is_tile(t, 2):
                            root(0)
                        if c == 4:
                            root(t - 1)

                def root(t):
                    n = n_rows(t)
                    act.wait_ge(var_done, t + 1)
                    act.activation(sd[:n, 1:2], sd[:n, 0:1], ACT.Sqrt).then_inc(sd_done, 1)
                tiles(act, step)
                root(NT)

            @block.vector
            def _(dve):
                def lo(x):
                    dve.wait_ge(h_hi_done, x.number + 1)
                    dve.tensor_tensor(h_lo[:, x.slot, :, :x.n], h_raw[:, x.slot, :, :x.n],
                                      h_hi[:, x.slot, :, :x.n].bitcast(F32), ALU.subtract).then_inc(h_lo_done, 1)

                def norm(t, p, i):
                    n = n_rows(t)
                    dve.wait_ge(x_loaded[p], 16 * (i + 1))
                    dve.wait_ge(piece_done, 2 * NPC - 1 if is_tile(t, 0) else NPC * (t + 1))
                    dve.scalar_tensor_tensor(out=y[:n, p, :], in0=y[:n, p, :], scalar=ALPHA, in1=ps_y[:n, 2 + p if isinstance(t, int) and t < 2 else p, :],
                                             op0=ALU.mult, op1=ALU.add).then_inc(sum_done, 1)
                    dve.wait_ge(sum_done, t + 1)
                    for c in range(2):
                        last = dve.bn_stats(stats[:n, c, :], y[:n, p, c * 512:(c + 1) * 512])
                    last.then_inc(bn_done, 1)
                    dve.wait_ge(bn_done, t + 1)
                    alone(dve)
                    dve.bn_aggr(mv[:n, :], stats[:n].rearrange("p a b -> p (a b)")).then_inc(aggr_done, 1)
                    dve.wait_ge(aggr_done, t + 1)
                    dve.tensor_scalar(sd[:n, 0:1], mv[:n, 1:2], EPS, None, ALU.add).then_inc(var_done, 1)

                def finish(t, p):
                    n = n_rows(t)
                    dve.wait_ge(sd_done, t + 1)
                    dve.reciprocal(rs[:n, :], sd[:n, 1:2]).then_inc(rs_done, 1)
                    dve.wait_ge(rs_done, t + 1)
                    if is_tile(t, 0):
                        dve.wait_ge(vec_loaded, 32)
                    dve.scalar_tensor_tensor(out=y[:n, p, :], in0=y[:n, p, :], scalar=mv[:n, 0:1], in1=g_ln[:n, :],
                                             op0=ALU.subtract, op1=ALU.mult).then_inc(gain_done, 1)
                    dve.wait_ge(gain_done, t + 1)
                    dve.scalar_tensor_tensor(out=y[:n, p, :], in0=y[:n, p, :], scalar=rs[:n, :], in1=b_ln[:n, :],
                                             op0=ALU.mult, op1=ALU.add).then_inc(y_done, 1)

                for ks, pieces in first_pieces():
                    for k in ks:
                        dve.wait_ge(w_hi_done, k + 1)
                        dve.tensor_tensor(w_lo[:, k, :], raw[:, k % NRAW, :], w_hi[:, k, :].bitcast(F32),
                                          ALU.subtract).then_inc(w_lo_done, 1)
                    for x in pieces:
                        lo(x)

                def step(t, p, i):
                    for c in range(NPC):
                        lo(Piece(t, c))
                        if is_tile(t, 2) and c == 0:
                            norm(0, 0, 0)
                        if is_tile(t, 2) and c == 1:
                            finish(0, 0)
                        if c == 2:
                            norm(t - 1, 1 - p, i - 1 + p)
                        if c == 5:
                            finish(t - 1, 1 - p)
                tiles(dve, step)
                norm(NT, 0, NT // 2)
                finish(NT, 0)

            @block.tensor
            def _(pe):
                def multiply(x, out):
                    pe.wait_ge(h_lo_done, x.number + 1)
                    for e in range(PK):
                        k = PK * x.c + e
                        for col in range(0, D, 512):
                            last = products(pe, ps_y[:x.n, out, col:col + 512], h_hi[:, x.slot, e, :x.n], h_lo[:, x.slot, e, :x.n],
                                            w_hi[:, k, col:col + 512], w_lo[:, k, col:col + 512], k == 0, k == KF - 1)
                    last.then_inc(piece_done, 1)

                for ks, pieces in first_pieces():
                    pe.wait_ge(w_lo_done, ks[-1] + 1)
                    for t, x in enumerate(pieces):
                        multiply(x, 2 + t)

                def step(t, p, i):
                    if not (isinstance(t, int) and t < 4):
                        pe.wait_ge(sum_done, t - 1)
                    for c in range(NPC):
                        multiply(Piece(t, c), p)
                tiles(pe, step)


INPUTS = [
    ("x_prompt", (SEQ, D)), ("x_sample", (NSMP, D)), ("cache_k", (CACHE, AW)), ("cache_v", (CACHE, AW)),
    ("state_ssm", (AW, STATE)), ("state_ssm_conv", (3, XBC)), ("state_ffn_conv", (2, 2 * DFF)),
    ("ln_in_g", (D,)), ("ln_in_b", (D,)), ("w_in", (D, N_IN)), ("rel_bias", (HEADS, REL)),
    ("ssm_conv_w", (4, XBC)), ("ssm_conv_b", (XBC,)), ("ssm_dt_bias", (HEADS,)), ("ssm_a_log", (HEADS,)), ("ssm_d", (HEADS,)),
    ("gmlp_w", (CG, P, P)), ("gmlp_b", (CG, P)), ("mix_norm_g", (D,)), ("w_out", (D, D)), ("ln1_g", (D,)), ("ln1_b", (D,)),
    ("ffn_w_in", (D, 2 * DFF)), ("ffn_conv_w", (3, 2 * DFF)), ("ffn_conv_b", (2 * DFF,)), ("ffn_w_out", (DFF, D)),
    ("ln2_g", (D,)), ("ln2_b", (D,)),
]
ARGUMENT = {"cache_k": "cache_attn_k", "cache_v": "cache_attn_v", "rel_bias": "attn_rel_bias"}
OUTPUTS = [
    ("y_prompt", (SEQ, D), (1, SEQ, D)), ("y_sample", (NSMP, D), (1, NSMP, D)),
    ("prompt_k", (CACHE, AW), (1, 1, CACHE, HEADS, HD)), ("prompt_v", (CACHE, AW), (1, 1, CACHE, HEADS, HD)),
    ("prompt_ssm", (AW, STATE), (1, 1, HEADS, HD, STATE)), ("prompt_ssm_conv", (3, XBC), (1, 1, 3, XBC)),
    ("prompt_ffn_conv", (2, 2 * DFF), (1, 1, 2, 2 * DFF)),
    ("sample_k", (NSMP, AW), (1, 1, NSMP, HEADS, HD)), ("sample_v", (NSMP, AW), (1, 1, NSMP, HEADS, HD)),
    ("sample_ssm", (AW, STATE), (1, 1, HEADS, HD, STATE)), ("sample_ssm_conv", (3, XBC), (1, 1, 3, XBC)),
    ("sample_gmlp_v", (NSMP, CW), (1, 1, NSMP, CW)), ("sample_ffn_conv", (2, 2 * DFF), (1, 1, 2, 2 * DFF)),
]
SCRATCH = [
    ("x_rows", (ROWS, D), F32), ("xt", (P, KD, ROWS), F32),
    ("v_rows", (ROWS, AW), F32), ("z_rows", (ROWS, AW), F32), ("dt_rows", (ROWS, HEADS), F32), ("uv_rows", (ROWS, 2 * CW), F32),
    ("qk_hi", (2 * AW, ROWS), F32), ("qk_lo", (2 * AW, ROWS), F32), ("xbc_t", (P, NXBC, ROWS), F32), ("rel_ext", (HEADS, WIN + P), F32),
    ("mixed", (ROWS, D), F32), ("x1_rows", (ROWS, D), F32), ("x1t", (P, KD, ROWS), F32),
    ("h_t", (P, KF, ROWS), F32),
]


def build(nc):
    d = {name: nc.dram_tensor(name, shape, F32, kind="ExternalInput").ap() for name, shape in INPUTS}
    d.update({name: nc.dram_tensor(name, shape, F32, kind="ExternalOutput").ap() for name, shape, _ in OUTPUTS})
    d.update({name: nc.dram_tensor(name, shape, dt, kind="Internal").ap() for name, shape, dt in SCRATCH})
    for stage in STAGES:
        stage(nc, d)


STAGES = (project_rows, project_features, attention, ssd_and_gmlp, mix_out, ffn_up, ffn_down)


def kernel(**inputs):
    import numpy as np
    import concourse.bacc as bacc
    from concourse.bass_utils import run_bass_kernel_spmd

    nc = bacc.Bacc("TRN2", target_bir_lowering=False, num_devices=1)
    build(nc)
    arrays = {name: np.ascontiguousarray(inputs[ARGUMENT.get(name, name)]).reshape(shape) for name, shape in INPUTS}
    r = run_bass_kernel_spmd(nc, [arrays], core_ids=[0])
    return tuple(r.results[0][name].reshape(shape) for name, _, shape in OUTPUTS)
```
